# Optimizing a Trainium2 kernel written in Bass

```python
import jax, jax.numpy as jnp
from jax import lax
import numpy as np

D_MODEL = 1024
BATCH = 1
SEQ = 512
DEPTH = 1
DEC_BATCH = 8
DEC_SEQ = 1
PAST_LEN = 256
PAGE_SIZE = 128

BRANCH_W = 512
CONV_W = BRANCH_W
CONV_K = 3
SB_HEADS = 8
SB_HEAD_DIM = 64
SB_W = SB_HEADS * SB_HEAD_DIM
SB_BIAS_INIT = -6.0
X_HEADS = 4
X_HEAD_DIM = 128
X_W = X_HEADS * X_HEAD_DIM
N_MEM = 256
N_BRANCH = 3
Q_BLOCK = 128
N_GROUPS = 4
EXPERTS_PER_GROUP = 8
N_EXPERTS = N_GROUPS * EXPERTS_PER_GROUP
TOP_K = 2
D_EXPERT = 512
MOE_BLOCK = 128
EPS = 1e-6
SPLIT_SIZES = (CONV_W, CONV_W, CONV_W, SB_W, SB_W, SB_W, X_W, N_BRANCH * D_MODEL)
SPLIT_POINTS = tuple(int(i) for i in np.cumsum(SPLIT_SIZES)[:-1])
D_IN = sum(SPLIT_SIZES)

kernel_name = 'hybrid_conv_stickbreak_memxattn_hmoe_step'

def rms_norm(x, g):
    xf = x.astype(jnp.float32)
    y = xf * lax.rsqrt(jnp.mean(xf * xf, axis=-1, keepdims=True) + EPS)
    return y.astype(x.dtype) * g

def mixer_inputs(x, norm1, w_in, q_norm):
    B, T, _ = x.shape
    u_in, c_gate, b_gate, q, k, v, qx, gate_logits = jnp.split(
        rms_norm(x, norm1) @ w_in, SPLIT_POINTS, axis=-1)
    sb = lambda t: t.reshape(B, T, SB_HEADS, SB_HEAD_DIM)
    qx = rms_norm(qx.reshape(B, T, X_HEADS, X_HEAD_DIM), q_norm)
    return c_gate * u_in, b_gate, sb(q), sb(k), sb(v), qx, gate_logits

def causal_conv(u_ext, w):
    T = u_ext.shape[1] - (CONV_K - 1)
    out = u_ext[:, 0:T] * w[0]
    for j in range(1, CONV_K):
        out = out + u_ext[:, j:j + T] * w[j]
    return out

def stick_breaking(q, k, v, sb_bias, q_pos, k_pos):
    z = jnp.einsum('bqhd,bkhd->bhqk', q, k, preferred_element_type=jnp.float32) * (SB_HEAD_DIM ** -0.5)
    z = z + sb_bias.astype(jnp.float32)[None, :, None, None]
    causal = k_pos[None, :] < q_pos[:, None]
    log_keep = jnp.where(causal, jax.nn.log_sigmoid(-z), 0.0)
    log_a = jax.nn.log_sigmoid(z) + lax.cumsum(log_keep, axis=3, reverse=True) - log_keep
    a = jnp.where(causal, jnp.exp(log_a), 0.0)
    return jnp.einsum('bhqk,bkhd->bqhd', a, v.astype(jnp.float32)).astype(v.dtype)

def stick_breaking_prompt(q, k, v, sb_bias):
    B, S, H, d = q.shape
    nb = S // Q_BLOCK
    qb = q.reshape(B, nb, Q_BLOCK, H, d).swapaxes(0, 1)
    pos = jnp.arange(S)
    out = lax.map(lambda a: stick_breaking(a[0], k, v, sb_bias, a[1], pos),
                  (qb, pos.reshape(nb, Q_BLOCK)))
    return out.swapaxes(0, 1).reshape(B, S, H, d)

def memory_kv(mem, mem_norm, w_mem_kv, k_norm):
    B, M, _ = mem.shape
    mk, mv = jnp.split(rms_norm(mem, mem_norm) @ w_mem_kv, 2, axis=-1)
    mk = rms_norm(mk.reshape(B, M, X_HEADS, X_HEAD_DIM), k_norm)
    return mk, mv.reshape(B, M, X_HEADS, X_HEAD_DIM)

def cross_attend(qx, mk, mv):
    s = jnp.einsum('bthd,bmhd->bhtm', qx, mk, preferred_element_type=jnp.float32) * (X_HEAD_DIM ** -0.5)
    p = jax.nn.softmax(s, axis=-1).astype(mv.dtype)
    return jnp.einsum('bhtm,bmhd->bthd', p, mv)

def grouped_experts(hf, expert, gate, w1, w3, w2):
    T, K = expert.shape
    n = T * K
    e_flat = expert.reshape(-1).astype(jnp.int32)
    tok = jnp.repeat(jnp.arange(T), K)
    order = jnp.argsort(e_flat * n + jnp.arange(n))
    e_sorted = e_flat[order]
    tok_sorted = tok[order]
    counts = jnp.bincount(e_flat, length=N_EXPERTS)
    starts = jnp.cumsum(counts) - counts
    padded = (counts + MOE_BLOCK - 1) // MOE_BLOCK * MOE_BLOCK
    ends = jnp.cumsum(padded)
    dest = (ends - padded)[e_sorted] + jnp.arange(n) - starts[e_sorted]
    n_blocks = -(-(n + N_EXPERTS * (MOE_BLOCK - 1)) // MOE_BLOCK)
    buf = jnp.zeros((n_blocks * MOE_BLOCK, hf.shape[1]), hf.dtype).at[dest].set(hf[tok_sorted])
    block_e = jnp.clip(jnp.searchsorted(ends, jnp.arange(n_blocks) * MOE_BLOCK, side='right'),
                       0, N_EXPERTS - 1)

    def run_block(a):
        xb, e = a
        return (jax.nn.silu(xb @ w1[e]) * (xb @ w3[e])) @ w2[e]

    ybuf = lax.map(run_block, (buf.reshape(n_blocks, MOE_BLOCK, -1), block_e)).reshape(n_blocks * MOE_BLOCK, -1)
    y_sorted = ybuf[dest] * gate.reshape(-1)[order][:, None].astype(hf.dtype)
    return jnp.zeros((T, ybuf.shape[1]), hf.dtype).at[tok_sorted].add(y_sorted)

def hier_moe(h, w_group, b_group, w_router, b_router, w1, w3, w2):
    shp = h.shape
    hf = h.reshape(-1, shp[-1])
    T = hf.shape[0]
    g_logits = (hf @ w_group + b_group).astype(jnp.float32)
    g_prob = jax.nn.softmax(g_logits, axis=-1)
    g_idx = jnp.argmax(g_logits, axis=-1)
    e_logits = (hf @ w_router + b_router).astype(jnp.float32).reshape(T, N_GROUPS, EXPERTS_PER_GROUP)
    e_in = jnp.take_along_axis(e_logits, g_idx[:, None, None], axis=1)[:, 0]
    top_v, top_i = lax.top_k(e_in, TOP_K)
    gate = jax.nn.softmax(top_v, axis=-1) * jnp.take_along_axis(g_prob, g_idx[:, None], axis=1)
    expert = g_idx[:, None] * EXPERTS_PER_GROUP + top_i
    return grouped_experts(hf, expert, gate, w1, w3, w2).reshape(shp)

def merge_and_ffn(x, y_conv, y_sb, y_x, gate_logits, w_branch, w_o, norm2,
                  w_group, b_group, w_router, b_router, w1, w3, w2):
    B, T, _ = x.shape
    ys = jnp.stack([y_conv, y_sb.reshape(B, T, SB_W), y_x.reshape(B, T, X_W)], axis=2)
    branch = jnp.einsum('btgc,gcd->btgd', ys, w_branch)
    gates = jax.nn.sigmoid(gate_logits.reshape(B, T, N_BRANCH, D_MODEL))
    x1 = x + jnp.sum(gates * branch, axis=2) @ w_o
    return x1 + hier_moe(rms_norm(x1, norm2), w_group, b_group, w_router, b_router, w1, w3, w2)

def setup_inputs(seed: int = 0) -> dict:
    key = jax.random.key(seed)
    ks = jax.random.split(key, 32)
    n_pages = PAST_LEN // PAGE_SIZE
    n_phys = (DEC_BATCH * n_pages * 5) // 4
    nrm = lambda k, shape, s: jax.random.normal(k, shape, jnp.float32) * s
    page_table = jax.random.permutation(ks[7], n_phys)[:DEC_BATCH * n_pages].reshape(
        DEC_BATCH, n_pages).astype(jnp.int32)
    return {
        'x_prompt': nrm(ks[0], (BATCH, SEQ, D_MODEL), 1.0),
        'x_sample': nrm(ks[1], (DEC_BATCH, DEC_SEQ, D_MODEL), 1.0),
        'mem_prompt': nrm(ks[2], (BATCH, N_MEM, D_MODEL), 1.0),
        'cache_k': nrm(ks[3], (n_phys, PAGE_SIZE, SB_HEADS, SB_HEAD_DIM), 1.0),
        'cache_v': nrm(ks[4], (n_phys, PAGE_SIZE, SB_HEADS, SB_HEAD_DIM), 1.0),
        'cache_mem_k': nrm(ks[5], (DEC_BATCH, N_MEM, X_HEADS, X_HEAD_DIM), 1.0),
        'cache_mem_v': nrm(ks[6], (DEC_BATCH, N_MEM, X_HEADS, X_HEAD_DIM), 1.0),
        'state_conv': nrm(ks[8], (DEC_BATCH, CONV_K - 1, CONV_W), 1.0),
        'page_table': page_table,
        'norm1': 1.0 + nrm(ks[9], (D_MODEL,), 0.02),
        'w_in': nrm(ks[10], (D_MODEL, D_IN), D_MODEL ** -0.5),
        'conv_w': nrm(ks[11], (CONV_K, CONV_W), CONV_K ** -0.5),
        'sb_bias': SB_BIAS_INIT + nrm(ks[26], (SB_HEADS,), 0.1),
        'mem_norm': 1.0 + nrm(ks[12], (D_MODEL,), 0.02),
        'w_mem_kv': nrm(ks[13], (D_MODEL, 2 * X_W), D_MODEL ** -0.5),
        'q_norm': 1.0 + nrm(ks[14], (X_HEAD_DIM,), 0.02),
        'k_norm': 1.0 + nrm(ks[15], (X_HEAD_DIM,), 0.02),
        'w_branch': nrm(ks[16], (N_BRANCH, BRANCH_W, D_MODEL), BRANCH_W ** -0.5),
        'w_o': nrm(ks[17], (D_MODEL, D_MODEL), D_MODEL ** -0.5),
        'norm2': 1.0 + nrm(ks[18], (D_MODEL,), 0.02),
        'w_group': nrm(ks[19], (D_MODEL, N_GROUPS), D_MODEL ** -0.5),
        'b_group': nrm(ks[20], (N_GROUPS,), 0.01),
        'w_router': nrm(ks[21], (D_MODEL, N_EXPERTS), D_MODEL ** -0.5),
        'b_router': nrm(ks[22], (N_EXPERTS,), 0.01),
        'w1': nrm(ks[23], (N_EXPERTS, D_MODEL, D_EXPERT), D_MODEL ** -0.5),
        'w3': nrm(ks[24], (N_EXPERTS, D_MODEL, D_EXPERT), D_MODEL ** -0.5),
        'w2': nrm(ks[25], (N_EXPERTS, D_EXPERT, D_MODEL), D_EXPERT ** -0.5),
    }

def reference(x_prompt, x_sample, mem_prompt, cache_k, cache_v, cache_mem_k, cache_mem_v,
              state_conv, page_table, norm1, w_in, conv_w, sb_bias, mem_norm, w_mem_kv, q_norm, k_norm,
              w_branch, w_o, norm2, w_group, b_group, w_router, b_router, w1, w3, w2):
    moe = (w_group, b_group, w_router, b_router, w1, w3, w2)
    u_p, bg_p, q_p, k_p, v_p, qx_p, gl_p = mixer_inputs(x_prompt, norm1, w_in, q_norm)
    y_conv_p = bg_p * causal_conv(jnp.pad(u_p, ((0, 0), (CONV_K - 1, 0), (0, 0))), conv_w)
    conv_prompt = u_p[:, -(CONV_K - 1):]
    y_sb_p = stick_breaking_prompt(q_p, k_p, v_p, sb_bias)
    mem_k_p, mem_v_p = memory_kv(mem_prompt, mem_norm, w_mem_kv, k_norm)
    y_x_p = cross_attend(qx_p, mem_k_p, mem_v_p)
    y_prompt = merge_and_ffn(x_prompt, y_conv_p, y_sb_p, y_x_p, gl_p, w_branch, w_o, norm2, *moe)
    n_batch, dec_seq = x_sample.shape[0], x_sample.shape[1]
    past = page_table.shape[1] * PAGE_SIZE
    u_s, bg_s, q_s, k_s, v_s, qx_s, gl_s = mixer_inputs(x_sample, norm1, w_in, q_norm)
    u_ext = jnp.concatenate([state_conv.astype(u_s.dtype), u_s], axis=1)
    y_conv_s = bg_s * causal_conv(u_ext, conv_w)
    conv_sample = u_ext[:, -(CONV_K - 1):]
    k_all = jnp.concatenate([cache_k[page_table].reshape(n_batch, past, SB_HEADS, SB_HEAD_DIM), k_s], axis=1)
    v_all = jnp.concatenate([cache_v[page_table].reshape(n_batch, past, SB_HEADS, SB_HEAD_DIM), v_s], axis=1)
    y_sb_s = stick_breaking(q_s, k_all, v_all, sb_bias, past + jnp.arange(dec_seq), jnp.arange(past + dec_seq))
    y_x_s = cross_attend(qx_s, cache_mem_k, cache_mem_v)
    y_sample = merge_and_ffn(x_sample, y_conv_s, y_sb_s, y_x_s, gl_s, w_branch, w_o, norm2, *moe)
    return (y_prompt, y_sample, k_p, v_p, conv_prompt, mem_k_p, mem_v_p, k_s, v_s, conv_sample)


_drawn_inputs = setup_inputs


def setup_inputs(seed=0):
    import zlib

    import numpy as np

    out = dict(_drawn_inputs(seed))
    spreads = {}
    factors = {'sb_bias': 6.983,
     'mem_norm': 2.895,
     'q_norm': 8.0,
     'k_norm': 2.808,
     'b_group': 17.731,
     'b_router': 7.229}
    for name, (base, spread) in spreads.items():
        noise = np.random.default_rng([zlib.crc32(name.encode()), seed]).standard_normal(out[name].shape)
        drawn = base * np.exp(spread * noise) if base else spread * noise
        out[name] = __import__('jax').numpy.asarray(drawn.astype(out[name].dtype))
    for name, factor in factors.items():
        out[name] = (out[name] * factor).astype(out[name].dtype)
    return out
```

```python
from contextlib import ExitStack

import concourse.bass as bass
from concourse import mybir

F32 = mybir.dt.float32
F32R = mybir.dt.float32r
I32 = mybir.dt.int32
ALU = mybir.AluOpType
ACT = mybir.ActivationFunctionType
AX = mybir.AxisListType

P = 128
D = 1024
SEQ = 512
NB = 8
TOK = SEQ + NB
NT = SEQ // P + 1
HALF_TOK = TOK // 2
KD = D // P
W = 512
CW = W // P
HEADS, HD = 8, 64
XH, XD = 4, 128
NM = 256
PAST = 256
PAGES = PAST // P
CONV_K = 3
NG, EPG = 4, 8
NE = NG * EPG
NR = NG + NE
DE = 512
EPS = 1e-6
SB_SCALE = HD ** -0.5
X_SCALE = XD ** -0.5

CHUNKS = 6656 // P
IN_CHUNKS = 28
RING = 4
U0, C0, B0, Q0, K0, V0, X0 = (CW * i for i in range(7))

CAP = 64
EXTRA = (2 * TOK) // CAP
BLOCKS = NE + EXTRA
SLOTS = BLOCKS * CAP

SCORE_AT = (0, 512, 1024, 896)
SCORE_N = 1280


def build(nc, io):
    ctx = ExitStack()
    with ctx:
        start = -(-nc.sbuf_base // 64) * 64
        at = {}
        for name, size in (("x", 20480), ("xn", 33280), ("ws", 32768), ("ys", 24960), ("qk", 33280),
                           ("t", 61824), ("misc", 6144)):
            at[name] = start
            start += size

        def place(name, region, offset, shape, dt=F32):
            return nc.alloc_sbuf_tensor_at(name, [P] + list(shape), dt, offset=at[region] + offset)

        used = [0]

        def misc(name, shape, dt=F32):
            n = 1
            for s in shape:
                n *= s
            t = place(name, "misc", used[0], shape, dt)
            used[0] += -(-4 * n // 32) * 32
            assert used[0] <= 6144, used
            return t

        def sem(name):
            return ctx.enter_context(nc.semaphore(name))

        ident = misc("ident", [P])
        tri_from = misc("tri_from", [P])
        tri_before = misc("tri_before", [P])
        ones = misc("ones", [P])
        norm1_t = misc("norm1_t", [KD])
        mnorm_t = misc("mnorm_t", [KD])
        qnorm_t = misc("qnorm_t", [1])
        conv_t = misc("conv_t", [CONV_K, CW])
        sbias_bc = misc("sbias_bc", [HEADS])
        knorm_bc = misc("knorm_bc", [XD])
        rbias_bc = misc("rbias_bc", [NR])
        ss = misc("ss", [NT + 2])
        rs = misc("rs", [NT + 2])
        ss_mk = misc("ss_mk", [2 * XH])
        rs_mk = misc("rs_mk", [2 * XH])
        ss_qx = misc("ss_qx", [NT * XH])
        rs_qx = misc("rs_qx", [NT * XH])
        page_i = misc("page_i", [NB * PAGES], I32)
        page_f = misc("page_f", [NB * PAGES])
        row_f = misc("row_f", [1])
        page_row = misc("page_row", [NB * PAGES], I32)
        xst_tmp = misc("xst_tmp", [KD, NB])
        state_t = misc("state_t", [2, CW, NB])
        xmax = misc("xmax", [2, NT - 1])
        xneg = misc("xneg", [2, NT - 1])
        xsum = misc("xsum", [2, NT - 1])
        xrec = misc("xrec", [2, NT - 1])
        pm_t = misc("pm_t", [2, NB * XH])
        ss2 = misc("ss2", [NT])
        rs2 = misc("rs2", [NT])

        x_in = place("x_in", "x", 0, [NT, D])
        q_s = place("q_s", "x", 0, [W])
        qx_s = place("qx_s", "x", 2048, [W])
        v_s = place("v_s", "x", 4096, [W])
        k_s = place("k_s", "x", 6144, [W])
        conv_out = place("conv_out", "x", 8192, [W])
        state = place("state", "x", 10240, [2 * W])
        zs = place("zs", "x", 14336, [2, NB, HEADS])
        z_abs = place("z_abs", "x", 14848, [2, NB, HEADS])
        z_sp = place("z_sp", "x", 15360, [2, NB, HEADS])
        a_s = place("a_s", "x", 15872, [2, NB, HEADS])
        z_raw = place("z_raw", "x", 16384, [2, NB, HEADS])
        zm = place("zm", "x", 16896, [2, NB, XH])
        pm = place("pm", "x", 17152, [NM])
        x1 = place("x1", "x", 0, [NT, D])
        xn_hi = place("xn_hi", "xn", 0, [KD, TOK], F32R)
        xn_lo = place("xn_lo", "xn", 16640, [KD, TOK], F32R)
        w_raw = place("w_raw", "ws", 0, [RING, KD, P])
        w_lo = place("w_lo", "ws", 0, [RING, KD, P], F32R)
        w_hi = place("w_hi", "ws", 16384, [RING, KD, P], F32R)
        proj = place("proj", "ys", 0, [IN_CHUNKS, TOK])
        w_o = place("w_o_sb", "qk", 0, [KD, D])
        w_mem = place("w_mem", "t", 0, [KD, D])
        junk = place("junk", "t", 45056, [D])
        mem_in = place("mem_in", "t", 53248, [2, D])
        mem_t = place("mem_t", "t", 32768, [KD, NM])
        v_tok = place("v_tok", "t", 32768, [NT - 1, W])
        mk = place("mk", "t", 40960, [2, W])
        k_out = place("k_out", "t", 40960, [2, W])
        mv = place("mv", "t", 45056, [2, W])
        mk_t = place("mk_t", "t", 49152, [XH, NM])
        cache = place("cache", "t", 53248, [2, PAGES, W])
        qx_sq = place("qx_sq", "t", 0, [XH, TOK])
        prob = place("prob", "t", 8704, [2, NT - 1, NM])
        prob_t = place("prob_t", "t", 16896, [2, 2, SEQ])
        mk_sq = place("mk_sq", "t", 25088, [2, W])
        z_sb = place("z_sb", "t", 0, [2, SCORE_N])
        sp_sb = place("sp_sb", "t", 10240, [2, SCORE_N])
        a_sb = place("a_sb", "t", 20480, [2, SCORE_N])
        dot = place("dot", "t", 0, [2, W])
        merged = place("merged", "t", 36992, [KD, TOK])
        w_br = place("w_br", "t", 53632, [RING, CW, P])
        gate_sb = place("gate_sb", "t", 32768, [2, TOK])

        w1_sb = [place("w1_a", "t", 0, [KD, DE]), place("w1_b", "ws", 16384, [KD, DE])]
        w3_sb = [place("w3_a", "t", 16384, [KD, DE]), place("w3_b", "qk", 0, [KD, DE])]
        w2_sb = [place("w2_a", "ws", 0, [CW, D]), place("w2_b", "qk", 16384, [CW, D])]
        h_tok = place("h_tok", "ys", 0, [NT, D])
        norm2_bc = place("norm2_bc", "ys", 20480, [D])
        h_t = place("h_t", "xn", 0, [KD, TOK])
        xg = place("xg", "xn", 16640, [2, D])
        xg_t = place("xg_t", "xn", 24832, [2, KD, CAP])
        y_out = place("y_out", "xn", 28928, [2, DE])
        up_sb = place("up_sb", "t", 36992, [2, DE])
        gate_h = place("gate_h", "t", 41088, [CW, CAP])
        act_t = place("act_t", "t", 42112, [2, CW, CAP])
        low_part = place("low_part", "t", 44160, [NE, NE])
        low_tri = place("low_tri", "t", 48256, [NE, NE])
        w_r = place("w_r", "t", 53632, [KD, NR])
        route_at = [53632 + 1152]

        def route(name, shape, dt=F32):
            n = 1
            for v in shape:
                n *= v
            t = place(name, "t", route_at[0], shape, dt)
            route_at[0] += -(-4 * n // 32) * 32
            assert route_at[0] <= 61824
            return t

        junk2 = place("junk2", "xn", 24832, [D])
        logits = route("logits", [NT, NR])
        g_top = route("g_top", [NT])
        g_exp = route("g_exp", [NT, NG])
        g_prob = route("g_prob", [NT])
        g_one = route("g_one", [NT, NG])
        g_tmp = route("g_tmp", [NT, NG])
        e_all = route("e_all", [NT, NG, EPG])
        e_in = route("e_in", [NT, EPG])
        e_tmp = route("e_tmp", [NT, EPG])
        one1 = route("one1", [NT, EPG])
        one2 = route("one2", [NT, EPG])
        top1 = route("top1", [NT])
        top2 = route("top2", [NT])
        gate1 = route("gate1", [NT])
        gate2 = route("gate2", [NT])
        valid = route("valid", [NT])
        rev = route("rev", [EPG])
        limits = route("limits", [TOK // CAP])
        over_part = route("over_part", [NE, TOK // CAP])
        pick1 = route("pick1", [NT, NG, EPG])
        pick2 = route("pick2", [NT, NG, EPG])
        picked = route("picked", [NT, NE])
        dest = route("dest", [NT, NE])
        over = route("over", [NT, NE])
        dest1 = route("dest1", [NT])
        dest2 = route("dest2", [NT])
        dest1_i = misc("dest1_i", [NT], I32)
        dest2_i = misc("dest2_i", [NT], I32)
        count = misc("count", [NE])
        extra = misc("extra", [NE])
        extra_end = misc("extra_end", [NE])
        first_slot = misc("first_slot", [NE])
        over_slot = misc("over_slot", [NE])
        steps = misc("steps", [EXTRA])
        tok_f = misc("tok_f", [NT])
        over_who = place("over_who", "t", 32768, [EXTRA, NE])
        zero_row = place("zero_row", "t", 34816, [NE])
        over_cnt = misc("over_cnt", [EXTRA])
        over_i = misc("over_i", [EXTRA + 1], I32)
        slot_rows = misc("slot_rows", [CAP])
        slot_tok = misc("slot_tok", [BLOCKS], I32)
        slot_now = misc("slot_now", [2], I32)
        ya = place("ya", "t", 0, [2, D])
        yb = place("yb", "t", 8192, [2, D])
        h_dram = nc.dram_tensor("h_dram", [TOK, D], F32, kind="Internal").ap()
        y_dram = nc.dram_tensor("y_dram", [SLOTS, D], F32, kind="Internal").ap()
        slot_dram = nc.dram_tensor("slot_dram", [SLOTS, 1], F32, kind="Internal").ap()

        acc_all = ctx.enter_context(nc.psum_tensor("acc_all", [P, 8 * 512], F32))

        def bank(b, n=1):
            return acc_all[:, b * 512:(b + n) * 512]

        def acc_pair(b):
            return bank(b, 2).rearrange("p (a n) -> p a n", a=2)[:, :, 0:HALF_TOK]

        def halves(tile):
            return tile.rearrange("p (a n) -> p a n", a=2)

        def rows(tt):
            return P if tt < NT - 1 else NB

        def tok(tt):
            return slice(tt * P, tt * P + rows(tt))

        consts = sem("consts")
        small_ld, x_ld, mem_ld, wmem_ld, state_ld, page_ld = (sem(n) for n in (
            "small_ld", "x_ld", "mem_ld", "wmem_ld", "state_ld", "page_ld"))
        dve_step, act_step, pool_step = sem("dve_step"), sem("act_step"), sem("pool_step")
        ss_init, sumsq_ok, ms_ok, sqrt_ok, xn_ok = (sem(n) for n in ("ss_init", "sumsq_ok", "ms_ok", "sqrt_ok", "xn_ok"))
        xt_ps, xt_hi, xt_lo, xst_ps, xst_f, xst_hi, xst_lo = (sem(n) for n in (
            "xt_ps", "xt_hi", "xt_lo", "xst_ps", "xst_f", "xst_hi", "xst_lo"))
        mt_ps, mt_sb, mp_ps, mp_sb = (sem(n) for n in ("mt_ps", "mt_sb", "mp_ps", "mp_sb"))
        w_ld = [sem(f"w_ld{j}") for j in range(RING)]
        split_hi, split_lo, w_used, pj_sb = (sem(n) for n in ("split_hi", "split_lo", "w_used", "pj_sb"))
        tp_ps, tp_sb = sem("tp_ps"), sem("tp_sb")
        conv_ok, u_ok, qxsq_ok, qxn_ok, qxms_ok, qxrt_ok, qxrs_ok = (sem(n) for n in (
            "conv_ok", "u_ok", "qxsq_ok", "qxn_ok", "qxms_ok", "qxrt_ok", "qxrs_ok"))
        mkms_ok, mkrt_ok, mk_ok = sem("mkms_ok"), sem("mkrt_ok"), sem("mk_ok")
        mk_st, kout_st, mid_st, out_st = sem("mk_st"), [sem("kout_st0"), sem("kout_st1")], sem("mid_st"), sem("out_st")
        rows_ok, cr_ld, cr_used = sem("rows_ok"), [sem("cr_ld0"), sem("cr_ld1")], sem("cr_used")
        bq_ps, bq_used, dot_ok = sem("bq_ps"), sem("bq_used"), sem("dot_ok")
        cs_ps, cs_mx, cs_exp, cs_nrm, ct_ps, ct_sb, cy_ps, cy_sb = (sem(n) for n in (
            "cs_ps", "cs_mx", "cs_exp", "cs_nrm", "ct_ps", "ct_sb", "cy_ps", "cy_sb"))
        z_ps, z_sbuf, z_read, ln_ok, sp_ok, sp_cut, s_ps, t_ok, t_cut, a_ok, y_ps, y_sb = (sem(n) for n in (
            "z_ps", "z_sbuf", "z_read", "ln_ok", "sp_ok", "sp_cut", "s_ps", "t_ok", "t_cut", "a_ok", "y_ps", "y_sb"))
        zs_ok, zsln_ok, zssp_ok, ss_ps, ts_ok, as_ok, yv_ps, yv_sb = (sem(n) for n in (
            "zs_ok", "zsln_ok", "zssp_ok", "ss_ps", "ts_ok", "as_ok", "yv_ps", "yv_sb"))
        zm_ok, zm_ps, zm_mx, pm_exp, pm_ok, pmt_ps, pmt_sb, ym_ps, ym_sb = (sem(n) for n in (
            "zm_ok", "zm_ps", "zm_mx", "pm_exp", "pm_ok", "pmt_ps", "pmt_sb", "ym_ps", "ym_sb"))
        br_ld = [sem(f"br_ld{j}") for j in range(RING)]
        gt_ps, gt_sb, br_ps, term_ok, mg_ok = (sem(n) for n in ("gt_ps", "gt_sb", "br_ps", "term_ok", "mg_ok"))
        GATES, MID_STORES = 3 * KD, 16 * 10
        POOL_CONSTS = 3 + 7 + 2
        fill_st = sem("fill_st")
        carried_pe, carried_pool = sem("carried_pe"), sem("carried_pool")
        wo_ld, x1_ld, n2_ld, wr_ld, wo_ps, x1_ok = (sem(n) for n in ("wo_ld", "x1_ld", "n2_ld", "wr_ld", "wo_ps", "x1_ok"))
        ss2_ok, ms2_ok, rt2_ok, h_ok, ht_ps, ht_sb, h_st = (sem(n) for n in (
            "ss2_ok", "ms2_ok", "rt2_ok", "h_ok", "ht_ps", "ht_sb", "h_st"))
        lg_ps, lg_max, lg_exp, top_ok, top_exp, pick_ok, rank_ps, dest_ok, ids_st, ids_ld, ids_ps, ids_ok, over_ok = (
            sem(n) for n in ("lg_ps", "lg_max", "lg_exp", "top_ok", "top_exp", "pick_ok", "rank_ps", "dest_ok",
                             "ids_st", "ids_ld", "ids_ps", "ids_ok", "over_ok"))
        w13_ld, w2_ld = [sem("w13_ld0"), sem("w13_ld1")], [sem("w2_ld0"), sem("w2_ld1")]
        now_ok, xgt_ps, xgt_sb, up_ps, up_ok, upt_ps, sig_ok, half_ok, actt_ok, y2_ps, y2_sb = (sem(n) for n in (
            "now_ok", "xgt_ps", "xgt_sb", "up_ps", "up_ok", "upt_ps", "sig_ok", "half_ok", "actt_ok", "y2_ps", "y2_sb"))
        xg_ld = [sem("xg_ld0"), sem("xg_ld1")]
        ydr_st, ys_ld, y_done = [sem("ydr_st0"), sem("ydr_st1")], [sem("ys_ld0"), sem("ys_ld1")], sem("y_done")

        (JOB_STATE, JOB_V, JOB_Q, JOB_QSS, JOB_QX, JOB_U, JOB_MK, JOB_K) = (0, 1, 6, 7, 8, 9, 10, 12)
        JOBS = 17

        def cut(pool, h, tile, ready, fill, done):
            pool.wait_ge(ready, h + 1)
            for kb in range(4):
                v = tile[:, h % 2, SCORE_AT[kb]:SCORE_AT[kb] + P]
                pool.affine_select(out=v, in_=v, compare_op=ALU.is_gt, fill=fill, base=0,
                                   pattern=[[1, P]], channel_multiplier=-1).then_inc(done, 1)

        def cross_out(act, h):
            act.wait_ge(ct_ps, h + 1)
            if h >= 2:
                act.wait_ge(cy_ps, h - 1)
            act.activation(prob_t[:, h % 2, :, :], bank(4, 2).rearrange("p (t n) -> p t n", t=2), ACT.Copy).then_inc(ct_sb, 1)
            act.wait_ge(cy_ps, h + 1)
            act.activation(proj[:, B0 + h, 0:SEQ], bank(6 + h % 2), ACT.Copy).then_inc(cy_sb, 1)

        block = ctx.enter_context(nc.Block())

        @block.sync
        def _(sp):
            for tile, name in ((norm1_t, "norm1"), (mnorm_t, "mem_norm"), (qnorm_t, "q_norm")):
                sp.dma_start(tile[:, :], io[name]).then_inc(small_ld, 16)
            sp.dma_start(conv_t[:, :, :], io["conv_w"]).then_inc(small_ld, 16)
            sp.dma_start(sbias_bc[:, :], io["sb_bias"].partition_broadcast(P)).then_inc(small_ld, 16)
            sp.dma_start(knorm_bc[:, :], io["k_norm"].partition_broadcast(P)).then_inc(small_ld, 16)
            sp.dma_start(rbias_bc[:, :], io["router_b"].partition_broadcast(P)).then_inc(small_ld, 16)
            sp.dma_start(x_in[:, 0:NT - 1, :], io["x_prompt"].rearrange("b (t p) d -> p (b t) d", p=P)).then_inc(x_ld, 16)
            sp.dma_start(x_in[0:NB, NT - 1, :], io["x_sample"].rearrange("b s d -> (b s) d")).then_inc(x_ld, 16)
            for j in range(RING):
                sp.dma_start(w_raw[:, j, :, :], io["w_in"][j]).then_inc(w_ld[j], 16)
            sp.dma_start(mem_in[:, :, :], io["mem_prompt"].rearrange("b (t p) d -> p (b t) d", p=P)).then_inc(mem_ld, 16)
            sp.dma_start(w_mem[:, :, :], io["w_mem_kv"].rearrange("(k p) n -> p k n", p=P)).then_inc(wmem_ld, 16)
            for part in range(EXTRA * CAP // SEQ):
                at_row = NE * CAP + part * SEQ
                sp.dma_start(y_dram[at_row:at_row + SEQ, :], io["x_prompt"].rearrange("b s d -> (b s) d")).then_inc(fill_st, 16)
            with sp.Fori(0, IN_CHUNKS // RING) as i:
                for j in range(RING):
                    sp.wait_ge(w_used, RING * i + j + 1)
                    sp.dma_start(w_raw[:, j, :, :], io["w_in"][RING * i + RING + j]).then_inc(w_ld[j], 16)
            sp.dma_start(state[0:NB, :], io["state_conv"].rearrange("b j c -> b (j c)")).then_inc(state_ld, 16)
            sp.wait_ge(tp_sb, JOB_V + 5)
            for tt in range(NT - 1):
                sp.dma_start(io["v_p"][tok(tt), :], v_tok[:, tt, :]).then_inc(mid_st, 16)
            sp.dma_start(io["v_s"], v_s[0:NB, :]).then_inc(mid_st, 16)
            sp.dma_start(io["conv_s"][:, 0, :], state[0:NB, W:2 * W]).then_inc(mid_st, 16)
            sp.wait_ge(mp_sb, 4)
            sp.dma_start(io["mem_v"].rearrange("(t p) c -> p t c", p=P), mv[:, :, :]).then_inc(mid_st, 16)
            sp.wait_ge(mk_ok, 1)
            sp.dma_start(io["mem_k"].rearrange("(t p) c -> p t c", p=P), mk[:, :, :]).then_inc(mk_st, 16)
            sp.wait_ge(tp_sb, JOB_U + 1)
            sp.dma_start(io["conv_p"], conv_out[0:2, :]).then_inc(mid_st, 16)
            sp.dma_start(io["conv_s"][:, 1, :], conv_out[2:2 + NB, :]).then_inc(mid_st, 16)
            for tt in range(NT):
                sp.wait_ge(tp_sb, JOB_K + tt + 1)
                if tt < NT - 1:
                    sp.dma_start(io["k_p"][tok(tt), :], k_out[:, tt % 2, :]).then_inc(kout_st[tt % 2], 16)
                else:
                    sp.dma_start(io["k_s"], k_s[0:NB, :]).then_inc(mid_st, 16)
            def load_branch(n):
                sp.dma_start(w_br[:, n % RING, :, :], io["w_branch"][n]).then_inc(br_ld[n % RING], 16)

            sp.wait_ge(ym_sb, 1)
            sp.wait_ge(mid_st, MID_STORES)
            sp.wait_ge(cr_used, 4 * NB)
            for j in range(RING):
                load_branch(j)
            sp.dma_start(w_o[:, :, :], io["w_o"].rearrange("(k p) n -> p k n", p=P)).then_inc(wo_ld, 16)
            sp.dma_start(x1[:, 0:NT - 1, :], io["x_prompt"].rearrange("b (t p) d -> p (b t) d", p=P)).then_inc(x1_ld, 16)
            sp.dma_start(x1[0:NB, NT - 1, :], io["x_sample"].rearrange("b s d -> (b s) d")).then_inc(x1_ld, 16)
            w1_d = io["w1"].rearrange("e (p k) n -> e p k n", p=P)
            w3_d = io["w3"].rearrange("e (p k) n -> e p k n", p=P)
            w2_d = io["w2"].rearrange("e (p c) n -> e p c n", p=P)
            sp.dma_start(w1_sb[0][:, :, :], w1_d[0]).then_inc(w13_ld[0], 16)
            sp.dma_start(w3_sb[0][:, :, :], w3_d[0]).then_inc(w13_ld[0], 16)
            with sp.Fori(0, (GATES - RING) // RING) as i:
                for j in range(RING):
                    sp.wait_ge(mg_ok, RING * i + j + 3)
                    sp.dma_start(w_raw[:, j, :, :], io["w_in"][IN_CHUNKS + RING * i + RING + j]).then_inc(w_ld[j], 16)
                    sp.dma_start(w_br[:, j, :, :], io["w_branch"][RING * i + RING + j]).then_inc(br_ld[j], 16)
            sp.wait_ge(mg_ok, GATES + 2)
            sp.dma_start(norm2_bc[:, :], io["norm2"].partition_broadcast(P)).then_inc(n2_ld, 16)
            sp.dma_start(w_r[:, :, :], io["router_w"]).then_inc(wr_ld, 16)
            sp.dma_start(w2_sb[0][:, :, :], w2_d[0]).then_inc(w2_ld[0], 16)
            sp.dma_start(w1_sb[1][:, :, :], w1_d[1]).then_inc(w13_ld[1], 16)
            sp.wait_ge(wo_ps, 2 * NT)
            sp.dma_start(w3_sb[1][:, :, :], w3_d[1]).then_inc(w13_ld[1], 16)
            sp.dma_start(w2_sb[1][:, :, :], w2_d[1]).then_inc(w2_ld[1], 16)
            with sp.Fori(0, NE // 2 - 1) as i:
                for j in range(2):
                    sp.wait_ge(up_ps, 2 * i + j + 1)
                    sp.dma_start(w1_sb[j][:, :, :], w1_d[2 * i + 2 + j]).then_inc(w13_ld[j], 16)
                    sp.dma_start(w3_sb[j][:, :, :], w3_d[2 * i + 2 + j]).then_inc(w13_ld[j], 16)
                    sp.wait_ge(y2_ps, 2 * i + j + 1)
                    sp.dma_start(w2_sb[j][:, :, :], w2_d[2 * i + 2 + j]).then_inc(w2_ld[j], 16)
            sp.wait_ge(over_ok, 1)
            n_extra = sp.value_load(over_i[0:1, EXTRA:EXTRA + 1], min_val=0, max_val=EXTRA)
            with sp.Fori(0, EXTRA) as i:
                with sp.If(n_extra > i):
                    e = sp.value_load(over_i[0:1, bass.ds(i, 1)], min_val=0, max_val=NE - 1)
                    sp.wait_ge(y2_ps, NE + i)
                    sp.dma_start(w1_sb[0][:, :, :], w1_d[e]).then_inc(w13_ld[0], 16)
                    sp.dma_start(w3_sb[0][:, :, :], w3_d[e]).then_inc(w13_ld[0], 16)
                    sp.dma_start(w2_sb[0][:, :, :], w2_d[e]).then_inc(w2_ld[0], 16)
            sp.wait_ge(mid_st, MID_STORES)
            for tt in range(NT):
                sp.wait_ge(y_done, tt + 1)
                if tt < NT - 1:
                    sp.dma_start(io["y_p"][tok(tt), :], x1[:, tt, :]).then_inc(out_st, 16)
                else:
                    sp.dma_start(io["y_s"], x1[0:NB, tt, :]).then_inc(out_st, 16)
            sp.wait_ge(out_st, 16 * NT)
            sp.wait_ge(mk_st, 16)
            for j in range(2):
                sp.wait_ge(kout_st[j], 32)

        @block.gpsimd
        def _(pool):
            steps_done = [0]

            def link(ins):
                steps_done[0] += 1
                ins.then_inc(pool_step, 1)
                pool.wait_ge(pool_step, steps_done[0])

            pool.memset(ident[:, :], 0.0).then_inc(pool_step, 1)
            pool.memset(tri_from[:, :], 1.0).then_inc(pool_step, 1)
            pool.memset(tri_before[:, :], 1.0).then_inc(pool_step, 1)
            steps_done[0] += 3
            pool.wait_ge(pool_step, 3)
            pool.affine_select(out=ident[:, :], in_=ident[:, :], compare_op=ALU.not_equal, fill=1.0, base=0,
                               pattern=[[-1, P]], channel_multiplier=1).then_inc(consts, 1)
            pool.affine_select(out=tri_from[:, :], in_=tri_from[:, :], compare_op=ALU.is_ge, fill=0.0, base=0,
                               pattern=[[-1, P]], channel_multiplier=1).then_inc(consts, 1)
            pool.affine_select(out=tri_before[:, :], in_=tri_before[:, :], compare_op=ALU.is_gt, fill=0.0, base=0,
                               pattern=[[1, P]], channel_multiplier=-1).then_inc(consts, 1)
            pool.memset(ones[:, :], 1.0).then_inc(consts, 1)
            pool.dma_start(page_i[:, :], io["page_table"].rearrange("b j -> (b j)").partition_broadcast(P)).then_inc(page_ld, 16)
            pool.iota(row_f[:, :], pattern=[[0, 1]], base=0, channel_multiplier=1,
                      allow_small_or_imprecise_dtypes=True).then_inc(consts, 1)
            pool.wait_ge(rows_ok, 1)

            def load_cache(n):
                kind, b = divmod(n, NB)
                if kind % 2 == 0:
                    src = io["cache_k" if kind == 0 else "cache_v"]
                    for j in range(PAGES):
                        pool.indirect_dma_start(
                            out=cache[:, n % 2, j, :], out_offset=None, in_=src,
                            in_offset=bass.IndirectOffsetOnAxis(ap=page_row[:, b * PAGES + j:b * PAGES + j + 1], axis=0),
                        ).then_inc(cr_ld[n % 2], 16)
                else:
                    src = io["cache_mem_k" if kind == 1 else "cache_mem_v"]
                    pool.dma_start(cache[:, n % 2, :, :], src[b].rearrange("(t p) c -> p t c", p=P)).then_inc(cr_ld[n % 2], 32)

            pool.wait_ge(mt_ps, 4)
            for n in range(4 * NB):
                if n >= 2:
                    pool.wait_ge(cr_used, n - 1)
                load_cache(n)
                if n == 2 * NB + 1:
                    for h in range(HEADS):
                        cut(pool, h, sp_sb, sp_ok, 0.0, sp_cut)
                        cut(pool, h, z_sb, t_ok, -1e30, t_cut)
            pool.wait_ge(wo_ps, 2 * NT)
            pool.iota(tok_f[:, :], pattern=[[P, NT]], base=0, channel_multiplier=1,
                      allow_small_or_imprecise_dtypes=True).then_inc(pool_step, 1)
            pool.iota(steps[:, :], pattern=[[1, EXTRA]], base=0, channel_multiplier=0,
                      allow_small_or_imprecise_dtypes=True).then_inc(pool_step, 1)
            pool.iota(first_slot[:, :], pattern=[[CAP, NE]], base=0, channel_multiplier=0,
                      allow_small_or_imprecise_dtypes=True).then_inc(pool_step, 1)
            pool.iota(rev[:, :], pattern=[[-1, EPG]], base=EPG, channel_multiplier=0,
                      allow_small_or_imprecise_dtypes=True).then_inc(pool_step, 1)
            pool.iota(limits[:, :], pattern=[[CAP, TOK // CAP]], base=CAP, channel_multiplier=0,
                      allow_small_or_imprecise_dtypes=True).then_inc(pool_step, 1)
            pool.memset(low_tri[:, :, :], 1.0).then_inc(pool_step, 1)
            pool.memset(valid[:, :], 1.0).then_inc(pool_step, 1)
            steps_done[0] += 7
            pool.wait_ge(pool_step, steps_done[0])
            link(pool.affine_select(out=low_tri[:, :, :], in_=low_tri[:, :, :], compare_op=ALU.is_gt, fill=0.0, base=0,
                                    pattern=[[1, NE], [-1, NE]], channel_multiplier=0))
            link(pool.affine_select(out=valid[:, NT - 1:NT], in_=valid[:, NT - 1:NT], compare_op=ALU.is_gt, fill=0.0,
                                    base=NB, pattern=[[0, 1]], channel_multiplier=-1))
            link(pool.memset(zero_row[:, :], 0.0))
            pool.dma_start(slot_dram.rearrange("(p n) o -> p (n o)", p=P), zero_row[:, 0:SLOTS // P]).then_inc(ids_st, 16)
            pool.wait_ge(ids_st, 16)
            pool.wait_ge(dest_ok, 1)
            for tt in range(NT):
                for d in (dest1_i, dest2_i):
                    pool.indirect_dma_start(
                        out=slot_dram, out_offset=bass.IndirectOffsetOnAxis(ap=d[0:rows(tt), tt:tt + 1], axis=0),
                        in_=tok_f[0:rows(tt), tt:tt + 1], in_offset=None).then_inc(ids_st, 16)
            pool.wait_ge(ids_st, 16 * (2 * NT + 1))
            pool.dma_start(slot_rows[0:BLOCKS, :], slot_dram.rearrange("(b n) o -> b (n o)", b=BLOCKS)).then_inc(ids_ld, 16)
            pool.wait_ge(ids_ok, 1)
            pool.wait_ge(h_st, 16 * NT)

            def gather(slot, block):
                pool.tensor_copy(slot_now[0:CAP, slot:slot + 1], slot_tok[0:CAP, bass.ds(block, 1)]).then_inc(now_ok, 1)
                pool.wait_ge(now_ok, block + 1)
                pool.sem_inc(carried_pool, 1)
                pool.indirect_dma_start(
                    out=xg[0:CAP, slot, :], out_offset=None, in_=h_dram,
                    in_offset=bass.IndirectOffsetOnAxis(ap=slot_now[0:CAP, slot:slot + 1], axis=0)).then_inc(xg_ld[slot], 16)

            gather(0, 0)
            gather(1, 1)
            with pool.Fori(0, NE // 2 - 1) as i:
                for j in range(2):
                    pool.wait_ge(xgt_ps, 2 * i + j + 1)
                    gather(j, 2 * i + j + 2)
            for j in range(2):
                pool.wait_ge(ydr_st[j], 32 * (NE // 2 + 1))
            pool.wait_ge(over_ok, 1)
            n_extra = pool.value_load(over_i[0:1, EXTRA:EXTRA + 1], min_val=0, max_val=EXTRA)
            with pool.Fori(0, EXTRA) as i:
                with pool.If(n_extra > i):
                    pool.wait_ge(xgt_ps, NE + i)
                    gather(0, NE + i)
                    pool.wait_ge(ydr_st[0], 32 * (NE // 2 + 2) + 32 * i)
            for n in range(2 * NT):
                tt, which = divmod(n, 2)
                if tt >= 2:
                    pool.wait_ge(y_done, tt - 1)
                buf, d = ((ya, dest1_i), (yb, dest2_i))[which]
                pool.indirect_dma_start(
                    out=buf[0:rows(tt), tt % 2, :], out_offset=None, in_=y_dram,
                    in_offset=bass.IndirectOffsetOnAxis(ap=d[0:rows(tt), tt:tt + 1], axis=0)).then_inc(ys_ld[tt % 2], 16)

        @block.tensor
        def _(pe):
            def turn(out, in_, k):
                return pe.transpose(out, in_, ident[0:k, 0:k])

            pe.wait_ge(consts, 5)
            for k in range(KD):
                if k >= 4:
                    pe.wait_ge(xt_lo, k - 3)
                for tt in range(NT - 1):
                    if k == 0:
                        pe.wait_ge(xn_ok, tt + 1)
                    mm = turn(bank(4 + k % 4)[:, tok(tt)], x_in[:, tt, k * P:(k + 1) * P], P)
                mm.then_inc(xt_ps, 1)
            pe.wait_ge(xn_ok, NT)
            for k in range(KD):
                mm = turn(bank(0)[:, k * NB:(k + 1) * NB], x_in[0:NB, NT - 1, k * P:(k + 1) * P], NB)
            mm.then_inc(xst_ps, 1)
            pe.wait_ge(xn_ok, NT + 2)
            for q in range(4):
                pe.wait_ge(xt_lo, q + 5)
                for kk in range(2):
                    for mt in range(2):
                        mm = turn(bank(4 + q)[:, kk * NM + mt * P:kk * NM + (mt + 1) * P],
                                  mem_in[:, mt, (2 * q + kk) * P:(2 * q + kk + 1) * P], P)
                mm.then_inc(mt_ps, 1)

            def three_pass(slot, out):
                for k in range(KD):
                    for a in range(2):
                        cols = slice(a * HALF_TOK, (a + 1) * HALF_TOK)
                        pe.matmul(out[:, a, :], w_hi[:, slot, k, :], xn_hi[:, k, cols], start=(k == 0), stop=False)
                    for a in range(2):
                        cols = slice(a * HALF_TOK, (a + 1) * HALF_TOK)
                        pe.matmul(out[:, a, :], w_hi[:, slot, k, :], xn_lo[:, k, cols], start=False, stop=False)
                    for a in range(2):
                        cols = slice(a * HALF_TOK, (a + 1) * HALF_TOK)
                        mm = pe.matmul(out[:, a, :], w_lo[:, slot, k, :], xn_hi[:, k, cols], start=False, stop=(k == KD - 1))
                return mm

            pe.wait_ge(xst_lo, 1)
            pe.wait_ge(xt_lo, KD)
            with pe.Fori(0, IN_CHUNKS // RING) as i:
                for j in range(RING):
                    pe.wait_ge(split_lo, RING * i + j + 1)
                    pe.wait_ge(pj_sb, RING * i + j + 1)
                    mm = three_pass(j, acc_pair(2 * (j % 2)))
                    mm.then_inc(w_used, 1)
            pe.wait_ge(state_ld, 16)
            pe.wait_ge(mt_sb, 4)
            for q in range(2 * CW):
                mm = turn(bank(4)[:, q * NB:(q + 1) * NB], state[0:NB, q * P:(q + 1) * P], NB)
            mm.then_inc(tp_ps, 1)
            pe.wait_ge(wmem_ld, 16)
            pe.wait_ge(pj_sb, IN_CHUNKS + 2)
            for q in range(4):
                mt, half = divmod(q, 2)
                for k in range(KD):
                    mm = pe.matmul(bank(q), mem_t[:, k, mt * P:(mt + 1) * P], w_mem[:, k, half * W:(half + 1) * W],
                                   start=(k == 0), stop=(k == KD - 1))
                mm.then_inc(mp_ps, 1)

            def job_bank(n):
                if n >= 4:
                    pe.wait_ge(tp_sb, n - 3)
                return bank(4 + n % 4)

            def turn_tokens(n, first, tt):
                out = job_bank(n)
                for c in range(CW):
                    mm = turn(out[0:rows(tt), c * P:(c + 1) * P], proj[:, first + c, tok(tt)], P)
                mm.then_inc(tp_ps, 1)

            for tt in range(NT):
                turn_tokens(JOB_V + tt, V0, tt)
            turn_tokens(JOB_Q, Q0, NT - 1)
            pe.wait_ge(qxsq_ok, 1)
            out = job_bank(JOB_QSS)
            for tt in range(NT):
                for h in range(XH):
                    mm = pe.matmul(out[0:rows(tt), tt * XH + h:tt * XH + h + 1], qx_sq[:, h, tok(tt)], ones[:, 0:1],
                                   start=True, stop=True)
            mm.then_inc(tp_ps, 1)
            pe.wait_ge(qxn_ok, 1)
            turn_tokens(JOB_QX, X0, NT - 1)
            pe.wait_ge(u_ok, 1)
            out = job_bank(JOB_U)
            for c in range(CW):
                mm = turn(out[0:2 + NB, c * P:(c + 1) * P], proj[:, C0 + c, SEQ - 2:TOK], P)
            mm.then_inc(tp_ps, 1)
            pe.wait_ge(mk_ok, 1)
            for q in range(2):
                out = job_bank(JOB_MK + q)
                for hh in range(2):
                    for mt in range(2):
                        mm = turn(out[:, hh * NM + mt * P:hh * NM + (mt + 1) * P],
                                  mk[:, mt, (2 * q + hh) * XD:(2 * q + hh + 1) * XD], P)
                mm.then_inc(tp_ps, 1)
            for tt in range(NT):
                turn_tokens(JOB_K + tt, K0, tt)
            for n in range(2 * NB):
                if n == 0:
                    pe.wait_ge(tp_sb, JOBS)
                if n >= 4:
                    pe.wait_ge(bq_used, n - 3)
                b = n % NB
                q = q_s if n < NB else qx_s
                pe.matmul(bank(4 + n % 4), ident[0:NB, b:b + 1].to_broadcast([NB, P]), q[0:NB, :], start=True,
                          stop=True).then_inc(bq_ps, 1)

            def cross_scores(h):
                if h >= 2:
                    pe.wait_ge(cs_exp, 4 * (h - 1))
                else:
                    pe.wait_ge(mp_sb, 4)
                out = bank(2 * (h % 2), 2).rearrange("p (t m) -> p t m", t=4)
                for tt in range(NT - 1):
                    mm = pe.matmul(out[:, tt, :], proj[:, X0 + h, tok(tt)], mk_t[:, h, :], start=True, stop=True)
                mm.then_inc(cs_ps, 1)

            def cross_values(h):
                pe.wait_ge(cs_nrm, h + 1)
                if h >= 1:
                    pe.wait_ge(ct_sb, h)
                else:
                    pe.wait_ge(bq_used, 2 * NB)
                for mt in range(2):
                    for tt in range(NT - 1):
                        mm = turn(bank(4 + mt)[:, tok(tt)], prob[:, h % 2, tt, mt * P:(mt + 1) * P], P)
                mm.then_inc(ct_ps, 1)
                pe.wait_ge(ct_sb, h + 1)
                if h >= 2:
                    pe.wait_ge(cy_sb, h - 1)
                for mt in range(2):
                    mm = pe.matmul(bank(6 + h % 2), mv[:, mt, h * XD:(h + 1) * XD], prob_t[:, h % 2, mt, :],
                                   start=(mt == 0), stop=(mt == 1))
                mm.then_inc(cy_ps, 1)

            cross_scores(0)
            for h in range(XH):
                if h + 1 < XH:
                    cross_scores(h + 1)
                cross_values(h)

            def scores(h):
                r, c = HD * (h % 2), h // 2
                pe.wait_ge(cs_exp, 4 * XH)
                if h >= 1:
                    pe.wait_ge(z_read, h)
                for kb in range(4):
                    mm = pe.matmul(acc_all[:, SCORE_AT[kb]:SCORE_AT[kb] + SEQ - kb * P],
                                   proj[r:r + HD, K0 + c, kb * P:(kb + 1) * P], proj[r:r + HD, Q0 + c, kb * P:SEQ],
                                   start=True, stop=True, skip_group_check=True)
                mm.then_inc(z_ps, 1)

            def suffix_sums(h):
                pe.wait_ge(sp_cut, 4 * (h + 1))
                if h >= 1:
                    pe.wait_ge(t_ok, h)
                else:
                    pe.wait_ge(cy_sb, XH)
                for kb in range(4):
                    at_kb = 2048 + SCORE_AT[kb]
                    mm = pe.matmul(acc_all[:, at_kb:at_kb + SEQ - kb * P], tri_from[:, :],
                                   sp_sb[:, h % 2, SCORE_AT[kb]:SCORE_AT[kb] + SEQ - kb * P], start=True, stop=(kb == 3),
                                   skip_group_check=True)
                    for later in range(kb + 1, 4):
                        off = (later - kb) * P
                        mm = pe.matmul(acc_all[:, at_kb + off:at_kb + SEQ - kb * P], ones[:, :],
                                       sp_sb[:, h % 2, SCORE_AT[later]:SCORE_AT[later] + SEQ - later * P],
                                       start=False, stop=(later == 3), skip_group_check=True)
                mm.then_inc(s_ps, 1)

            def values(h):
                r, c = HD * (h % 2), h // 2
                pe.wait_ge(a_ok, h + 1)
                if h >= 2:
                    pe.wait_ge(y_sb, h - 1)
                out = bank(3 if h % 2 == 0 else 7)
                for kb in range(4):
                    mm = pe.matmul(out[r:r + HD, kb * P:SEQ], v_tok[:, kb, h * HD:(h + 1) * HD],
                                   a_sb[:, h % 2, SCORE_AT[kb]:SCORE_AT[kb] + SEQ - kb * P],
                                   start=(kb == 0), stop=(kb == 3), skip_group_check=True)
                mm.then_inc(y_ps, 1)

            scores(0)
            for h in range(HEADS):
                if h + 1 < HEADS:
                    scores(h + 1)
                suffix_sums(h)
                if h >= 1:
                    values(h - 1)
            values(HEADS - 1)

            pe.wait_ge(zssp_ok, 1)
            pe.wait_ge(z_read, HEADS)
            cols = NB * HEADS
            pe.matmul(bank(0)[:, 0:cols], tri_from[:, :], z_sp[:, 0, :, :], start=True, stop=False, skip_group_check=True)
            pe.matmul(bank(0)[:, 0:cols], ones[:, :], z_sp[:, 1, :, :], start=False, stop=True, skip_group_check=True)
            pe.matmul(bank(1)[:, 0:cols], tri_from[:, :], z_sp[:, 1, :, :], start=True, stop=True).then_inc(ss_ps, 1)
            pe.wait_ge(zm_ok, 1)
            for mt in range(2):
                mm = turn(bank(2)[0:NB * XH, mt * P:(mt + 1) * P], zm[:, mt, :, :].rearrange("p b h -> p (b h)"), P)
            mm.then_inc(zm_ps, 1)
            pe.wait_ge(as_ok, 1)
            for b in range(NB):
                pair = 2 * NB + b
                pe.wait_ge(cr_ld[pair % 2], 32 * (pair // 2 + 1))
                for c in range(CW):
                    o = bank(3)[:, (b * CW + c) * 2:(b * CW + c) * 2 + 2]
                    if b == 0 and c == 0:
                        pe.wait_ge(y_sb, HEADS)
                    for j in range(PAGES):
                        mm = pe.matmul(o, cache[:, pair % 2, j, c * P:(c + 1) * P], a_s[:, j, b, 2 * c:2 * c + 2],
                                       start=(j == 0), stop=(j == 1))
                mm.then_inc(cr_used, 1)
            pe.wait_ge(pm_ok, 1)
            for mt in range(2):
                mm = turn(bank(4)[:, mt * NB * XH:(mt + 1) * NB * XH], pm[0:NB * XH, mt * P:(mt + 1) * P], NB * XH)
            mm.then_inc(pmt_ps, 1)
            pe.wait_ge(pmt_sb, 1)
            for b in range(NB):
                pair = 3 * NB + b
                pe.wait_ge(cr_ld[pair % 2], 32 * (pair // 2 + 1))
                for h in range(XH):
                    col = b * XH + h
                    for mt in range(2):
                        mm = pe.matmul(bank(5)[:, col:col + 1], cache[:, pair % 2, mt, h * XD:(h + 1) * XD],
                                       pm_t[:, mt, col:col + 1], start=(mt == 0), stop=(mt == 1))
                mm.then_inc(cr_used, 1)
            pe.wait_ge(ym_sb, 1)
            for g in range(3):
                with pe.Fori(0, KD // RING) as i:
                    for j in range(RING):
                        n = KD * g + RING * i + j
                        pe.wait_ge(split_lo, IN_CHUNKS + n + 1)
                        pe.wait_ge(mg_ok, n + 1)
                        mm = three_pass(j, acc_pair(2 * (j % 2)))
                        mm.then_inc(gt_ps, 1)
                        pe.wait_ge(br_ld[j], 16 * (2 * g + i + 1))
                        out = acc_pair(4 + 2 * (j % 2))
                        for c in range(CW):
                            for a in range(2):
                                mm = pe.matmul(out[:, a, :], w_br[:, j, c, :],
                                               proj[:, CW * g + c, a * HALF_TOK:(a + 1) * HALF_TOK],
                                               start=(c == 0), stop=(c == CW - 1))
                        mm.then_inc(br_ps, 1)
            pe.wait_ge(wo_ld, 16)
            for n in range(2 * NT):
                tt, half = divmod(n, 2)
                if n == 0:
                    pe.wait_ge(mg_ok, GATES + 2)
                if n >= 4:
                    pe.wait_ge(x1_ok, n - 3)
                for k in range(KD):
                    mm = pe.matmul(bank(n % 4)[0:rows(tt), :], merged[:, k, tok(tt)], w_o[:, k, half * 512:(half + 1) * 512],
                                   start=(k == 0), stop=(k == KD - 1))
                mm.then_inc(wo_ps, 1)
            for tt in range(NT):
                pe.wait_ge(h_ok, tt + 1)
                for q in range(2):
                    n = 2 * tt + q
                    if n >= 4:
                        pe.wait_ge(ht_sb, n - 3)
                    for kk in range(4):
                        k = 4 * q + kk
                        mm = turn(bank(4 + n % 4)[:, kk * rows(tt):(kk + 1) * rows(tt)],
                                  h_tok[0:rows(tt), tt, k * P:(k + 1) * P], rows(tt))
                    mm.then_inc(ht_ps, 1)
            pe.wait_ge(wr_ld, 16)
            pe.wait_ge(x1_ok, 2 * NT)
            pe.wait_ge(ht_sb, 2 * NT)
            for tt in range(NT):
                for k in range(KD):
                    mm = pe.matmul(bank(0)[0:rows(tt), tt * NR:(tt + 1) * NR], h_t[:, k, tok(tt)], w_r[:, k, :],
                                   start=(k == 0), stop=(k == KD - 1))
            mm.then_inc(lg_ps, 1)
            pe.wait_ge(pick_ok, 1)
            for tt in range(NT):
                o = bank(1)[:, tt * NE:(tt + 1) * NE]
                pe.matmul(o, tri_before[:, :], picked[:, tt, :], start=True, stop=(tt == 0))
                for earlier in range(tt):
                    pe.matmul(o, ones[:, :], picked[:, earlier, :], start=False, stop=(earlier == tt - 1))
            for tt in range(NT):
                mm = pe.matmul(bank(2)[:, 0:NE], ones[:, :], picked[:, tt, :], start=(tt == 0), stop=(tt == NT - 1))
            mm.then_inc(rank_ps, 1)
            pe.wait_ge(ids_ld, 16)
            turn(bank(3)[0:CAP, 0:BLOCKS], slot_rows[0:BLOCKS, :], BLOCKS).then_inc(ids_ps, 1)

            def expert(slot, n, w13_loads, w2_loads, xg_loads):
                pe.wait_ge(xg_ld[slot], xg_loads)
                pe.sem_inc(carried_pe, 1)
                for k in range(KD):
                    mm = turn(bank(4)[:, k * CAP:(k + 1) * CAP], xg[0:CAP, slot, k:D:KD], CAP)
                mm.then_inc(xgt_ps, 1)
                pe.wait_ge(w13_ld[slot], w13_loads)
                pe.wait_ge(xgt_sb, n + 1)
                for k in range(KD):
                    pe.matmul(bank(5)[0:CAP, :], xg_t[:, slot, k, :], w1_sb[slot][:, k, :], start=(k == 0), stop=(k == KD - 1))
                    mm = pe.matmul(bank(5)[CAP:P, :], xg_t[:, slot, k, :], w3_sb[slot][:, k, :], start=(k == 0),
                                   stop=(k == KD - 1))
                mm.then_inc(up_ps, 1)
                pe.wait_ge(up_ok, n + 1)
                for c in range(CW):
                    mm = turn(bank(6)[:, c * P:(c + 1) * P], up_sb[:, slot, c:DE:CW], P)
                mm.then_inc(upt_ps, 1)
                pe.wait_ge(w2_ld[slot], w2_loads)
                pe.wait_ge(actt_ok, n + 1)
                pe.wait_ge(y2_sb, n + 1)
                for c in range(CW):
                    pe.matmul(bank(7)[0:CAP, :], act_t[:, slot, c, :], w2_sb[slot][:, c, 0:DE], start=(c == 0),
                              stop=(c == CW - 1))
                    mm = pe.matmul(bank(7)[CAP:P, :], act_t[:, slot, c, :], w2_sb[slot][:, c, DE:D], start=(c == 0),
                                   stop=(c == CW - 1))
                mm.then_inc(y2_ps, 1)

            with pe.Fori(0, NE // 2) as i:
                for j in range(2):
                    expert(j, 2 * i + j, 32 * i + 32, 16 * i + 16, 16 * i + 16)
            pe.wait_ge(over_ok, 1)
            n_extra = pe.value_load(over_i[0:1, EXTRA:EXTRA + 1], min_val=0, max_val=EXTRA)
            with pe.Fori(0, EXTRA) as i:
                with pe.If(n_extra > i):
                    expert(0, NE + i, 16 * NE + 32 * i + 32, 8 * NE + 16 * i + 16, 8 * NE + 16 * i + 16)

        @block.scalar
        def _(act):
            steps_done = [0]

            def link(ins):
                steps_done[0] += 1
                ins.then_inc(act_step, 1)
                act.wait_ge(act_step, steps_done[0])

            act.wait_ge(ss_init, 1)
            act.wait_ge(x_ld, 32)
            for t in range(NT + 2):
                if t == NT:
                    act.wait_ge(mem_ld, 16)
                n = NB if t == NT - 1 else P
                src = x_in[0:n, t, :] if t < NT else mem_in[:, t - NT, :]
                if t >= 1:
                    act.wait_ge(sumsq_ok, t)
                act.activation(junk[0:n, :], src, ACT.Square, accum_out=ss[0:n, t:t + 1]).then_inc(sumsq_ok, 1)
            act.wait_ge(ms_ok, 1)
            act.activation(rs[:, :], ss[:, :], ACT.Sqrt).then_inc(sqrt_ok, 1)

            act.sem_inc(pj_sb, 2)
            act.sem_inc(y2_sb, 1)
            for j in range(2):
                act.sem_inc(ydr_st[j], 32)

            def split(slot, loads):
                act.wait_ge(w_ld[slot], loads)
                act.activation(w_hi[:, slot, :, :], w_raw[:, slot, :, :], ACT.Copy).then_inc(split_hi, 1)

            split(0, 16)
            split(1, 16)
            act.wait_ge(small_ld, 16 * 7)
            for k in range(KD):
                act.wait_ge(xt_ps, k + 1)
                act.activation(xn_hi[:, k, 0:SEQ], bank(4 + k % 4), ACT.Copy, scale=norm1_t[:, k:k + 1]).then_inc(xt_hi, 1)
            act.wait_ge(xst_f, 1)
            act.activation(xn_hi[:, :, SEQ:TOK], xst_tmp[:, :, :], ACT.Copy).then_inc(xst_hi, 1)
            with act.Fori(0, IN_CHUNKS // RING) as i:
                for j in range(RING):
                    split((j + 2) % RING, 16 * i + (16 if j < 2 else 32))
                    act.wait_ge(w_used, RING * i + j + 1)
                    act.activation(halves(proj[:, bass.ds(RING * i + j, 1), :].rearrange("p o n -> p (o n)")),
                                   acc_pair(2 * (j % 2)), ACT.Copy).then_inc(pj_sb, 1)
            act.wait_ge(mp_ps, 4)
            act.activation(qx_sq[:, :, :], proj[:, X0:X0 + XH, :], ACT.Square).then_inc(qxsq_ok, 1)
            for q in range(4):
                mt, half = divmod(q, 2)
                act.activation((mk, mv)[half][:, mt, :], bank(q), ACT.Copy).then_inc(mp_sb, 1)
            act.wait_ge(qxms_ok, 1)
            act.activation(rs_qx[:, :], ss_qx[:, :], ACT.Sqrt).then_inc(qxrt_ok, 1)
            act.wait_ge(mkms_ok, 1)
            act.activation(rs_mk[:, :], ss_mk[:, :], ACT.Sqrt).then_inc(mkrt_ok, 1)

            for h in range(XH):
                act.wait_ge(cs_mx, h + 1)
                out = bank(2 * (h % 2), 2).rearrange("p (t m) -> p t m", t=4)
                if h >= 2:
                    act.wait_ge(ct_ps, h - 1)
                for tt in range(NT - 1):
                    ins = act.activation(prob[:, h % 2, tt, :], out[:, tt, :], ACT.Exp, bias=xneg[:, h % 2, tt:tt + 1],
                                         scale=rs_qx[:, tt * XH + h:tt * XH + h + 1], accum_out=xsum[:, h % 2, tt:tt + 1])
                    ins.then_inc(cs_exp, 1)
                if h >= 1:
                    cross_out(act, h - 1)
            cross_out(act, XH - 1)

            def front(h):
                act.wait_ge(z_ps, h + 1)
                if h >= 2:
                    act.wait_ge(y_ps, h - 1)
                act.activation(z_sb[:, h % 2, :], acc_all[:, 0:SCORE_N], ACT.Identity, bias=sbias_bc[:, h:h + 1],
                               scale=SB_SCALE)
                act.activation(a_sb[:, h % 2, :], acc_all[:, 0:SCORE_N], ACT.Abs, bias=sbias_bc[:, h:h + 1],
                               scale=SB_SCALE).then_inc(z_read, 1)
                act.wait_ge(z_read, h + 1)
                link(act.activation(a_sb[:, h % 2, :], a_sb[:, h % 2, :], ACT.Exp, scale=-1.0))
                act.activation(a_sb[:, h % 2, :], a_sb[:, h % 2, :], ACT.Ln, bias=1.0).then_inc(ln_ok, 1)

            def weights(h):
                act.wait_ge(t_cut, 4 * (h + 1))
                act.activation(a_sb[:, h % 2, :], z_sb[:, h % 2, :], ACT.Exp).then_inc(a_ok, 1)

            def stick_out(h):
                r, c = HD * (h % 2), h // 2
                act.wait_ge(y_ps, h + 1)
                act.activation(proj[r:r + HD, C0 + c, 0:SEQ], bank(3 if h % 2 == 0 else 7)[r:r + HD, :],
                               ACT.Copy).then_inc(y_sb, 1)

            act.wait_ge(cy_ps, XH)
            front(0)
            for h in range(HEADS):
                if h + 1 < HEADS:
                    front(h + 1)
                weights(h)
                if h >= 1:
                    stick_out(h - 1)
            stick_out(HEADS - 1)

            act.wait_ge(zs_ok, 1)
            link(act.activation(z_abs[:, :, :, :], zs[:, :, :, :], ACT.Abs))
            link(act.activation(z_abs[:, :, :, :], z_abs[:, :, :, :], ACT.Exp, scale=-1.0))
            act.activation(z_abs[:, :, :, :], z_abs[:, :, :, :], ACT.Ln, bias=1.0).then_inc(zsln_ok, 1)
            act.wait_ge(ts_ok, 1)
            act.activation(a_s[:, :, :, :], zs[:, :, :, :], ACT.Exp).then_inc(as_ok, 1)
            act.wait_ge(zm_mx, 1)
            act.activation(pm[0:NB * XH, :], bank(2)[0:NB * XH, 0:NM], ACT.Exp, bias=xneg[0:NB * XH, 0, 0:1],
                           accum_out=xsum[0:NB * XH, 0, 0:1]).then_inc(pm_exp, 1)

            for g in range(3):
                with act.Fori(0, KD // RING) as i:
                    for j in range(RING):
                        n = KD * g + RING * i + j
                        split_next = not (g == 2 and j >= 2)
                        if split_next:
                            split((j + 2) % RING, 16 * (7 + 2 * g) + 16 * i + (16 if j < 2 else 32))
                        else:
                            with act.If(i < 1):
                                split((j + 2) % RING, 16 * (7 + 2 * g) + 16 * i + 32)
                        act.wait_ge(gt_ps, n + 1)
                        act.wait_ge(mg_ok, n + 1)
                        act.activation(halves(gate_sb[:, j % 2, :]), acc_pair(2 * (j % 2)), ACT.Sigmoid).then_inc(gt_sb, 1)

            for tt in range(NT):
                n = rows(tt)
                act.wait_ge(x1_ok, 2 * tt + 2)
                if tt >= 1:
                    act.wait_ge(ss2_ok, tt)
                act.activation(junk2[0:n, :], x1[0:n, tt, :], ACT.Square, accum_out=ss2[0:n, tt:tt + 1]).then_inc(ss2_ok, 1)
                act.wait_ge(ms2_ok, tt + 1)
                act.activation(rs2[0:n, tt:tt + 1], rs2[0:n, tt:tt + 1], ACT.Sqrt).then_inc(rt2_ok, 1)
                act.wait_ge(h_ok, tt + 1)
                act.dma_start(h_dram[tok(tt), :], h_tok[0:n, tt, :]).then_inc(h_st, 16)
            for tt in range(NT):
                n = rows(tt)
                for q in range(2):
                    m = 2 * tt + q
                    act.wait_ge(ht_ps, m + 1)
                    act.activation(h_t[:, 4 * q:4 * q + 4, tok(tt)],
                                   bank(4 + m % 4)[:, 0:4 * n].rearrange("p (k n) -> p k n", k=4), ACT.Copy).then_inc(ht_sb, 1)
            act.wait_ge(lg_max, 1)
            act.activation(g_exp[:, :, :], g_tmp[:, :, :], ACT.Exp).then_inc(lg_exp, 1)
            act.wait_ge(top_ok, 1)
            act.activation(top2[:, :], top1[:, :], ACT.Exp).then_inc(top_exp, 1)

            def block_act(slot, n, store, stored):
                act.wait_ge(upt_ps, n + 1)
                up = bank(6).rearrange("p (c t) -> p c t", c=CW)
                act.activation(gate_h[:, :, :], up[:, :, 0:CAP], ACT.Sigmoid).then_inc(sig_ok, 1)
                act.wait_ge(y2_ps, n + 1)
                act.wait_ge(ydr_st[slot], stored)
                act.activation(y_out[:, slot, :], bank(7), ACT.Copy).then_inc(y2_sb, 1)
                act.wait_ge(y2_sb, n + 2)
                for half in range(2):
                    act.dma_start(store[:, half * DE:(half + 1) * DE], y_out[half * CAP:(half + 1) * CAP, slot, :]
                                  ).then_inc(ydr_st[slot], 16)

            act.wait_ge(fill_st, 16 * (EXTRA * CAP // SEQ))
            with act.Fori(0, NE // 2) as i:
                for j in range(2):
                    block_act(j, 2 * i + j, y_dram[bass.ds((2 * i + j) * CAP, CAP), :], 32 * i + 32)
            act.wait_ge(over_ok, 1)
            n_extra = act.value_load(over_i[0:1, EXTRA:EXTRA + 1], min_val=0, max_val=EXTRA)
            with act.Fori(0, EXTRA) as i:
                with act.If(n_extra > i):
                    block_act(0, NE + i, y_dram[bass.ds((NE + i) * CAP, CAP), :], 32 * (NE // 2 + 1) + 32 * i)

        @block.vector
        def _(dve):
            steps_done = [0]

            def link(ins):
                steps_done[0] += 1
                ins.then_inc(dve_step, 1)
                dve.wait_ge(dve_step, steps_done[0])

            dve.sem_inc(mg_ok, 2)
            dve.memset(ss[:, :], 1.0).then_inc(ss_init, 1)
            dve.wait_ge(sumsq_ok, NT + 2)
            dve.tensor_scalar(ss[:, :], ss[:, :], 1.0 / D, EPS, ALU.mult, ALU.add).then_inc(ms_ok, 1)
            dve.wait_ge(sqrt_ok, 1)
            link(dve.reciprocal(rs[:, :], rs[:, :]))
            for t in range(NT + 2):
                n = NB if t == NT - 1 else P
                v = x_in[0:n, t, :] if t < NT else mem_in[:, t - NT, :]
                dve.tensor_scalar(v, v, rs[0:n, t:t + 1], None, ALU.mult).then_inc(xn_ok, 1)
            dve.wait_ge(small_ld, 16 * 7)
            for k in range(KD):
                dve.wait_ge(xt_hi, k + 1)
                dve.scalar_tensor_tensor(out=xn_lo[:, k, 0:SEQ], in0=bank(4 + k % 4), scalar=norm1_t[:, k:k + 1],
                                         in1=xn_hi[:, k, 0:SEQ].bitcast(F32), op0=ALU.mult, op1=ALU.subtract).then_inc(xt_lo, 1)
            dve.wait_ge(xst_ps, 1)
            dve.tensor_tensor(xst_tmp[:, :, :], bank(0)[:, 0:KD * NB].rearrange("p (k b) -> p k b", k=KD),
                              norm1_t[:, :].unsqueeze(2).to_broadcast([P, KD, NB]), ALU.mult).then_inc(xst_f, 1)
            dve.wait_ge(xst_hi, 1)
            dve.tensor_tensor(xn_lo[:, :, SEQ:TOK], xst_tmp[:, :, :], xn_hi[:, :, SEQ:TOK].bitcast(F32),
                              ALU.subtract).then_inc(xst_lo, 1)
            for q in range(4):
                dve.wait_ge(mt_ps, q + 1)
                dve.tensor_tensor(mem_t[:, 2 * q:2 * q + 2, :], bank(4 + q).rearrange("p (k m) -> p k m", k=2),
                                  mnorm_t[:, 2 * q:2 * q + 2].unsqueeze(2).to_broadcast([P, 2, NM]), ALU.mult).then_inc(mt_sb, 1)

            def rest(slot, m):
                dve.wait_ge(split_hi, m + 1)
                dve.tensor_tensor(w_lo[:, slot, :, :], w_raw[:, slot, :, :], w_hi[:, slot, :, :].bitcast(F32),
                                  ALU.subtract).then_inc(split_lo, 1)

            with dve.Fori(0, IN_CHUNKS // RING) as i:
                for j in range(RING):
                    rest(j, RING * i + j)
            rest(0, IN_CHUNKS)
            rest(1, IN_CHUNKS + 1)
            dve.wait_ge(page_ld, 16)
            dve.wait_ge(consts, 5)
            link(dve.tensor_copy(page_f[:, :], page_i[:, :]))
            link(dve.tensor_scalar(page_f[:, :], page_f[:, :], float(P), row_f[:, 0:1], ALU.mult, ALU.add))
            dve.tensor_copy(page_row[:, :], page_f[:, :]).then_inc(rows_ok, 1)

            dve.wait_ge(tp_ps, 1)
            dve.tensor_copy(state_t[:, :, :, :], bank(4)[:, 0:2 * CW * NB].rearrange("p (j c b) -> p j c b", j=2, c=CW)
                            ).then_inc(tp_sb, 1)
            dve.wait_ge(tp_sb, 1)
            dve.wait_ge(pj_sb, IN_CHUNKS + 2)
            dve.tensor_tensor(proj[:, C0:C0 + CW, :], proj[:, C0:C0 + CW, :], proj[:, U0:U0 + CW, :], ALU.mult).then_inc(u_ok, 1)
            dve.wait_ge(u_ok, 1)
            for c in range(CW):
                last = dve.tensor_scalar(proj[:, c, :], proj[:, C0 + c, :], conv_t[:, 2, c:c + 1], None, ALU.mult)
            link(last)
            for back in (1, 2):
                for c in range(CW):
                    tap = conv_t[:, 2 - back, c:c + 1]
                    dve.scalar_tensor_tensor(out=proj[:, c, back:SEQ], in0=proj[:, C0 + c, 0:SEQ - back], scalar=tap,
                                             in1=proj[:, c, back:SEQ], op0=ALU.mult, op1=ALU.add)
                    last = dve.scalar_tensor_tensor(out=proj[:, c, SEQ:TOK], in0=state_t[:, 2 - back, c, :], scalar=tap,
                                                    in1=proj[:, c, SEQ:TOK], op0=ALU.mult, op1=ALU.add)
                link(last)
            link(dve.tensor_tensor(proj[:, 0:CW, :], proj[:, 0:CW, :], proj[:, B0:B0 + CW, :], ALU.mult))
            dve.wait_ge(qxsq_ok, 1)
            dve.tensor_scalar(proj[:, X0:X0 + XH, :], proj[:, X0:X0 + XH, :], qnorm_t[:, 0:1], None, ALU.mult).then_inc(qxn_ok, 1)

            def take(n, out, src):
                dve.wait_ge(tp_ps, n + 1)
                dve.tensor_copy(out, src).then_inc(tp_sb, 1)

            for tt in range(NT):
                n = JOB_V + tt
                take(n, v_tok[:, tt, :] if tt < NT - 1 else v_s[0:NB, :], bank(4 + n % 4)[0:rows(tt), :])
            take(JOB_Q, q_s[0:NB, :], bank(4 + JOB_Q % 4)[0:NB, :])
            link(dve.memset(ss_qx[:, :], 1.0))
            dve.wait_ge(tp_ps, JOB_QSS + 1)
            full = (NT - 1) * XH
            out = bank(4 + JOB_QSS % 4)
            link(dve.tensor_scalar(ss_qx[:, 0:full], out[:, 0:full], 1.0 / XD, EPS, ALU.mult, ALU.add))
            dve.tensor_scalar(ss_qx[0:NB, full:full + XH], out[0:NB, full:full + XH], 1.0 / XD, EPS, ALU.mult,
                              ALU.add).then_inc(tp_sb, 1)
            dve.wait_ge(tp_sb, JOB_QSS + 1)
            dve.sem_inc(qxms_ok, 1)
            dve.wait_ge(qxrt_ok, 1)
            link(dve.reciprocal(rs_qx[:, :], rs_qx[:, :]))
            dve.tensor_scalar(rs_qx[:, :], rs_qx[:, :], X_SCALE, None, ALU.mult).then_inc(qxrs_ok, 1)
            dve.wait_ge(qxrs_ok, 1)
            dve.wait_ge(tp_ps, JOB_QX + 1)
            dve.tensor_tensor(qx_s[0:NB, :].rearrange("p (h d) -> p h d", h=XH),
                              bank(4 + JOB_QX % 4)[0:NB, :].rearrange("p (h d) -> p h d", h=XH),
                              rs_qx[0:NB, full:full + XH].unsqueeze(2).to_broadcast([NB, XH, XD]), ALU.mult).then_inc(tp_sb, 1)
            take(JOB_U, conv_out[0:2 + NB, :], bank(4 + JOB_U % 4)[0:2 + NB, :])
            dve.wait_ge(mp_sb, 4)
            heads = mk[:, :, :].rearrange("p t (h d) -> p (t h) d", d=XD)
            link(dve.tensor_tensor(mk_sq[:, :, :], mk[:, :, :], mk[:, :, :], ALU.mult))
            link(dve.tensor_reduce(ss_mk[:, :], mk_sq[:, :, :].rearrange("p t (h d) -> p (t h) d", d=XD), AX.X, ALU.add))
            dve.tensor_scalar(ss_mk[:, :], ss_mk[:, :], 1.0 / XD, EPS, ALU.mult, ALU.add).then_inc(mkms_ok, 1)
            dve.wait_ge(mkrt_ok, 1)
            link(dve.reciprocal(rs_mk[:, :], rs_mk[:, :]))
            link(dve.tensor_tensor(heads, heads, rs_mk[:, :].unsqueeze(2).to_broadcast([P, 2 * XH, XD]), ALU.mult))
            dve.tensor_tensor(heads, heads, knorm_bc[:, :].unsqueeze(1).to_broadcast([P, 2 * XH, XD]), ALU.mult).then_inc(mk_ok, 1)
            for q in range(2):
                n = JOB_MK + q
                take(n, mk_t[:, 2 * q:2 * q + 2, :], bank(4 + n % 4).rearrange("p (h m) -> p h m", h=2))
            dve.wait_ge(mk_st, 16)
            for tt in range(NT):
                n = JOB_K + tt
                if 2 <= tt < NT - 1:
                    dve.wait_ge(kout_st[tt % 2], 16)
                take(n, k_out[:, tt % 2, :] if tt < NT - 1 else k_s[0:NB, :], bank(4 + n % 4)[0:rows(tt), :])

            for n in range(2 * NB):
                b = n % NB
                heads_n, dim = (HEADS, HD) if n < NB else (XH, XD)
                dve.wait_ge(bq_ps, n + 1)
                dve.wait_ge(cr_ld[n % 2], 32 * (n // 2 + 1))
                if n >= 1:
                    dve.wait_ge(dot_ok, n)
                dve.tensor_tensor(dot[:, :, :], cache[:, n % 2, :, :], bank(4 + n % 4).unsqueeze(1).to_broadcast([P, 2, W]),
                                  ALU.mult).then_inc(bq_used, 1)
                dve.wait_ge(bq_used, n + 1)
                dve.sem_inc(cr_used, 1)
                out = z_raw[:, :, b, :] if n < NB else zm[:, :, b, :]
                dve.tensor_reduce(out, dot[:, :, :].rearrange("p j (h d) -> p j h d", d=dim), AX.X, ALU.add).then_inc(dot_ok, 1)

            for h in range(XH):
                dve.wait_ge(cs_ps, h + 1)
                if h >= 2:
                    dve.wait_ge(cs_exp, 4 * (h - 1))
                out = bank(2 * (h % 2), 2).rearrange("p (t m) -> p t m", t=4)
                link(dve.tensor_reduce(xmax[:, h % 2, :], out, AX.X, ALU.max))
                dve.scalar_tensor_tensor(out=xneg[:, h % 2, :], in0=xmax[:, h % 2, :], scalar=-1.0, in1=rs_qx[:, h:full:XH],
                                         op0=ALU.mult, op1=ALU.mult).then_inc(cs_mx, 1)
                dve.wait_ge(cs_exp, 4 * (h + 1))
                link(dve.reciprocal(xrec[:, h % 2, :], xsum[:, h % 2, :]))
                dve.tensor_tensor(prob[:, h % 2, :, :], prob[:, h % 2, :, :],
                                  xrec[:, h % 2, :].unsqueeze(2).to_broadcast([P, NT - 1, NM]), ALU.mult).then_inc(cs_nrm, 1)

            def softplus(h):
                dve.wait_ge(ln_ok, h + 1)
                if h >= 2:
                    dve.wait_ge(s_ps, h - 1)
                dve.scalar_tensor_tensor(out=sp_sb[:, h % 2, :], in0=z_sb[:, h % 2, :], scalar=0.0, in1=a_sb[:, h % 2, :],
                                         op0=ALU.max, op1=ALU.add).then_inc(sp_ok, 1)

            softplus(0)
            for h in range(HEADS):
                if h + 1 < HEADS:
                    softplus(h + 1)
                dve.wait_ge(s_ps, h + 1)
                dve.tensor_tensor(z_sb[:, h % 2, :], z_sb[:, h % 2, :], acc_all[:, 2048:2048 + SCORE_N],
                                  ALU.subtract).then_inc(t_ok, 1)
            dve.wait_ge(dot_ok, 2 * NB)
            dve.sem_inc(zm_ok, 1)
            flat = "p j b h -> p (j b) h"
            dve.scalar_tensor_tensor(out=zs[:, :, :, :].rearrange(flat), in0=z_raw[:, :, :, :].rearrange(flat),
                                     scalar=SB_SCALE, in1=sbias_bc[:, :].unsqueeze(1).to_broadcast([P, 2 * NB, HEADS]),
                                     op0=ALU.mult, op1=ALU.add).then_inc(zs_ok, 1)
            dve.wait_ge(zsln_ok, 1)
            dve.scalar_tensor_tensor(out=z_sp[:, :, :, :], in0=zs[:, :, :, :], scalar=0.0, in1=z_abs[:, :, :, :],
                                     op0=ALU.max, op1=ALU.add).then_inc(zssp_ok, 1)
            dve.wait_ge(ss_ps, 1)
            per = NB * HEADS
            dve.tensor_tensor(zs[:, :, :, :].rearrange("p j b h -> p j (b h)"), zs[:, :, :, :].rearrange("p j b h -> p j (b h)"),
                              bank(0, 2).rearrange("p (j n) -> p j n", j=2)[:, :, 0:per], ALU.subtract).then_inc(ts_ok, 1)
            m = NB * XH
            dve.wait_ge(zm_ps, 1)
            link(dve.tensor_reduce(xmax[0:m, 0, 0:1], bank(2)[0:m, 0:NM], AX.X, ALU.max))
            dve.tensor_scalar(xneg[0:m, 0, 0:1], xmax[0:m, 0, 0:1], -1.0, None, ALU.mult).then_inc(zm_mx, 1)
            dve.wait_ge(pm_exp, 1)
            link(dve.reciprocal(xrec[0:m, 0, 0:1], xsum[0:m, 0, 0:1]))
            dve.tensor_scalar(pm[0:m, :], pm[0:m, :], xrec[0:m, 0, 0:1], None, ALU.mult).then_inc(pm_ok, 1)
            dve.wait_ge(pmt_ps, 1)
            dve.tensor_copy(pm_t[:, :, :], bank(4)[:, 0:2 * m].rearrange("p (t n) -> p t n", t=2)).then_inc(pmt_sb, 1)
            dve.wait_ge(cr_used, 3 * NB)
            outs = bank(3)[:, 0:2 * NB * CW].rearrange("p (b c r) -> p c b r", b=NB, c=CW)
            for r in range(2):
                pr = slice(r * HD, (r + 1) * HD)
                dve.tensor_copy(proj[pr, C0:C0 + CW, SEQ:TOK], outs[pr, :, :, r])
            dve.wait_ge(cr_used, 4 * NB)
            dve.tensor_copy(proj[:, B0:B0 + XH, SEQ:TOK], bank(5)[:, 0:m].rearrange("p (b h) -> p h b", b=NB)).then_inc(ym_sb, 1)

            for g in range(3):
                with dve.Fori(0, KD // RING) as i:
                    for j in range(RING):
                        n = KD * g + RING * i + j
                        if not (g == 2 and j >= 2):
                            rest((j + 2) % RING, IN_CHUNKS + 2 + n)
                        else:
                            with dve.If(i < 1):
                                rest((j + 2) % RING, IN_CHUNKS + 2 + n)
                        dve.wait_ge(gt_sb, n + 1)
                        dve.wait_ge(br_ps, n + 1)
                        d = bass.ds(RING * i + j, 1)
                        total = halves(merged[:, d, :].rearrange("p o n -> p (o n)"))
                        gate = halves(gate_sb[:, j % 2, :])
                        part = acc_pair(4 + 2 * (j % 2))
                        if g == 0:
                            dve.tensor_tensor(total, gate, part, ALU.mult).then_inc(mg_ok, 1)
                        else:
                            dve.tensor_tensor(gate, gate, part, ALU.mult).then_inc(term_ok, 1)
                            dve.wait_ge(term_ok, n - KD + 1)
                            dve.tensor_tensor(total, total, gate, ALU.add).then_inc(mg_ok, 1)

            dve.wait_ge(x1_ld, 32)
            dve.wait_ge(n2_ld, 16)
            for tt in range(NT):
                n = rows(tt)
                for half in range(2):
                    q = 2 * tt + half
                    dve.wait_ge(wo_ps, q + 1)
                    v = x1[0:n, tt, half * 512:(half + 1) * 512]
                    dve.tensor_tensor(v, v, bank(q % 4)[0:n, :], ALU.add).then_inc(x1_ok, 1)
                dve.wait_ge(ss2_ok, tt + 1)
                dve.tensor_scalar(rs2[0:n, tt:tt + 1], ss2[0:n, tt:tt + 1], 1.0 / D, EPS, ALU.mult, ALU.add).then_inc(ms2_ok, 1)
                dve.wait_ge(rt2_ok, tt + 1)
                link(dve.reciprocal(rs2[0:n, tt:tt + 1], rs2[0:n, tt:tt + 1]))
                dve.scalar_tensor_tensor(out=h_tok[0:n, tt, :], in0=x1[0:n, tt, :], scalar=rs2[0:n, tt:tt + 1],
                                         in1=norm2_bc[0:n, :], op0=ALU.mult, op1=ALU.mult).then_inc(h_ok, 1)

            def bc(v, shape):
                return v.to_broadcast(shape)

            link(dve.memset(logits[:, :, :], 0.0))
            dve.wait_ge(lg_ps, 1)
            dve.wait_ge(pool_step, POOL_CONSTS)
            lg = bank(0)[:, 0:NT * NR].rearrange("p (t r) -> p t r", t=NT)
            link(dve.tensor_tensor(logits[:, 0:NT - 1, :], lg[:, 0:NT - 1, :], bc(rbias_bc[:, :].unsqueeze(1), [P, NT - 1, NR]), ALU.add))
            link(dve.tensor_tensor(logits[0:NB, NT - 1, :], lg[0:NB, NT - 1, :], rbias_bc[0:NB, :], ALU.add))
            link(dve.tensor_reduce(g_top[:, :], logits[:, :, 0:NG], AX.X, ALU.max))
            dve.tensor_tensor(g_tmp[:, :, :], logits[:, :, 0:NG], bc(g_top[:, :].unsqueeze(2), [P, NT, NG]),
                              ALU.subtract).then_inc(lg_max, 1)

            def first_best(one, values, best, tmp, n):
                link(dve.tensor_tensor(tmp, values, bc(best.unsqueeze(2), [P, NT, n]), ALU.is_equal))
                link(dve.tensor_tensor(tmp, tmp, bc(rev[:, EPG - n:EPG].unsqueeze(1), [P, NT, n]), ALU.mult))
                link(dve.tensor_reduce(best, tmp, AX.X, ALU.max))
                link(dve.tensor_tensor(one, tmp, bc(best.unsqueeze(2), [P, NT, n]), ALU.is_equal))

            dve.wait_ge(lg_exp, 1)
            link(dve.tensor_reduce(g_prob[:, :], g_exp[:, :, :], AX.X, ALU.add))
            link(dve.reciprocal(g_prob[:, :], g_prob[:, :]))
            first_best(g_one[:, :, :], logits[:, :, 0:NG], g_top[:, :], g_tmp[:, :, :], NG)
            link(dve.tensor_tensor(g_one[:, :, :], g_one[:, :, :], bc(valid[:, :].unsqueeze(2), [P, NT, NG]), ALU.mult))
            for tt in range(NT):
                last = dve.tensor_tensor(e_all[:, tt, :, :], logits[:, tt, NG:NR].rearrange("p (g x) -> p g x", g=NG),
                                         bc(g_one[:, tt, :].unsqueeze(2), [P, NG, EPG]), ALU.mult)
            link(last)
            link(dve.tensor_reduce(e_in[:, :, :], e_all[:, :, :, :].rearrange("p t g x -> p t x g"), AX.X, ALU.add))
            link(dve.tensor_reduce(top1[:, :], e_in[:, :, :], AX.X, ALU.max))
            link(dve.tensor_copy(gate1[:, :], top1[:, :]))
            first_best(one1[:, :, :], e_in[:, :, :], top1[:, :], e_tmp[:, :, :], EPG)
            link(dve.scalar_tensor_tensor(out=e_in[:, :, :], in0=one1[:, :, :], scalar=-1e30, in1=e_in[:, :, :],
                                          op0=ALU.mult, op1=ALU.add))
            link(dve.tensor_reduce(top2[:, :], e_in[:, :, :], AX.X, ALU.max))
            link(dve.tensor_tensor(top1[:, :], top2[:, :], gate1[:, :], ALU.subtract))
            first_best(one2[:, :, :], e_in[:, :, :], top2[:, :], e_tmp[:, :, :], EPG)
            dve.sem_inc(top_ok, 1)
            for pick, one in ((pick1, one1), (pick2, one2)):
                for tt in range(NT):
                    last = dve.tensor_tensor(pick[:, tt, :, :], bc(g_one[:, tt, :].unsqueeze(2), [P, NG, EPG]),
                                             bc(one[:, tt, :].unsqueeze(1), [P, NG, EPG]), ALU.mult)
            link(last)
            experts = "p t g x -> p t (g x)"
            dve.tensor_tensor(picked[:, :, :], pick1[:, :, :, :].rearrange(experts), pick2[:, :, :, :].rearrange(experts),
                              ALU.add).then_inc(pick_ok, 1)
            dve.wait_ge(top_exp, 1)
            link(dve.tensor_scalar(gate1[:, :], top2[:, :], 1.0, None, ALU.add))
            link(dve.reciprocal(gate1[:, :], gate1[:, :]))
            link(dve.tensor_tensor(gate1[:, :], gate1[:, :], g_prob[:, :], ALU.mult))
            link(dve.tensor_tensor(gate2[:, :], gate1[:, :], top2[:, :], ALU.mult))
            dve.wait_ge(rank_ps, 1)
            link(dve.tensor_copy(count[:, :], bank(2)[:, 0:NE]))
            link(dve.tensor_tensor(over_part[:, :, :], bc(count[:, :].unsqueeze(2), [P, NE, TOK // CAP]),
                                   bc(limits[:, :].unsqueeze(1), [P, NE, TOK // CAP]), ALU.is_gt))
            link(dve.tensor_reduce(extra[:, :], over_part[:, :, :], AX.X, ALU.add))
            link(dve.tensor_tensor(low_part[:, :, :], low_tri[:, :, :], bc(extra[:, :].unsqueeze(1), [P, NE, NE]), ALU.mult))
            link(dve.tensor_reduce(over_slot[:, :], low_part[:, :, :], AX.X, ALU.add))
            link(dve.tensor_tensor(extra_end[:, :], over_slot[:, :], extra[:, :], ALU.add))
            link(dve.tensor_scalar(over_slot[:, :], over_slot[:, :], float(CAP), float((NE - 1) * CAP), ALU.mult, ALU.add))
            link(dve.tensor_tensor(over_slot[:, :], over_slot[:, :], first_slot[:, :], ALU.subtract))
            rank = bank(1)[:, 0:NT * NE].rearrange("p (t e) -> p t e", t=NT)
            link(dve.tensor_tensor(dest[:, :, :], rank, bc(first_slot[:, :].unsqueeze(1), [P, NT, NE]), ALU.add))
            link(dve.tensor_scalar(over[:, :, :], rank, float(CAP), None, ALU.is_ge))
            link(dve.tensor_tensor(over[:, :, :], over[:, :, :], bc(over_slot[:, :].unsqueeze(1), [P, NT, NE]), ALU.mult))
            link(dve.tensor_tensor(dest[:, :, :], dest[:, :, :], over[:, :, :], ALU.add))
            for pick, d, d_i in ((pick1, dest1, dest1_i), (pick2, dest2, dest2_i)):
                link(dve.tensor_tensor(over[:, :, :], dest[:, :, :], pick[:, :, :, :].rearrange(experts), ALU.mult))
                link(dve.tensor_reduce(d[:, :], over[:, :, :], AX.X, ALU.add))
                link(dve.tensor_copy(d_i[:, :], d[:, :]))
            dve.sem_inc(dest_ok, 1)
            link(dve.tensor_tensor(over_who[:, :, :], bc(steps[:, :].unsqueeze(2), [P, EXTRA, NE]),
                                   bc(extra_end[:, :].unsqueeze(1), [P, EXTRA, NE]), ALU.is_ge))
            link(dve.tensor_reduce(over_cnt[:, :], over_who[:, :, :], AX.X, ALU.add))
            link(dve.tensor_scalar(over_cnt[:, :], over_cnt[:, :], float(NE - 1), None, ALU.min))
            link(dve.tensor_copy(over_i[:, 0:EXTRA], over_cnt[:, :]))
            dve.tensor_copy(over_i[:, EXTRA:EXTRA + 1], extra_end[:, NE - 1:NE]).then_inc(over_ok, 1)
            dve.wait_ge(ids_ps, 1)
            dve.tensor_copy(slot_tok[0:CAP, :], bank(3)[0:CAP, 0:BLOCKS]).then_inc(ids_ok, 1)

            def block_dve(slot, n):
                dve.wait_ge(xgt_ps, n + 1)
                dve.tensor_copy(xg_t[:, slot, :, :], bank(4).rearrange("p (k t) -> p k t", k=KD)).then_inc(xgt_sb, 1)
                dve.wait_ge(up_ps, n + 1)
                dve.tensor_copy(up_sb[:, slot, :], bank(5)).then_inc(up_ok, 1)
                dve.wait_ge(sig_ok, n + 1)
                up = bank(6).rearrange("p (c t) -> p c t", c=CW)
                dve.tensor_tensor(gate_h[:, :, :], gate_h[:, :, :], up[:, :, 0:CAP], ALU.mult).then_inc(half_ok, 1)
                dve.wait_ge(half_ok, n + 1)
                dve.tensor_tensor(act_t[:, slot, :, :], gate_h[:, :, :], up[:, :, CAP:P], ALU.mult).then_inc(actt_ok, 1)

            with dve.Fori(0, NE // 2) as i:
                for j in range(2):
                    block_dve(j, 2 * i + j)
            dve.wait_ge(over_ok, 1)
            n_extra = dve.value_load(over_i[0:1, EXTRA:EXTRA + 1], min_val=0, max_val=EXTRA)
            with dve.Fori(0, EXTRA) as i:
                with dve.If(n_extra > i):
                    block_dve(0, NE + i)
            for tt in range(NT):
                n = rows(tt)
                dve.wait_ge(ys_ld[tt % 2], 32 * (tt // 2 + 1))
                link(dve.scalar_tensor_tensor(out=x1[0:n, tt, :], in0=ya[0:n, tt % 2, :], scalar=gate1[0:n, tt:tt + 1],
                                              in1=x1[0:n, tt, :], op0=ALU.mult, op1=ALU.add))
                dve.scalar_tensor_tensor(out=x1[0:n, tt, :], in0=yb[0:n, tt % 2, :], scalar=gate2[0:n, tt:tt + 1],
                                         in1=x1[0:n, tt, :], op0=ALU.mult, op1=ALU.add).then_inc(y_done, 1)


INS = {
    "x_prompt": (1, SEQ, D), "x_sample": (NB, 1, D), "mem_prompt": (1, NM, D), "cache_k": None, "cache_v": None,
    "cache_mem_k": None, "cache_mem_v": None, "state_conv": None, "page_table": None, "norm1": None, "w_in": None,
    "conv_w": None, "sb_bias": None, "mem_norm": None, "w_mem_kv": None, "q_norm": None, "k_norm": None,
    "w_branch": None, "w_o": None, "norm2": None, "router_w": None, "router_b": None, "w1": None, "w3": None, "w2": None,
}
OUTS = (
    ("y_p", (1, SEQ, D)), ("y_s", (NB, 1, D)), ("k_p", (1, SEQ, HEADS, HD)), ("v_p", (1, SEQ, HEADS, HD)),
    ("conv_p", (1, CONV_K - 1, W)), ("mem_k", (1, NM, XH, XD)), ("mem_v", (1, NM, XH, XD)),
    ("k_s", (NB, 1, HEADS, HD)), ("v_s", (NB, 1, HEADS, HD)), ("conv_s", (NB, CONV_K - 1, W)),
)
FLAT = {
    "y_p": "b s d -> (b s) d", "y_s": "b s d -> (b s) d", "k_p": "b s h d -> (b s) (h d)", "v_p": "b s h d -> (b s) (h d)",
    "conv_p": "b j c -> (b j) c", "mem_k": "b m h d -> (b m) (h d)", "mem_v": "b m h d -> (b m) (h d)",
    "k_s": "b s h d -> (b s) (h d)", "v_s": "b s h d -> (b s) (h d)", "conv_s": "b j c -> b j c",
}


def kernel(**inputs):
    import numpy as np
    import concourse.bacc as bacc
    from concourse.bass_utils import run_bass_kernel_spmd

    a = {name: np.asarray(v) for name, v in inputs.items()}
    a["norm1"] = a["norm1"].reshape(KD, P).T
    a["mem_norm"] = a["mem_norm"].reshape(KD, P).T
    a["q_norm"] = a["q_norm"].reshape(XD, 1)
    a["conv_w"] = a["conv_w"].reshape(CONV_K, CW, P).transpose(2, 0, 1)
    a["w_in"] = a["w_in"].reshape(KD, P, CHUNKS, P).transpose(2, 1, 0, 3)
    a["w_branch"] = a["w_branch"].reshape(3, CW, P, KD, P).transpose(0, 3, 2, 1, 4).reshape(3 * KD, P, CW, P)
    a["router_w"] = np.concatenate([a["w_group"], a["w_router"]], axis=1).reshape(KD, P, NR).transpose(1, 0, 2)
    a["router_b"] = np.concatenate([a["b_group"], a["b_router"]])
    a["cache_k"] = a["cache_k"].reshape(-1, W)
    a["cache_v"] = a["cache_v"].reshape(-1, W)
    a["cache_mem_k"] = a["cache_mem_k"].reshape(NB, NM, W)
    a["cache_mem_v"] = a["cache_mem_v"].reshape(NB, NM, W)

    nc = bacc.Bacc("TRN2", target_bir_lowering=False, num_devices=1)
    arrays, io = {}, {}
    for name in INS:
        v = np.ascontiguousarray(a[name])
        arrays["in_" + name] = v
        io[name] = nc.dram_tensor("in_" + name, v.shape, mybir.dt.from_np(v.dtype), kind="ExternalInput").ap()
    for name, shape in OUTS:
        io[name] = nc.dram_tensor("out_" + name, shape, F32, kind="ExternalOutput").ap().rearrange(FLAT[name])
    build(nc, io)
    r = run_bass_kernel_spmd(nc, [arrays], core_ids=[0])
    return tuple(r.results[0]["out_" + name] for name, _ in OUTS)
```

```python
from contextlib import ExitStack

import concourse.bass as bass
from concourse import mybir

F32 = mybir.dt.float32
F32R = mybir.dt.float32r
I32 = mybir.dt.int32
ALU = mybir.AluOpType
ACT = mybir.ActivationFunctionType
AX = mybir.AxisListType

P = 128
D = 1024
SEQ = 512
NB = 8
TOK = SEQ + NB
NT = SEQ // P + 1
HALF_TOK = TOK // 2
KD = D // P
W = 512
CW = W // P
HEADS, HD = 8, 64
XH, XD = 4, 128
NM = 256
PAST = 256
PAGES = PAST // P
CONV_K = 3
NG, EPG = 4, 8
NE = NG * EPG
NR = NG + NE
DE = 512
EPS = 1e-6
SB_SCALE = HD ** -0.5
X_SCALE = XD ** -0.5

CHUNKS = 6656 // P
IN_CHUNKS = 28
RING = 4
U0, C0, B0, X0, V0, K0, Q0 = (CW * i for i in range(7))
PART1, FIRST = 4 * CW, 3 * CW
BRANCH_ORDER = (0, 2, 1)
YS_AT = (U0, B0, C0)
KEY_RING = 3
COLS = 32
PER = P // COLS

CAP = 64
EXTRA = (2 * TOK) // CAP
BLOCKS = NE + EXTRA
SLOTS = BLOCKS * CAP

SCORE_AT = (0, 512, 1024, 896)
SCORE_N = 1280
SUM_AT = (1536, 2048, 1280, 2432)


def build(nc, io):
    ctx = ExitStack()
    with ctx:
        start = -(-nc.sbuf_base // 64) * 64
        at = {}
        for name, size in (("x", 20480), ("xn", 33280), ("ws", 32768), ("ys", 24960), ("qk", 33280),
                           ("t", 61824), ("misc", 6144)):
            at[name] = start
            start += size

        def place(name, region, offset, shape, dt=F32):
            return nc.alloc_sbuf_tensor_at(name, [P] + list(shape), dt, offset=at[region] + offset)

        used = [0]

        def misc(name, shape, dt=F32):
            n = 1
            for s in shape:
                n *= s
            t = place(name, "misc", used[0], shape, dt)
            used[0] += -(-4 * n // 32) * 32
            assert used[0] <= 6144, used
            return t

        def sem(name):
            return ctx.enter_context(nc.semaphore(name))

        ident = misc("ident", [P])
        tri_from = misc("tri_from", [P])
        tri_before = misc("tri_before", [P])
        ones = misc("ones", [P])
        norm1_t = misc("norm1_t", [KD])
        mnorm_t = misc("mnorm_t", [KD])
        qnorm_t = misc("qnorm_t", [1])
        conv_t = misc("conv_t", [CONV_K, CW])
        sbias_bc = misc("sbias_bc", [HEADS])
        knorm_bc = misc("knorm_bc", [XD])
        rbias_bc = misc("rbias_bc", [NR])
        ss = misc("ss", [NT])
        rs = misc("rs", [NT])
        ss_mem = misc("ss_mem", [2])
        rs_mem = misc("rs_mem", [2])
        ss_mk = misc("ss_mk", [2 * XH])
        rs_mk = misc("rs_mk", [2 * XH])
        ss_qx = misc("ss_qx", [NT * XH])
        rs_qx = misc("rs_qx", [NT * XH])
        page_i = misc("page_i", [NB * PAGES], I32)
        page_f = misc("page_f", [NB * PAGES])
        row_f = misc("row_f", [1])
        page_row = misc("page_row", [NB * PAGES], I32)
        xst_tmp = misc("xst_tmp", [KD, NB])
        state_t = misc("state_t", [2, CW, NB])
        xmax = misc("xmax", [2, 2])
        xneg = misc("xneg", [2, 2])
        xsum = misc("xsum", [2, 2])
        xrec = misc("xrec", [2, 2])
        pm_max = misc("pm_max", [1])
        pm_neg = misc("pm_neg", [1])
        pm_sum = misc("pm_sum", [1])
        pm_rec = misc("pm_rec", [1])

        ss2 = misc("ss2", [NT])
        rs2 = misc("rs2", [NT])

        x_in = place("x_in", "x", 0, [NT, D])
        q_s = place("q_s", "x", 0, [W])
        qx_s = place("qx_s", "x", 2048, [W])
        v_s = place("v_s", "x", 4096, [W])
        k_s = place("k_s", "x", 6144, [W])
        conv_out = place("conv_out", "x", 8192, [W])
        state = place("state", "x", 10240, [2 * W])
        zs = place("zs", "x", 14336, [2, NB, HEADS])
        z_abs = place("z_abs", "x", 14848, [2, NB, HEADS])
        z_sp = place("z_sp", "x", 15360, [2, NB, HEADS])
        z_raw = place("z_raw", "x", 15872, [2, NB, HEADS])
        zm = place("zm", "x", 16384, [2, NB, XH])
        pm = place("pm", "x", 16640, [NM])
        pm_t = place("pm_t", "x", 17664, [2, NB, COLS])
        y_four = [place("y_four0", "x", 12288, [W]), place("y_four1", "x", 2048, [W])]
        vals = place("vals", "x", 4096, [2, PAGES, W])
        x1 = place("x1", "x", 0, [NT, D])
        xn_hi = place("xn_hi", "xn", 0, [KD, TOK], F32R)
        xn_lo = place("xn_lo", "xn", 16640, [KD, TOK], F32R)
        w_raw = place("w_raw", "ws", 0, [RING, KD, P])
        w_lo = place("w_lo", "ws", 0, [RING, KD, P], F32R)
        w_hi = place("w_hi", "ws", 16384, [RING, KD, P], F32R)
        proj = place("proj", "ys", 0, [IN_CHUNKS, TOK])
        w_o = place("w_o_sb", "qk", 0, [KD, D])
        v_tok = place("v_tok", "t", 0, [NT - 1, W])
        mem_t = place("mem_t", "t", 8192, [KD, NM])
        mem_in = place("mem_in", "t", 16384, [2, D])
        junk = place("junk", "t", 24576, [D])
        w_mem = place("w_mem", "t", 29056, [KD, D])
        keys = place("keys", "t", 8192, [KEY_RING, PAGES, W])
        k_out = place("k_out", "t", 16384, [2, W])
        mk = place("mk", "t", 20480, [2, W])
        dot = place("dot", "t", 20480, [2, W])
        mv = place("mv", "t", 24576, [2, W])
        mk_t = place("mk_t", "t", 28672, [XH, NM])
        mk_sq = place("mk_sq", "t", 36992, [2, W])
        a_s = place("a_s", "t", 28672, [2, NB, COLS])
        z_sb = place("z_sb", "t", 8192, [2, SCORE_N])
        sp_sb = place("sp_sb", "t", 18432, [2, SCORE_N])
        gate_sb = place("gate_sb", "t", 32768, [2, TOK])
        merged = place("merged", "t", 36992, [KD, TOK])
        w_br = place("w_br", "t", 53632, [RING, CW, P])
        chunk = 4 * TOK
        qx_sq = place("qx_sq", "ys", U0 * chunk, [XH, TOK])
        prob = place("prob", "ys", C0 * chunk, [2, 2, NM])
        prob_t = place("prob_t", "qk", (V0 - FIRST) * chunk, [2, SEQ])
        a_sb = place("a_sb", "qk", 0, [2, SCORE_N])

        w1_sb = [place("w1_a", "t", 0, [KD, DE]), place("w1_b", "ws", 16384, [KD, DE])]
        w3_sb = [place("w3_a", "t", 16384, [KD, DE]), place("w3_b", "qk", 0, [KD, DE])]
        w2_sb = [place("w2_a", "ws", 0, [CW, D]), place("w2_b", "qk", 16384, [CW, D])]
        h_tok = place("h_tok", "ys", 0, [NT, D])
        norm2_bc = place("norm2_bc", "ys", 20480, [D])
        h_t = place("h_t", "xn", 0, [KD, TOK])
        xg = place("xg", "xn", 16640, [2, D])
        xg_t = place("xg_t", "xn", 24832, [2, KD, CAP])
        y_out = place("y_out", "xn", 28928, [2, DE])
        up_sb = place("up_sb", "t", 36992, [2, DE])
        gate_h = place("gate_h", "t", 41088, [CW, CAP])
        act_t = place("act_t", "t", 42112, [2, CW, CAP])
        low_part = place("low_part", "t", 44160, [NE, NE])
        low_tri = place("low_tri", "t", 48256, [NE, NE])
        w_r = place("w_r", "t", 53632, [KD, NR])
        route_at = [53632 + 1152]

        def route(name, shape, dt=F32):
            n = 1
            for v in shape:
                n *= v
            t = place(name, "t", route_at[0], shape, dt)
            route_at[0] += -(-4 * n // 32) * 32
            assert route_at[0] <= 61824
            return t

        junk2 = place("junk2", "xn", 24832, [D])
        logits = route("logits", [NT, NR])
        g_top = route("g_top", [NT])
        g_exp = route("g_exp", [NT, NG])
        g_prob = route("g_prob", [NT])
        g_one = route("g_one", [NT, NG])
        g_tmp = route("g_tmp", [NT, NG])
        e_all = route("e_all", [NT, NG, EPG])
        e_in = route("e_in", [NT, EPG])
        e_tmp = route("e_tmp", [NT, EPG])
        one1 = route("one1", [NT, EPG])
        one2 = route("one2", [NT, EPG])
        top1 = route("top1", [NT])
        top2 = route("top2", [NT])
        gate1 = route("gate1", [NT])
        gate2 = route("gate2", [NT])
        valid = route("valid", [NT])
        rev = route("rev", [EPG])
        limits = route("limits", [TOK // CAP])
        over_part = route("over_part", [NE, TOK // CAP])
        pick1 = route("pick1", [NT, NG, EPG])
        pick2 = route("pick2", [NT, NG, EPG])
        picked = route("picked", [NT + 1, NE])
        block_at = place("block_at", "t", 52352, [BLOCKS + 1])
        pos_at = place("pos_at", "t", 52576, [CAP])
        place_in = place("place_in", "t", 52832, [2 * NT])
        dest = route("dest", [NT, NE])
        over = route("over", [NT, NE])
        dests = place("dests", "t", 52896, [2 * NT])
        dest1, dest2 = dests[:, 0:NT], dests[:, NT:2 * NT]
        dest1_i = misc("dest1_i", [NT], I32)
        dest2_i = misc("dest2_i", [NT], I32)
        count = misc("count", [NE])
        extra = misc("extra", [NE])
        extra_end = misc("extra_end", [NE])
        first_slot = misc("first_slot", [NE])
        over_slot = misc("over_slot", [NE])
        steps = misc("steps", [EXTRA])
        tok_f = misc("tok_f", [NT])
        over_who = place("over_who", "t", 32768, [EXTRA, NE])
        logits_t = place("logits_t", "t", 32768, [TOK])
        from_block = place("from_block", "t", 34880, [2 * NT, BLOCKS + 1])
        at_pos = place("at_pos", "t", 36992, [2 * NT, CAP])
        in_block = place("in_block", "t", 39552, [2 * NT, BLOCKS])
        over_cnt = misc("over_cnt", [EXTRA])
        over_i = misc("over_i", [EXTRA + 1], I32)

        slot_tok = misc("slot_tok", [BLOCKS], I32)
        slot_now = misc("slot_now", [2], I32)
        ya = place("ya", "t", 0, [NT, D])
        yb = place("yb", "t", 20480, [NT, D])
        h_dram = nc.dram_tensor("h_dram", [TOK, D], F32, kind="Internal").ap()
        y_dram = nc.dram_tensor("y_dram", [SLOTS, D], F32, kind="Internal").ap()


        acc_all = ctx.enter_context(nc.psum_tensor("acc_all", [P, 8 * 512], F32))

        def bank(b, n=1):
            return acc_all[:, b * 512:(b + n) * 512]

        def acc_pair(b):
            return bank(b, 2).rearrange("p (a n) -> p a n", a=2)[:, :, 0:HALF_TOK]

        def halves(tile):
            return tile.rearrange("p (a n) -> p a n", a=2)

        def rows(tt):
            return P if tt < NT - 1 else NB

        def tok(tt):
            return slice(tt * P, tt * P + rows(tt))

        consts = sem("consts")
        norm_ld, small_ld, mem_ld, wmem_ld, state_ld, page_ld = (sem(n) for n in (
            "norm_ld", "small_ld", "mem_ld", "wmem_ld", "state_ld", "page_ld"))
        x_ld = [sem(f"x_ld{t}") for t in range(NT)]
        dve_step, act_step, pool_step = sem("dve_step"), sem("act_step"), sem("pool_step")
        ss_init, sumsq_ok, ms_ok, sqrt_ok, xn_ok = (sem(n) for n in ("ss_init", "sumsq_ok", "ms_ok", "sqrt_ok", "xn_ok"))
        memsq_ok, memn_ok = sem("memsq_ok"), sem("memn_ok")
        MS_MEM, MS_QX, MS_MK = NT + 1, NT + 2, NT + 3
        xt_ps, xt_hi, xt_lo, xst_ps, xst_f, xst_hi, xst_lo = (sem(n) for n in (
            "xt_ps", "xt_hi", "xt_lo", "xst_ps", "xst_f", "xst_hi", "xst_lo"))
        w_ld = [sem(f"w_ld{j}") for j in range(RING)]
        split_hi, split_lo, w_used, pj_sb = (sem(n) for n in ("split_hi", "split_lo", "w_used", "pj_sb"))
        tp_ps, tp_sb = sem("tp_ps"), sem("tp_sb")
        conv_ok, u_ok, qxsq_ok, qxn_ok, qxrs_ok = (sem(n) for n in (
            "conv_ok", "u_ok", "qxsq_ok", "qxn_ok", "qxrs_ok"))
        mk_ok = sem("mk_ok")
        mk_st, kout_st, mid_st, out_st = sem("mk_st"), [sem("kout_st0"), sem("kout_st1")], sem("mid_st"), sem("out_st")
        rows_ok, key_ld = sem("rows_ok"), [sem(f"key_ld{j}") for j in range(KEY_RING)]
        val_ld, val_used = [sem("val_ld0"), sem("val_ld1")], sem("val_used")
        bq_ps, bq_used, dot_ok = sem("bq_ps"), sem("bq_used"), sem("dot_ok")
        cs_ps, cs_mx, cs_exp, cs_nrm, ct_ps, ct_sb, cy_ps, cy_sb = (sem(n) for n in (
            "cs_ps", "cs_mx", "cs_exp", "cs_nrm", "ct_ps", "ct_sb", "cy_ps", "cy_sb"))
        z_ps, z_read, ln_ok, sp_ok, sp_cut, s_ps, t_ok, t_cut, a_ok, y_ps, y_sb = (sem(n) for n in (
            "z_ps", "z_read", "ln_ok", "sp_ok", "sp_cut", "s_ps", "t_ok", "t_cut", "a_ok", "y_ps", "y_sb"))
        zs_ok, zsln_ok, zssp_ok, ss_ps, ts_ok, as_ok = (sem(n) for n in (
            "zs_ok", "zsln_ok", "zssp_ok", "ss_ps", "ts_ok", "as_ok"))
        zm_ps, zm_mx, pm_exp, pm_ok, pmt_ps, pmt_sb = (sem(n) for n in (
            "zm_ps", "zm_mx", "pm_exp", "pm_ok", "pmt_ps", "pmt_sb"))
        yg_sb, yt_ps, yt_sb = (sem(n) for n in ("yg_sb", "yt_ps", "yt_sb"))
        br_ld = [sem(f"br_ld{j}") for j in range(RING)]
        gt_ps, gt_sb, br_ps, term_ok, mg_ok = (sem(n) for n in ("gt_ps", "gt_sb", "br_ps", "term_ok", "mg_ok"))
        GATES, MID_STORES = 3 * KD, 16 * 10
        POOL_CONSTS = 3 + 9 + 2
        fill_st = sem("fill_st")
        carried_pe, carried_pool = sem("carried_pe"), sem("carried_pool")
        wo_ld, x1_ld, n2_ld, wr_ld, wo_ps, x1_ok = (sem(n) for n in ("wo_ld", "x1_ld", "n2_ld", "wr_ld", "wo_ps", "x1_ok"))
        ss2_ok, ms2_ok, rt2_ok, h_ok, ht_ps, ht_sb, h_st = (sem(n) for n in (
            "ss2_ok", "ms2_ok", "rt2_ok", "h_ok", "ht_ps", "ht_sb", "h_st"))
        lgt_ps, lgt_sb, lg_ps, lg_max, lg_exp, top_ok, top_exp, pick_ok, rank_ps, dest_ok, ids_ps, ids_ok, over_ok = (
            sem(n) for n in ("lgt_ps", "lgt_sb", "lg_ps", "lg_max", "lg_exp", "top_ok", "top_exp", "pick_ok", "rank_ps",
                             "dest_ok", "ids_ps", "ids_ok", "over_ok"))
        w13_ld, w2_ld = [sem("w13_ld0"), sem("w13_ld1")], [sem("w2_ld0"), sem("w2_ld1")]
        now_ok, xgt_ps, xgt_sb, up_ps, up_ok, upt_ps, sig_ok, half_ok, actt_ok, y2_ps, y2_sb = (sem(n) for n in (
            "now_ok", "xgt_ps", "xgt_sb", "up_ps", "up_ok", "upt_ps", "sig_ok", "half_ok", "actt_ok", "y2_ps", "y2_sb"))
        xg_ld = [sem("xg_ld0"), sem("xg_ld1")]
        ydr_st, ys_ld, y_done = [sem("ydr_st0"), sem("ydr_st1")], [sem(f"ys_ld{t}") for t in range(NT)], sem("y_done")

        (JOB_QSS, JOB_MT, JOB_V, JOB_STATE, JOB_MP, JOB_Q, JOB_QX, JOB_K, JOB_U, JOB_MK, JOBS) = (
            0, 1, 5, 10, 11, 15, 16, 17, 22, 23, 25)

        START_TILES = (NT - 1, 0, 1, 2, 3)

        def cols(b, first, n):
            return acc_all[:, b * 512 + first:b * 512 + first + n]

        ZM_AT, PMT_AT, SUMS_AT = 0, 256, 0

        def cut(pool, h, tile, ready, fill, done):
            pool.wait_ge(ready, h + 1)
            for kb in range(4):
                v = tile[:, h % 2, SCORE_AT[kb]:SCORE_AT[kb] + P]
                pool.affine_select(out=v, in_=v, compare_op=ALU.is_gt, fill=fill, base=0,
                                   pattern=[[1, P]], channel_multiplier=-1).then_inc(done, 1)

        block = ctx.enter_context(nc.Block())

        @block.sync
        def _(sp):
            for t in START_TILES:
                if t == NT - 1:
                    sp.dma_start(x_in[0:NB, t, :], io["x_sample"].rearrange("b s d -> (b s) d")).then_inc(x_ld[t], 16)
                else:
                    sp.dma_start(x_in[:, t, :], io["x_prompt"].rearrange("b s d -> (b s) d")[tok(t), :]).then_inc(x_ld[t], 16)
            sp.dma_start(norm1_t[:, :], io["norm1"]).then_inc(norm_ld, 16)
            for j in range(2):
                sp.dma_start(w_raw[:, j, :, :], io["w_in"][j]).then_inc(w_ld[j], 16)
            for tile, name in ((mnorm_t, "mem_norm"), (qnorm_t, "q_norm")):
                sp.dma_start(tile[:, :], io[name]).then_inc(small_ld, 16)
            for j in range(2, RING):
                sp.dma_start(w_raw[:, j, :, :], io["w_in"][j]).then_inc(w_ld[j], 16)
            sp.dma_start(mem_in[:, :, :], io["mem_prompt"].rearrange("b (t p) d -> p (b t) d", p=P)).then_inc(mem_ld, 16)
            sp.dma_start(conv_t[:, :, :], io["conv_w"]).then_inc(small_ld, 16)
            sp.dma_start(sbias_bc[:, :], io["sb_bias"].partition_broadcast(P)).then_inc(small_ld, 16)
            sp.dma_start(knorm_bc[:, :], io["k_norm"].partition_broadcast(P)).then_inc(small_ld, 16)
            sp.dma_start(rbias_bc[:, :], io["router_b"].partition_broadcast(P)).then_inc(small_ld, 16)

            def load_chunk(m):
                sp.wait_ge(w_used, m - RING + 1)
                sp.dma_start(w_raw[:, m % RING, :, :], io["w_in"][m]).then_inc(w_ld[m % RING], 16)

            load_chunk(RING)
            load_chunk(RING + 1)
            sp.dma_start(w_mem[:, :, :], io["w_mem_kv"].rearrange("(k p) n -> p k n", p=P)).then_inc(wmem_ld, 16)
            load_chunk(RING + 2)
            load_chunk(RING + 3)
            with sp.Fori(1, PART1 // RING) as i:
                for j in range(RING):
                    sp.wait_ge(w_used, RING * i + j + 1)
                    sp.dma_start(w_raw[:, j, :, :], io["w_in"][RING * i + RING + j]).then_inc(w_ld[j], 16)
            sp.dma_start(state[0:NB, :], io["state_conv"].rearrange("b j c -> b (j c)")).then_inc(state_ld, 16)
            for part in range(EXTRA * CAP // SEQ):
                at_row = NE * CAP + part * SEQ
                sp.dma_start(y_dram[at_row:at_row + SEQ, :], io["x_prompt"].rearrange("b s d -> (b s) d")).then_inc(fill_st, 16)

            def load_branch(n):
                sp.dma_start(w_br[:, n % RING, :, :], io["w_branch"][n]).then_inc(br_ld[n % RING], 16)

            for m in range(PART1, IN_CHUNKS):
                load_chunk(m + RING)
                if m == 20:
                    sp.wait_ge(tp_sb, JOB_V + NT)
                    for tt in range(NT - 1):
                        sp.dma_start(io["v_p"][tok(tt), :], v_tok[:, tt, :]).then_inc(mid_st, 16)
                    sp.dma_start(io["v_s"], v_s[0:NB, :]).then_inc(mid_st, 16)
                if m == 24:
                    sp.wait_ge(tp_sb, JOB_MP + 4)
                    sp.dma_start(io["mem_v"].rearrange("(t p) c -> p t c", p=P), mv[:, :, :]).then_inc(mid_st, 16)
                    for n in range(RING):
                        load_branch(n)
                if m == 25:
                    sp.wait_ge(mk_ok, 1)
                    sp.dma_start(io["mem_k"].rearrange("(t p) c -> p t c", p=P), mk[:, :, :]).then_inc(mk_st, 16)
                    sp.dma_start(io["conv_s"][:, 0, :], state[0:NB, W:2 * W]).then_inc(mid_st, 16)
            for tt in range(NT):
                sp.wait_ge(tp_sb, JOB_K + tt + 1)
                if tt < NT - 1:
                    sp.dma_start(io["k_p"][tok(tt), :], k_out[:, tt % 2, :]).then_inc(kout_st[tt % 2], 16)
                else:
                    sp.dma_start(io["k_s"], k_s[0:NB, :]).then_inc(mid_st, 16)
            sp.wait_ge(tp_sb, JOB_U + 1)
            sp.dma_start(io["conv_p"], conv_out[0:2, :]).then_inc(mid_st, 16)
            sp.dma_start(io["conv_s"][:, 1, :], conv_out[2:2 + NB, :]).then_inc(mid_st, 16)
            w1_d = io["w1"].rearrange("e (p k) n -> e p k n", p=P)
            w3_d = io["w3"].rearrange("e (p k) n -> e p k n", p=P)
            w2_d = io["w2"].rearrange("e (p c) n -> e p c n", p=P)
            with sp.Fori(0, 2 * KD // RING) as i:
                for j in range(RING):
                    sp.wait_ge(mg_ok, RING * i + j + 3)
                    sp.dma_start(w_raw[:, j, :, :], io["w_in"][IN_CHUNKS + RING * i + RING + j]).then_inc(w_ld[j], 16)
                    sp.dma_start(w_br[:, j, :, :], io["w_branch"][RING * i + RING + j]).then_inc(br_ld[j], 16)
            sp.wait_ge(y_sb, HEADS)
            sp.wait_ge(yt_sb, 4)
            sp.dma_start(w_o[:, :, :], io["w_o"].rearrange("(k p) n -> p k n", p=P)).then_inc(wo_ld, 16)
            sp.dma_start(x1[:, 0:NT - 1, :], io["x_prompt"].rearrange("b (t p) d -> p (b t) d", p=P)).then_inc(x1_ld, 16)
            sp.dma_start(x1[0:NB, NT - 1, :], io["x_sample"].rearrange("b s d -> (b s) d")).then_inc(x1_ld, 16)
            for j in range(RING):
                n = 2 * KD + j
                sp.wait_ge(mg_ok, n + 3)
                sp.dma_start(w_raw[:, j, :, :], io["w_in"][IN_CHUNKS + RING + n]).then_inc(w_ld[j], 16)
                load_branch(n + RING)
            sp.wait_ge(mid_st, MID_STORES)
            sp.dma_start(w1_sb[0][:, :, :], w1_d[0]).then_inc(w13_ld[0], 16)
            sp.dma_start(w3_sb[0][:, :, :], w3_d[0]).then_inc(w13_ld[0], 16)
            sp.wait_ge(mg_ok, GATES + 2)
            sp.dma_start(norm2_bc[:, :], io["norm2"].partition_broadcast(P)).then_inc(n2_ld, 16)
            sp.dma_start(w_r[:, :, :], io["router_w"]).then_inc(wr_ld, 16)
            sp.dma_start(w2_sb[0][:, :, :], w2_d[0]).then_inc(w2_ld[0], 16)
            sp.dma_start(w1_sb[1][:, :, :], w1_d[1]).then_inc(w13_ld[1], 16)
            sp.wait_ge(wo_ps, 2 * NT)
            sp.dma_start(w3_sb[1][:, :, :], w3_d[1]).then_inc(w13_ld[1], 16)
            sp.dma_start(w2_sb[1][:, :, :], w2_d[1]).then_inc(w2_ld[1], 16)
            with sp.Fori(0, NE // 2 - 1) as i:
                for j in range(2):
                    sp.wait_ge(up_ps, 2 * i + j + 1)
                    sp.dma_start(w1_sb[j][:, :, :], w1_d[2 * i + 2 + j]).then_inc(w13_ld[j], 16)
                    sp.dma_start(w3_sb[j][:, :, :], w3_d[2 * i + 2 + j]).then_inc(w13_ld[j], 16)
                    sp.wait_ge(y2_ps, 2 * i + j + 1)
                    sp.dma_start(w2_sb[j][:, :, :], w2_d[2 * i + 2 + j]).then_inc(w2_ld[j], 16)
            sp.wait_ge(over_ok, 1)
            n_extra = sp.value_load(over_i[0:1, EXTRA:EXTRA + 1], min_val=0, max_val=EXTRA)
            with sp.If(n_extra > 0):
                with sp.Fori(0, EXTRA) as i:
                    with sp.If(n_extra > i):
                        e = sp.value_load(over_i[0:1, bass.ds(i, 1)], min_val=0, max_val=NE - 1)
                        sp.wait_ge(y2_ps, NE + i)
                        sp.dma_start(w1_sb[0][:, :, :], w1_d[e]).then_inc(w13_ld[0], 16)
                        sp.dma_start(w3_sb[0][:, :, :], w3_d[e]).then_inc(w13_ld[0], 16)
                        sp.dma_start(w2_sb[0][:, :, :], w2_d[e]).then_inc(w2_ld[0], 16)
            sp.wait_ge(mid_st, MID_STORES)
            for tt in range(NT):
                sp.wait_ge(y_done, tt + 1)
                if tt < NT - 1:
                    sp.dma_start(io["y_p"][tok(tt), :], x1[:, tt, :]).then_inc(out_st, 16)
                else:
                    sp.dma_start(io["y_s"], x1[0:NB, tt, :]).then_inc(out_st, 16)
            sp.wait_ge(out_st, 16 * NT)
            sp.wait_ge(mk_st, 16)
            for j in range(2):
                sp.wait_ge(kout_st[j], 32)

        @block.gpsimd
        def _(pool):
            steps_done = [0]

            def link(ins):
                steps_done[0] += 1
                ins.then_inc(pool_step, 1)
                pool.wait_ge(pool_step, steps_done[0])

            pool.memset(ident[:, :], 0.0).then_inc(pool_step, 1)
            pool.memset(tri_from[:, :], 1.0).then_inc(pool_step, 1)
            pool.memset(tri_before[:, :], 1.0).then_inc(pool_step, 1)
            steps_done[0] += 3
            pool.wait_ge(pool_step, 3)
            pool.affine_select(out=ident[:, :], in_=ident[:, :], compare_op=ALU.not_equal, fill=1.0, base=0,
                               pattern=[[-1, P]], channel_multiplier=1).then_inc(consts, 1)
            pool.affine_select(out=tri_from[:, :], in_=tri_from[:, :], compare_op=ALU.is_ge, fill=0.0, base=0,
                               pattern=[[-1, P]], channel_multiplier=1).then_inc(consts, 1)
            pool.affine_select(out=tri_before[:, :], in_=tri_before[:, :], compare_op=ALU.is_gt, fill=0.0, base=0,
                               pattern=[[1, P]], channel_multiplier=-1).then_inc(consts, 1)
            pool.memset(ones[:, :], 1.0).then_inc(consts, 1)
            pool.dma_start(page_i[:, :], io["page_table"].rearrange("b j -> (b j)").partition_broadcast(P)).then_inc(page_ld, 16)
            pool.iota(row_f[:, :], pattern=[[0, 1]], base=0, channel_multiplier=1,
                      allow_small_or_imprecise_dtypes=True).then_inc(consts, 1)
            pool.wait_ge(rows_ok, 1)

            def load_key(n):
                slot, b = n % KEY_RING, n % NB
                if n < NB:
                    pool.dma_start(keys[:, slot, :, :], io["cache_mem_k"][b].rearrange("(t p) c -> p t c", p=P)
                                   ).then_inc(key_ld[slot], 32)
                else:
                    for j in range(PAGES):
                        pool.indirect_dma_start(
                            out=keys[:, slot, j, :], out_offset=None, in_=io["cache_k"],
                            in_offset=bass.IndirectOffsetOnAxis(ap=page_row[:, b * PAGES + j:b * PAGES + j + 1], axis=0),
                        ).then_inc(key_ld[slot], 16)

            def load_val(n):
                slot, b = n % 2, n % NB
                if n >= 2:
                    pool.wait_ge(val_used, n - 1)
                if n < NB:
                    pool.dma_start(vals[:, slot, :, :], io["cache_mem_v"][b].rearrange("(t p) c -> p t c", p=P)
                                   ).then_inc(val_ld[slot], 32)
                else:
                    for j in range(PAGES):
                        pool.indirect_dma_start(
                            out=vals[:, slot, j, :], out_offset=None, in_=io["cache_v"],
                            in_offset=bass.IndirectOffsetOnAxis(ap=page_row[:, b * PAGES + j:b * PAGES + j + 1], axis=0),
                        ).then_inc(val_ld[slot], 16)

            pool.wait_ge(tp_sb, JOB_MP + 4)
            load_key(0)
            load_key(1)
            for j in range(2):
                pool.wait_ge(kout_st[j], 32)
            load_key(2)
            pool.wait_ge(mid_st, MID_STORES)
            load_val(0)
            load_val(1)
            for n in range(KEY_RING, 2 * NB):
                pool.wait_ge(bq_used, n - KEY_RING + 1)
                load_key(n)
                if n >= 2 * NB - 1:
                    for v in range(2, NB):
                        load_val(v)
            for h in range(HEADS):
                if h == 0:
                    cut(pool, 0, sp_sb, sp_ok, 0.0, sp_cut)
                if h + 1 < HEADS:
                    cut(pool, h + 1, sp_sb, sp_ok, 0.0, sp_cut)
                cut(pool, h, z_sb, t_ok, -1e30, t_cut)
                if h < 2:
                    load_val(NB + h)
                elif h < 5:
                    load_val(NB + 2 * h - 2)
                    load_val(NB + 2 * h - 1)
            pool.wait_ge(wo_ps, 2 * NT)
            pool.iota(tok_f[:, :], pattern=[[P, NT]], base=0, channel_multiplier=1,
                      allow_small_or_imprecise_dtypes=True).then_inc(pool_step, 1)
            pool.iota(steps[:, :], pattern=[[1, EXTRA]], base=0, channel_multiplier=0,
                      allow_small_or_imprecise_dtypes=True).then_inc(pool_step, 1)
            pool.iota(first_slot[:, :], pattern=[[CAP, NE]], base=0, channel_multiplier=0,
                      allow_small_or_imprecise_dtypes=True).then_inc(pool_step, 1)
            pool.iota(rev[:, :], pattern=[[-1, EPG]], base=EPG, channel_multiplier=0,
                      allow_small_or_imprecise_dtypes=True).then_inc(pool_step, 1)
            pool.iota(limits[:, :], pattern=[[CAP, TOK // CAP]], base=CAP, channel_multiplier=0,
                      allow_small_or_imprecise_dtypes=True).then_inc(pool_step, 1)
            pool.iota(block_at[:, :], pattern=[[CAP, BLOCKS + 1]], base=0, channel_multiplier=0,
                      allow_small_or_imprecise_dtypes=True).then_inc(pool_step, 1)
            pool.iota(pos_at[:, :], pattern=[[1, CAP]], base=-CAP, channel_multiplier=0,
                      allow_small_or_imprecise_dtypes=True).then_inc(pool_step, 1)
            pool.memset(low_tri[:, :, :], 1.0).then_inc(pool_step, 1)
            pool.memset(valid[:, :], 1.0).then_inc(pool_step, 1)
            steps_done[0] += 9
            pool.wait_ge(pool_step, steps_done[0])
            link(pool.affine_select(out=low_tri[:, :, :], in_=low_tri[:, :, :], compare_op=ALU.is_gt, fill=0.0, base=0,
                                    pattern=[[1, NE], [-1, NE]], channel_multiplier=0))
            link(pool.affine_select(out=valid[:, NT - 1:NT], in_=valid[:, NT - 1:NT], compare_op=ALU.is_gt, fill=0.0,
                                    base=NB, pattern=[[0, 1]], channel_multiplier=-1))
            pool.wait_ge(ids_ok, 1)
            pool.wait_ge(h_st, 16 * NT)

            def gather(slot, block):
                pool.tensor_copy(slot_now[0:CAP, slot:slot + 1], slot_tok[0:CAP, bass.ds(block, 1)]).then_inc(now_ok, 1)
                pool.wait_ge(now_ok, block + 1)
                pool.sem_inc(carried_pool, 1)
                pool.indirect_dma_start(
                    out=xg[0:CAP, slot, :], out_offset=None, in_=h_dram,
                    in_offset=bass.IndirectOffsetOnAxis(ap=slot_now[0:CAP, slot:slot + 1], axis=0)).then_inc(xg_ld[slot], 16)

            gather(0, 0)
            gather(1, 1)
            with pool.Fori(0, NE // 2 - 1) as i:
                for j in range(2):
                    pool.wait_ge(xgt_ps, 2 * i + j + 1)
                    gather(j, 2 * i + j + 2)
            for j in range(2):
                pool.wait_ge(ydr_st[j], 32 * (NE // 2 + 1))
            pool.wait_ge(over_ok, 1)
            n_extra = pool.value_load(over_i[0:1, EXTRA:EXTRA + 1], min_val=0, max_val=EXTRA)
            with pool.If(n_extra > 0):
                with pool.Fori(0, EXTRA) as i:
                    with pool.If(n_extra > i):
                        pool.wait_ge(xgt_ps, NE + i)
                        gather(0, NE + i)
                        pool.wait_ge(ydr_st[0], 32 * (NE // 2 + 2) + 32 * i)
            for n in range(2 * NT):
                tt, which = divmod(n, 2)
                buf, d = ((ya, dest1_i), (yb, dest2_i))[which]
                pool.indirect_dma_start(
                    out=buf[0:rows(tt), tt, :], out_offset=None, in_=y_dram,
                    in_offset=bass.IndirectOffsetOnAxis(ap=d[0:rows(tt), tt:tt + 1], axis=0)).then_inc(ys_ld[tt], 16)

        @block.tensor
        def _(pe):
            def turn(out, in_, k):
                return pe.transpose(out, in_, ident[0:k, 0:k])

            pe.wait_ge(consts, 5)
            pe.wait_ge(xn_ok, 1)
            for k in range(KD):
                mm = turn(cols(2, 384 + k * NB, NB), x_in[0:NB, NT - 1, k * P:(k + 1) * P], NB)
            mm.then_inc(xst_ps, 1)

            for tt in range(NT - 1):
                pe.wait_ge(xn_ok, tt + 2)
                for k in range(4):
                    mm = turn(bank(4 + k)[:, tok(tt)], x_in[:, tt, k * P:(k + 1) * P], P)
                    if tt == NT - 2:
                        mm.then_inc(xt_ps, 1)

            def three_products(slot, k, out):
                for w, x, first, last in ((w_hi, xn_hi, k == 0, False), (w_hi, xn_lo, False, False),
                                          (w_lo, xn_hi, False, k == KD - 1)):
                    for a in range(2):
                        mm = pe.matmul(out[:, a, :], w[:, slot, k, :], x[:, k, a * HALF_TOK:(a + 1) * HALF_TOK],
                                       start=first, stop=last)
                return mm

            def three_pass(slot, out):
                for k in range(KD):
                    mm = three_products(slot, k, out)
                return mm

            pe.wait_ge(split_lo, 1)
            pe.wait_ge(xst_lo, 1)
            for k in range(KD):
                pe.wait_ge(xt_lo, k + 1)
                if k + 4 < KD:
                    for tt in range(NT - 1):
                        mm = turn(bank(4 + k)[:, tok(tt)], x_in[:, tt, (k + 4) * P:(k + 5) * P], P)
                    mm.then_inc(xt_ps, 1)
                three_products(0, k, acc_pair(0))
                pe.wait_ge(split_lo, 2)
                mm = three_products(1, k, acc_pair(2))
            mm.then_inc(w_used, 2)

            def project(m, slot):
                pe.wait_ge(split_lo, m + 1)
                pe.wait_ge(pj_sb, m + 1)
                three_pass(slot, acc_pair(2 * (slot % 2))).then_inc(w_used, 1)

            project(2, 2)
            project(3, 3)
            with pe.Fori(1, PART1 // RING) as i:
                for j in range(RING):
                    project(RING * i + j, j)

            def job_bank(n):
                if n >= 4:
                    pe.wait_ge(tp_sb, n - 3)
                return bank(4 + n % 4)

            def turn_tokens(n, first, tt):
                out = job_bank(n)
                for c in range(CW):
                    mm = turn(out[0:rows(tt), c * P:(c + 1) * P], proj[:, first + c, tok(tt)], P)
                mm.then_inc(tp_ps, 1)

            def turn_memory(q):
                out = job_bank(JOB_MT + q)
                for kk in range(2):
                    for mt in range(2):
                        mm = turn(out[:, kk * NM + mt * P:kk * NM + (mt + 1) * P],
                                  mem_in[:, mt, (2 * q + kk) * P:(2 * q + kk + 1) * P], P)
                mm.then_inc(tp_ps, 1)

            def project_memory(q):
                mt, half = divmod(q, 2)
                out = job_bank(JOB_MP + q)
                for k in range(KD):
                    mm = pe.matmul(out, mem_t[:, k, mt * P:(mt + 1) * P], w_mem[:, k, half * W:(half + 1) * W],
                                   start=(k == 0), stop=(k == KD - 1))
                mm.then_inc(tp_ps, 1)

            for m in range(PART1, IN_CHUNKS):
                project(m, m % RING)
                if m == 16:
                    pe.wait_ge(qxsq_ok, 1)
                    out = job_bank(JOB_QSS)
                    for tt in range(NT):
                        for h in range(XH):
                            mm = pe.matmul(out[0:rows(tt), tt * XH + h:tt * XH + h + 1], qx_sq[:, h, tok(tt)],
                                           ones[:, 0:1], start=True, stop=True)
                    mm.then_inc(tp_ps, 1)
                    pe.wait_ge(memn_ok, 2)
                elif m in (17, 18):
                    turn_memory(2 * (m - 17))
                    turn_memory(2 * (m - 17) + 1)
                elif m == 19:
                    for tt in range(NT):
                        turn_tokens(JOB_V + tt, V0, tt)
                    pe.wait_ge(state_ld, 16)
                    out = job_bank(JOB_STATE)
                    for q in range(2 * CW):
                        mm = turn(out[:, q * NB:(q + 1) * NB], state[0:NB, q * P:(q + 1) * P], NB)
                    mm.then_inc(tp_ps, 1)
                elif m in (20, 21, 22, 23):
                    pe.wait_ge(wmem_ld, 16)
                    if m == 20:
                        pe.wait_ge(tp_sb, JOB_MT + 4)
                    project_memory(m - 20)
                elif m == 24:
                    turn_tokens(JOB_Q, Q0, NT - 1)
                    pe.wait_ge(qxn_ok, 1)
                    turn_tokens(JOB_QX, X0, NT - 1)
                elif m == 25:
                    for tt in range(3):
                        turn_tokens(JOB_K + tt, K0, tt)
                elif m == 26:
                    for tt in range(3, NT):
                        turn_tokens(JOB_K + tt, K0, tt)
                elif m == 27:
                    pe.wait_ge(u_ok, CW)
                    out = job_bank(JOB_U)
                    for c in range(CW):
                        mm = turn(out[0:2 + NB, c * P:(c + 1) * P], proj[:, C0 + c, SEQ - 2:TOK], P)
                    mm.then_inc(tp_ps, 1)
                    pe.wait_ge(mk_ok, 1)
                    for q in range(2):
                        out = job_bank(JOB_MK + q)
                        for hh in range(2):
                            for mt in range(2):
                                mm = turn(out[:, hh * NM + mt * P:hh * NM + (mt + 1) * P],
                                          mk[:, mt, (2 * q + hh) * XD:(2 * q + hh + 1) * XD], P)
                        mm.then_inc(tp_ps, 1)

            def branch(slot, group, out):
                first = YS_AT[group]
                for c in range(CW):
                    for a in range(2):
                        mm = pe.matmul(out[:, a, :], w_br[:, slot, c, :],
                                       proj[:, first + c, a * HALF_TOK:(a + 1) * HALF_TOK],
                                       start=(c == 0), stop=(c == CW - 1))
                return mm

            def broadcast_query(n):
                if n >= 1:
                    pe.wait_ge(bq_used, n)
                b = n % NB
                q = qx_s if n < NB else q_s
                pe.matmul(bank(4), ident[0:NB, b:b + 1].to_broadcast([NB, P]), q[0:NB, :], start=True,
                          stop=True).then_inc(bq_ps, 1)

            def cross_scores(u):
                h, part = divmod(u, 2)
                if u >= 1:
                    pe.wait_ge(cs_exp, 2 * u)
                out = bank(6).rearrange("p (t m) -> p t m", t=2)
                for t in range(2):
                    mm = pe.matmul(out[:, t, :], proj[:, X0 + h, tok(2 * part + t)], mk_t[:, h, :], start=True, stop=True)
                mm.then_inc(cs_ps, 1)

            def turn_probs(u):
                h, part = divmod(u, 2)
                pe.wait_ge(cs_nrm, u + 1)
                if u >= 1:
                    pe.wait_ge(ct_sb, u)
                if h >= 1:
                    pe.wait_ge(cy_sb, h)
                for mt in range(2):
                    for t in range(2):
                        mm = turn(bank(7)[:, (2 * mt + t) * P:(2 * mt + t + 1) * P], prob[:, u % 2, t, mt * P:(mt + 1) * P], P)
                mm.then_inc(ct_ps, 1)

            def cross_values(h):
                pe.wait_ge(ct_sb, 2 * h + 2)
                for mt in range(2):
                    mm = pe.matmul(bank(7), mv[:, mt, h * XD:(h + 1) * XD], prob_t[:, mt, :], start=(mt == 0), stop=(mt == 1))
                mm.then_inc(cy_ps, 1)

            def two_values(kind, b, weight):
                pe.wait_ge(val_ld[0], 32 * ((kind * NB + b) // 2 + 1))
                pe.wait_ge(val_ld[1], 32 * ((kind * NB + b) // 2 + 1))
                for j in range(2):
                    for s in (b, b + 1):
                        at = COLS * (s % PER)
                        mm = pe.matmul(bank(5)[at:at + COLS, :], weight[:, j, s, :], vals[:, s % 2, j, :], start=(j == 0),
                                       stop=(j == 1))
                mm.then_inc(val_used, 2)

            def turn_four(kind, g, b):
                pe.wait_ge(yg_sb, 4 * kind + 2 * g + 2)
                for c in range(CW):
                    mm = turn(bank(b)[:, c * P:(c + 1) * P], y_four[g][:, c * P:(c + 1) * P], P)
                mm.then_inc(yt_ps, 1)

            def point(p):
                broadcast_query(p)
                if p % 2 == 0:
                    cross_scores(p // 2)
                else:
                    turn_probs(p // 2)
                if p % 4 == 0 and p >= 4:
                    cross_values(p // 4 - 1)
                if p == 9:
                    pe.wait_ge(dot_ok, NB)
                    for mt in range(2):
                        mm = turn(cols(5, ZM_AT + mt * P, P)[0:NB * XH, :], zm[:, mt, :, :].rearrange("p b h -> p (b h)"), P)
                    mm.then_inc(zm_ps, 1)
                if p == 11:
                    pe.wait_ge(pm_ok, 1)
                    for mt in range(2):
                        mm = turn(cols(5, PMT_AT + mt * NB * XH, NB * XH), pm[0:NB * XH, mt * P:(mt + 1) * P], NB * XH)
                    mm.then_inc(pmt_ps, 1)
                if p >= 12:
                    pe.wait_ge(pmt_sb, 1)
                    if p >= 14:
                        pe.wait_ge(yg_sb, 2)
                    two_values(0, 2 * (p - 12), pm_t)

            pe.wait_ge(tp_sb, JOBS)
            for n in range(KD):
                pe.wait_ge(split_lo, IN_CHUNKS + n + 1)
                if n == 0:
                    pe.wait_ge(pj_sb, IN_CHUNKS + 2)
                else:
                    pe.wait_ge(gt_sb, n)
                three_pass(n % RING, acc_pair(0)).then_inc(gt_ps, 1)
                point(2 * n)
                pe.wait_ge(br_ld[n % RING], 16 * (n // RING + 1))
                if n == 0:
                    pe.wait_ge(conv_ok, 1)
                pe.wait_ge(mg_ok, n + 2)
                branch(n % RING, 0, acc_pair(2)).then_inc(br_ps, 1)
                point(2 * n + 1)
            cross_values(XH - 1)
            pe.wait_ge(yg_sb, 4)
            turn_four(0, 0, 5)
            pe.wait_ge(bq_used, 2 * NB)
            turn_four(0, 1, 4)

            def scores(h):
                r, c = HD * (h % 2), h // 2
                if h >= 1:
                    pe.wait_ge(z_read, h)
                for kb in range(4):
                    mm = pe.matmul(acc_all[:, SCORE_AT[kb]:SCORE_AT[kb] + SEQ - kb * P],
                                   proj[r:r + HD, K0 + c, kb * P:(kb + 1) * P], proj[r:r + HD, Q0 + c, kb * P:SEQ],
                                   start=True, stop=True, skip_group_check=True)
                mm.then_inc(z_ps, 1)

            def suffix_sums(h):
                pe.wait_ge(sp_cut, 4 * (h + 1))
                if h >= 1:
                    pe.wait_ge(t_ok, h)
                for kb in (0, 1, 3, 2):
                    if kb == 2 and h + 1 < HEADS:
                        pe.wait_ge(z_read, h + 2)
                    mm = pe.matmul(acc_all[:, SUM_AT[kb]:SUM_AT[kb] + SEQ - kb * P], tri_from[:, :],
                                   sp_sb[:, h % 2, SCORE_AT[kb]:SCORE_AT[kb] + SEQ - kb * P], start=True, stop=(kb == 3),
                                   skip_group_check=True)
                    for later in range(kb + 1, 4):
                        off = (later - kb) * P
                        mm = pe.matmul(acc_all[:, SUM_AT[kb] + off:SUM_AT[kb] + SEQ - kb * P], ones[:, :],
                                       sp_sb[:, h % 2, SCORE_AT[later]:SCORE_AT[later] + SEQ - later * P],
                                       start=False, stop=(later == 3), skip_group_check=True)
                mm.then_inc(s_ps, 1)

            def values(h):
                r = HD * (h % 2)
                pe.wait_ge(a_ok, h + 1)
                if h >= 2:
                    pe.wait_ge(y_sb, h - 1)
                for kb in range(4):
                    mm = pe.matmul(bank(5)[r:r + HD, kb * P:SEQ], v_tok[:, kb, h * HD:(h + 1) * HD],
                                   a_sb[:, h % 2, SCORE_AT[kb]:SCORE_AT[kb] + SEQ - kb * P],
                                   start=(kb == 0), stop=(kb == 3), skip_group_check=True)
                mm.then_inc(y_ps, 1)



            pe.wait_ge(mg_ok, KD + 2)
            pe.wait_ge(gt_sb, KD)
            pe.wait_ge(yt_sb, 2)
            scores(0)
            for h in range(HEADS):
                n = KD + h
                pe.wait_ge(split_lo, IN_CHUNKS + n + 1)
                if h == 0:
                    pe.wait_ge(cs_exp, 4 * XH)
                    pe.wait_ge(cy_sb, XH)
                    pe.wait_ge(bq_used, 2 * NB)
                else:
                    pe.wait_ge(term_ok, h)
                three_pass(n % RING, acc_pair(6)).then_inc(gt_ps, 1)
                if h + 1 < HEADS:
                    scores(h + 1)
                suffix_sums(h)
                if h >= 2:
                    pe.wait_ge(y_sb, h - 1)
                    if h < 6:
                        pe.wait_ge(as_ok, 1)
                        two_values(1, 2 * (h - 2), a_s)
                    else:
                        turn_four(1, h - 6, 5)
                pe.wait_ge(br_ld[n % RING], 16 * (n // RING + 1))
                pe.wait_ge(gt_sb, n + 1)
                branch(n % RING, 1, acc_pair(6)).then_inc(br_ps, 1)
                if h == 0:
                    pe.wait_ge(zssp_ok, 1)
                    per = NB * HEADS
                    pe.matmul(cols(5, SUMS_AT, per), tri_from[:, :], z_sp[:, 0, :, :], start=True, stop=False,
                              skip_group_check=True)
                    pe.matmul(cols(5, SUMS_AT, per), ones[:, :], z_sp[:, 1, :, :], start=False, stop=True,
                              skip_group_check=True)
                    pe.matmul(cols(5, SUMS_AT + per, per), tri_from[:, :], z_sp[:, 1, :, :], start=True, stop=True,
                              skip_group_check=True).then_inc(ss_ps, 1)
                else:
                    if h == 1:
                        pe.wait_ge(ts_ok, 1)
                    elif h < 6:
                        pe.wait_ge(yg_sb, 4 + h - 1)
                    else:
                        pe.wait_ge(yt_sb, 2 + h - 5)
                    values(h - 1)
            values(HEADS - 1)

            pe.wait_ge(z_read, HEADS)
            pe.wait_ge(t_ok, HEADS)
            pe.wait_ge(y_sb, HEADS)
            pe.wait_ge(yt_sb, 4)
            with pe.Fori(0, KD // RING) as i:
                for j in range(RING):
                    n = 2 * KD + RING * i + j
                    pe.wait_ge(split_lo, IN_CHUNKS + n + 1)
                    pe.wait_ge(gt_sb, n)
                    three_pass(j, acc_pair(0)).then_inc(gt_ps, 1)
                    pe.wait_ge(br_ld[j], 16 * (i + 2 * KD // RING + 1))
                    pe.wait_ge(term_ok, n - KD)
                    branch(j, 2, acc_pair(2)).then_inc(br_ps, 1)
            pe.wait_ge(wo_ld, 16)
            def merge_out(n):
                tt, half = divmod(n, 2)
                if n >= 4:
                    pe.wait_ge(x1_ok, n - 3)
                for k in range(KD):
                    mm = pe.matmul(bank(n % 4)[0:rows(tt), :], merged[:, k, tok(tt)], w_o[:, k, half * 512:(half + 1) * 512],
                                   start=(k == 0), stop=(k == KD - 1))
                mm.then_inc(wo_ps, 1)

            def turn_h(tt):
                pe.wait_ge(h_ok, tt + 1)
                for q in range(2):
                    n = 2 * tt + q
                    if n >= 2:
                        pe.wait_ge(ht_sb, n - 1)
                    for kk in range(4):
                        k = 4 * q + kk
                        mm = turn(bank(4 + n % 2)[:, kk * rows(tt):(kk + 1) * rows(tt)],
                                  h_tok[0:rows(tt), tt, k * P:(k + 1) * P], rows(tt))
                    mm.then_inc(ht_ps, 1)

            def route_h(tt):
                pe.wait_ge(ht_sb, 2 * tt + 2)
                out = bank(6)[0:NR, tok(tt)] if tt < NT - 1 else bank(7)[0:NR, 0:NB]
                for k in range(KD):
                    mm = pe.matmul(out, w_r[:, k, :], h_t[:, k, tok(tt)], start=(k == 0), stop=(k == KD - 1))
                return mm

            pe.wait_ge(mg_ok, GATES + 2)
            for tt in range(NT):
                merge_out(2 * tt)
                merge_out(2 * tt + 1)
                if tt == 0:
                    pe.wait_ge(wr_ld, 16)
                else:
                    turn_h(tt - 1)
                if tt >= 2:
                    route_h(tt - 2)
            route_h(NT - 2)
            turn_h(NT - 1)
            route_h(NT - 1).then_inc(lgt_ps, 1)
            pe.wait_ge(lgt_sb, 2)
            pe.wait_ge(x1_ok, 2 * NT)
            for tt in range(NT):
                mm = turn(bank(0)[0:rows(tt), tt * NR:(tt + 1) * NR], logits_t[0:NR, tok(tt)], NR)
            mm.then_inc(lg_ps, 1)
            pe.wait_ge(pick_ok, 1)
            o = bank(1)[:, 0:(NT + 1) * NE]
            pe.matmul(o, tri_before[:, :], picked[:, :, :], start=True, stop=False, skip_group_check=True)
            for back in range(1, NT + 1):
                mm = pe.matmul(o[:, back * NE:], ones[:, :], picked[:, 0:NT + 1 - back, :], start=False, stop=(back == NT),
                               skip_group_check=True)
            mm.then_inc(rank_ps, 1)
            pe.wait_ge(dest_ok, 1)
            for q in range(2 * NT):
                n = rows(q % NT)
                mm = pe.matmul(bank(3)[0:CAP, 0:BLOCKS], at_pos[0:n, q, :], in_block[0:n, q, :], start=(q == 0),
                               stop=(q == 2 * NT - 1))
            mm.then_inc(ids_ps, 1)

            def expert(slot, n, w13_loads, w2_loads, xg_loads):
                pe.wait_ge(xg_ld[slot], xg_loads)
                pe.sem_inc(carried_pe, 1)
                for k in range(KD):
                    mm = turn(bank(4)[:, k * CAP:(k + 1) * CAP], xg[0:CAP, slot, k:D:KD], CAP)
                mm.then_inc(xgt_ps, 1)
                pe.wait_ge(w13_ld[slot], w13_loads)
                pe.wait_ge(xgt_sb, n + 1)
                for k in range(KD):
                    pe.matmul(bank(5)[0:CAP, :], xg_t[:, slot, k, :], w1_sb[slot][:, k, :], start=(k == 0), stop=(k == KD - 1))
                    mm = pe.matmul(bank(5)[CAP:P, :], xg_t[:, slot, k, :], w3_sb[slot][:, k, :], start=(k == 0),
                                   stop=(k == KD - 1))
                mm.then_inc(up_ps, 1)
                pe.wait_ge(up_ok, n + 1)
                for c in range(CW):
                    mm = turn(bank(6)[:, c * P:(c + 1) * P], up_sb[:, slot, c:DE:CW], P)
                mm.then_inc(upt_ps, 1)
                pe.wait_ge(w2_ld[slot], w2_loads)
                pe.wait_ge(actt_ok, n + 1)
                pe.wait_ge(y2_sb, n + 1)
                for c in range(CW):
                    pe.matmul(bank(7)[0:CAP, :], act_t[:, slot, c, :], w2_sb[slot][:, c, 0:DE], start=(c == 0),
                              stop=(c == CW - 1))
                    mm = pe.matmul(bank(7)[CAP:P, :], act_t[:, slot, c, :], w2_sb[slot][:, c, DE:D], start=(c == 0),
                                   stop=(c == CW - 1))
                mm.then_inc(y2_ps, 1)

            with pe.Fori(0, NE // 2) as i:
                for j in range(2):
                    expert(j, 2 * i + j, 32 * i + 32, 16 * i + 16, 16 * i + 16)
            pe.wait_ge(over_ok, 1)
            n_extra = pe.value_load(over_i[0:1, EXTRA:EXTRA + 1], min_val=0, max_val=EXTRA)
            with pe.If(n_extra > 0):
              with pe.Fori(0, EXTRA) as i:
                with pe.If(n_extra > i):
                    expert(0, NE + i, 16 * NE + 32 * i + 32, 8 * NE + 16 * i + 16, 8 * NE + 16 * i + 16)

        @block.scalar
        def _(act):
            steps_done = [0]

            def link(ins):
                steps_done[0] += 1
                ins.then_inc(act_step, 1)
                act.wait_ge(act_step, steps_done[0])

            act.wait_ge(ss_init, 1)
            act.activation(rs_mem[:, :], ss_mem[:, :], ACT.Sqrt).then_inc(act_step, 1)
            steps_done[0] += 1

            def root(i):
                t = START_TILES[i]
                n = rows(t)
                act.wait_ge(ms_ok, i + 1)
                act.activation(rs[0:n, t:t + 1], ss[0:n, t:t + 1], ACT.Sqrt).then_inc(sqrt_ok, 1)

            for i, t in enumerate(START_TILES):
                n = rows(t)
                act.wait_ge(x_ld[t], 16)
                if i >= 1:
                    act.wait_ge(sumsq_ok, i)
                act.activation(junk[0:n, :], x_in[0:n, t, :], ACT.Square, accum_out=ss[0:n, t:t + 1]).then_inc(sumsq_ok, 1)
                if i >= 1:
                    root(i - 1)
            root(NT - 1)

            act.sem_inc(pj_sb, 2)
            act.sem_inc(y2_sb, 1)
            for j in range(2):
                act.sem_inc(ydr_st[j], 32)

            def split(slot, loads):
                act.wait_ge(w_ld[slot], loads)
                act.activation(w_hi[:, slot, :, :], w_raw[:, slot, :, :], ACT.Copy).then_inc(split_hi, 1)

            def split_chunk(m):
                split(m % RING, 16 * (m // RING + 1))

            def copy_chunk(m, slot, place):
                act.wait_ge(w_used, m + 1)
                act.activation(halves(place), acc_pair(2 * (slot % 2)), ACT.Copy).then_inc(pj_sb, 1)

            split_chunk(0)
            act.wait_ge(xst_f, 1)
            act.activation(xn_hi[:, :, SEQ:TOK], xst_tmp[:, :, :], ACT.Copy).then_inc(xst_hi, 1)
            split_chunk(1)
            act.wait_ge(norm_ld, 16)
            for k in range(KD):
                act.wait_ge(xt_ps, k + 1)
                act.activation(xn_hi[:, k, 0:SEQ], bank(4 + k % 4), ACT.Copy, scale=norm1_t[:, k:k + 1]).then_inc(xt_hi, 1)
            split_chunk(2)
            split_chunk(3)
            for m in range(RING):
                copy_chunk(m, m, proj[:, FIRST + m, :])
                if m < 2:
                    act.wait_ge(mem_ld, 16)
                    if m == 1:
                        act.wait_ge(memsq_ok, 1)
                    else:
                        act.wait_ge(sumsq_ok, NT)
                    act.activation(junk[:, :], mem_in[:, m, :], ACT.Square, accum_out=ss_mem[:, m:m + 1]).then_inc(memsq_ok, 1)
                else:
                    if m == 2:
                        act.wait_ge(ms_ok, MS_MEM)
                        act.activation(rs_mem[:, :], ss_mem[:, :], ACT.Sqrt).then_inc(sqrt_ok, 1)
                    split_chunk(m + 2)
            with act.Fori(1, PART1 // RING) as i:
                for j in range(RING):
                    split((j + 2) % RING, 16 * i + (16 if j < 2 else 32))
                    copy_chunk(RING * i + j, j, proj[:, bass.ds(RING * i + j + FIRST, 1), :].rearrange("p o n -> p (o n)"))
            for m in range(PART1, IN_CHUNKS):
                split_chunk(m + 2)
                if m == 16:
                    act.wait_ge(pj_sb, RING + 2)
                    act.activation(qx_sq[:, :, :], proj[:, X0:X0 + XH, :], ACT.Square).then_inc(qxsq_ok, 1)
                    act.wait_ge(tp_ps, JOB_QSS + 1)
                if m == 18:
                    act.wait_ge(ms_ok, MS_QX)
                    act.activation(rs_qx[:, :], ss_qx[:, :], ACT.Sqrt).then_inc(sqrt_ok, 1)
                copy_chunk(m, m % RING, proj[:, m - PART1, :])
                if m == 24:
                    act.wait_ge(ms_ok, MS_MK)
                    act.activation(rs_mk[:, :], ss_mk[:, :], ACT.Sqrt).then_inc(sqrt_ok, 1)

            def sigmoid(n, pair):
                act.wait_ge(gt_ps, n + 1)
                act.wait_ge(mg_ok, n + 1)
                act.activation(halves(gate_sb[:, n % 2, :]), acc_pair(pair), ACT.Sigmoid).then_inc(gt_sb, 1)

            act.wait_ge(conv_ok, 1)
            for n in range(KD):
                if n == 5:
                    act.wait_ge(zm_mx, 1)
                    act.activation(pm[0:NB * XH, :].rearrange("p (j n) -> p j n", j=2), cols(5, ZM_AT, NM)[0:NB * XH].rearrange("p (j n) -> p j n", j=2),
                                   ACT.Exp, bias=pm_neg[0:NB * XH, :], accum_out=pm_sum[0:NB * XH, :]).then_inc(pm_exp, 1)
                split_chunk(IN_CHUNKS + n + 2)
                sigmoid(n, 0)
                u, h, part = n, n // 2, n % 2
                act.wait_ge(cs_mx, u + 1)
                if u >= 2:
                    act.wait_ge(ct_ps, u - 1)
                out = bank(6).rearrange("p (t m) -> p t m", t=2)
                for t in range(2):
                    col = (2 * part + t) * XH + h
                    act.activation(prob[:, u % 2, t, :], out[:, t, :], ACT.Exp, bias=xneg[:, u % 2, t:t + 1],
                                   scale=rs_qx[:, col:col + 1], accum_out=xsum[:, u % 2, t:t + 1]).then_inc(cs_exp, 1)
                if n % 2 == 0 and n >= 2:
                    act.wait_ge(cy_ps, n // 2)
                    act.activation(proj[:, B0 + n // 2 - 1, 0:SEQ], bank(7), ACT.Copy).then_inc(cy_sb, 1)
                act.wait_ge(ct_ps, u + 1)
                act.activation(prob_t[:, :, part * 2 * P:(part + 1) * 2 * P], bank(7).rearrange("p (t n) -> p t n", t=2),
                               ACT.Copy).then_inc(ct_sb, 1)
            act.wait_ge(cy_ps, XH)
            act.activation(proj[:, B0 + XH - 1, 0:SEQ], bank(7), ACT.Copy).then_inc(cy_sb, 1)

            def front(h):
                act.wait_ge(z_ps, h + 1)
                if h >= 2:
                    act.wait_ge(a_ok, h - 1)
                    act.wait_ge(s_ps, h - 1)
                else:
                    act.wait_ge(dot_ok, 2 * NB)
                act.activation(z_sb[:, h % 2, :], acc_all[:, 0:SCORE_N], ACT.Identity, bias=sbias_bc[:, h:h + 1],
                               scale=SB_SCALE)
                act.activation(sp_sb[:, h % 2, :], acc_all[:, 0:SCORE_N], ACT.Abs, bias=sbias_bc[:, h:h + 1],
                               scale=SB_SCALE).then_inc(z_read, 1)
                act.wait_ge(z_read, h + 1)
                link(act.activation(sp_sb[:, h % 2, :], sp_sb[:, h % 2, :], ACT.Exp, scale=-1.0))
                act.activation(sp_sb[:, h % 2, :], sp_sb[:, h % 2, :], ACT.Ln, bias=1.0).then_inc(ln_ok, 1)

            def weights(h):
                act.wait_ge(t_cut, 4 * (h + 1))
                if h >= 2:
                    act.wait_ge(y_ps, h - 1)
                act.activation(a_sb[:, h % 2, :], z_sb[:, h % 2, :], ACT.Exp).then_inc(a_ok, 1)

            def stick_out(h):
                r, c = HD * (h % 2), h // 2
                act.wait_ge(y_ps, h + 1)
                act.activation(proj[r:r + HD, C0 + c, 0:SEQ], bank(5)[r:r + HD, :], ACT.Copy).then_inc(y_sb, 1)

            act.wait_ge(small_ld, 16 * 6)
            front(0)
            act.wait_ge(zs_ok, 1)
            link(act.activation(z_abs[:, :, :, :], zs[:, :, :, :], ACT.Abs))
            link(act.activation(z_abs[:, :, :, :], z_abs[:, :, :, :], ACT.Exp, scale=-1.0))
            act.activation(z_abs[:, :, :, :], z_abs[:, :, :, :], ACT.Ln, bias=1.0).then_inc(zsln_ok, 1)
            for h in range(HEADS):
                n = KD + h
                split_chunk(IN_CHUNKS + n + 2)
                if h == 1:
                    act.wait_ge(ts_ok, 1)
                    act.activation(a_s[:, :, :, 0:HEADS].rearrange("p j b h -> p (j b) h"),
                                   zs[:, :, :, :].rearrange("p j b h -> p (j b) h"), ACT.Exp).then_inc(as_ok, 1)
                sigmoid(n, 6)
                if h + 1 < HEADS:
                    front(h + 1)
                weights(h)
                if h >= 1:
                    stick_out(h - 1)
            stick_out(HEADS - 1)

            with act.Fori(0, KD // RING) as i:
                for j in range(RING):
                    n = 2 * KD + RING * i + j
                    loads = 16 * (2 * KD // RING + 7) + 16 * i + (16 if j < 2 else 32)
                    if j < 2:
                        split((j + 2) % RING, loads)
                    else:
                        with act.If(i < 1):
                            split((j + 2) % RING, loads)
                    act.wait_ge(gt_ps, n + 1)
                    act.wait_ge(mg_ok, n + 1)
                    act.activation(halves(gate_sb[:, j % 2, :]), acc_pair(0), ACT.Sigmoid).then_inc(gt_sb, 1)

            for tt in range(NT):
                n = rows(tt)
                act.wait_ge(x1_ok, 2 * tt + 2)
                if tt >= 1:
                    act.wait_ge(ss2_ok, tt)
                act.activation(junk2[0:n, :], x1[0:n, tt, :], ACT.Square, accum_out=ss2[0:n, tt:tt + 1]).then_inc(ss2_ok, 1)
                act.wait_ge(ms2_ok, tt + 1)
                act.activation(rs2[0:n, tt:tt + 1], rs2[0:n, tt:tt + 1], ACT.Sqrt).then_inc(rt2_ok, 1)
                act.wait_ge(h_ok, tt + 1)
                act.dma_start(h_dram[tok(tt), :], h_tok[0:n, tt, :]).then_inc(h_st, 16)
                for q in range(2):
                    m = 2 * tt + q
                    act.wait_ge(ht_ps, m + 1)
                    act.activation(h_t[:, 4 * q:4 * q + 4, tok(tt)],
                                   bank(4 + m % 2)[:, 0:4 * n].rearrange("p (k n) -> p k n", k=4), ACT.Copy).then_inc(ht_sb, 1)
            act.wait_ge(lgt_ps, 1)
            act.activation(logits_t[0:NR, 0:SEQ], bank(6)[0:NR, :], ACT.Copy).then_inc(lgt_sb, 1)
            act.activation(logits_t[0:NR, SEQ:TOK], bank(7)[0:NR, 0:NB], ACT.Copy).then_inc(lgt_sb, 1)
            act.wait_ge(lg_max, 1)
            act.activation(g_exp[:, :, :], g_tmp[:, :, :], ACT.Exp).then_inc(lg_exp, 1)
            act.wait_ge(top_ok, 1)
            act.activation(top2[:, :], top1[:, :], ACT.Exp).then_inc(top_exp, 1)

            def block_act(slot, n, store, stored):
                act.wait_ge(upt_ps, n + 1)
                up = bank(6).rearrange("p (c t) -> p c t", c=CW)
                act.activation(gate_h[:, :, :], up[:, :, 0:CAP], ACT.Sigmoid).then_inc(sig_ok, 1)
                act.wait_ge(y2_ps, n + 1)
                act.wait_ge(ydr_st[slot], stored)
                act.activation(y_out[:, slot, :], bank(7), ACT.Copy).then_inc(y2_sb, 1)
                act.wait_ge(y2_sb, n + 2)
                for half in range(2):
                    act.dma_start(store[:, half * DE:(half + 1) * DE], y_out[half * CAP:(half + 1) * CAP, slot, :]
                                  ).then_inc(ydr_st[slot], 16)

            act.wait_ge(fill_st, 16 * (EXTRA * CAP // SEQ))
            with act.Fori(0, NE // 2) as i:
                for j in range(2):
                    block_act(j, 2 * i + j, y_dram[bass.ds((2 * i + j) * CAP, CAP), :], 32 * i + 32)
            act.wait_ge(over_ok, 1)
            n_extra = act.value_load(over_i[0:1, EXTRA:EXTRA + 1], min_val=0, max_val=EXTRA)
            with act.If(n_extra > 0):
              with act.Fori(0, EXTRA) as i:
                with act.If(n_extra > i):
                    block_act(0, NE + i, y_dram[bass.ds((NE + i) * CAP, CAP), :], 32 * (NE // 2 + 1) + 32 * i)

        @block.vector
        def _(dve):
            steps_done = [0]

            def link(ins):
                steps_done[0] += 1
                ins.then_inc(dve_step, 1)
                dve.wait_ge(dve_step, steps_done[0])

            dve.sem_inc(mg_ok, 2)
            dve.memset(ss_mem[:, :], 1.0).then_inc(ss_init, 1)

            def mean_square(i):
                t = START_TILES[i]
                n = rows(t)
                dve.wait_ge(sumsq_ok, i + 1)
                dve.tensor_scalar(ss[0:n, t:t + 1], ss[0:n, t:t + 1], 1.0 / D, EPS, ALU.mult, ALU.add).then_inc(ms_ok, 1)

            mean_square(0)
            for i, t in enumerate(START_TILES):
                n = rows(t)
                if i + 1 < NT:
                    mean_square(i + 1)
                dve.wait_ge(sqrt_ok, i + 1)
                link(dve.reciprocal(rs[0:n, t:t + 1], rs[0:n, t:t + 1]))
                dve.tensor_scalar(x_in[0:n, t, :], x_in[0:n, t, :], rs[0:n, t:t + 1], None, ALU.mult).then_inc(xn_ok, 1)

            def rest(slot, m):
                dve.wait_ge(split_hi, m + 1)
                dve.tensor_tensor(w_lo[:, slot, :, :], w_raw[:, slot, :, :], w_hi[:, slot, :, :].bitcast(F32),
                                  ALU.subtract).then_inc(split_lo, 1)

            def rest_chunk(m):
                rest(m % RING, m)

            dve.wait_ge(norm_ld, 16)
            dve.wait_ge(xst_ps, 1)
            dve.tensor_tensor(xst_tmp[:, :, :], cols(2, 384, KD * NB).rearrange("p (k b) -> p k b", k=KD),
                              norm1_t[:, :].unsqueeze(2).to_broadcast([P, KD, NB]), ALU.mult).then_inc(xst_f, 1)
            rest_chunk(0)
            dve.wait_ge(xst_hi, 1)
            dve.tensor_tensor(xn_lo[:, :, SEQ:TOK], xst_tmp[:, :, :], xn_hi[:, :, SEQ:TOK].bitcast(F32),
                              ALU.subtract).then_inc(xst_lo, 1)
            rest_chunk(1)
            for k in range(KD):
                dve.wait_ge(xt_hi, k + 1)
                dve.scalar_tensor_tensor(out=xn_lo[:, k, 0:SEQ], in0=bank(4 + k % 4), scalar=norm1_t[:, k:k + 1],
                                         in1=xn_hi[:, k, 0:SEQ].bitcast(F32), op0=ALU.mult, op1=ALU.subtract).then_inc(xt_lo, 1)
            rest_chunk(2)
            rest_chunk(3)
            dve.wait_ge(memsq_ok, 2)
            dve.tensor_scalar(ss_mem[:, :], ss_mem[:, :], 1.0 / D, EPS, ALU.mult, ALU.add).then_inc(ms_ok, 1)
            rest_chunk(4)
            dve.wait_ge(sqrt_ok, MS_MEM)
            link(dve.reciprocal(rs_mem[:, :], rs_mem[:, :]))
            rest_chunk(5)
            dve.wait_ge(page_ld, 16)
            dve.wait_ge(consts, 5)
            link(dve.tensor_copy(page_f[:, :], page_i[:, :]))
            link(dve.tensor_scalar(page_f[:, :], page_f[:, :], float(P), row_f[:, 0:1], ALU.mult, ALU.add))
            dve.tensor_copy(page_row[:, :], page_f[:, :]).then_inc(rows_ok, 1)
            with dve.Fori(1, PART1 // RING) as i:
                for j in range(RING):
                    rest((j + 2) % RING, RING * i + j + 2)
            for t in range(2):
                dve.tensor_scalar(mem_in[:, t, :], mem_in[:, t, :], rs_mem[:, t:t + 1], None, ALU.mult).then_inc(memn_ok, 1)

            def take(n, out, src):
                dve.wait_ge(tp_ps, n + 1)
                dve.tensor_copy(out, src).then_inc(tp_sb, 1)

            def job_out(n):
                return bank(4 + n % 4)

            full = (NT - 1) * XH
            heads = mk[:, :, :].rearrange("p t (h d) -> p (t h) d", d=XD)
            dve.wait_ge(xt_ps, KD)
            dve.memset(ss_qx[:, :], 1.0).then_inc(dve_step, 1)
            dve.memset(pm_t[:, :, :, :], 0.0).then_inc(dve_step, 1)
            steps_done[0] += 2
            dve.wait_ge(small_ld, 16 * 6)
            for m in range(PART1, IN_CHUNKS):
                rest_chunk(m + 2)
                if m == 16:
                    dve.wait_ge(tp_ps, JOB_QSS + 1)
                    dve.wait_ge(dve_step, steps_done[0])
                    out = job_out(JOB_QSS)
                    link(dve.tensor_scalar(ss_qx[:, 0:full], out[:, 0:full], 1.0 / XD, EPS, ALU.mult, ALU.add))
                    dve.tensor_scalar(ss_qx[0:NB, full:full + XH], out[0:NB, full:full + XH], 1.0 / XD, EPS, ALU.mult,
                                      ALU.add).then_inc(tp_sb, 1)
                    dve.wait_ge(tp_sb, JOB_QSS + 1)
                    dve.sem_inc(ms_ok, 1)
                elif m in (17, 18):
                    for q in (2 * (m - 17), 2 * (m - 17) + 1):
                        n = JOB_MT + q
                        dve.wait_ge(tp_ps, n + 1)
                        dve.tensor_tensor(mem_t[:, 2 * q:2 * q + 2, :], job_out(n).rearrange("p (k m) -> p k m", k=2),
                                          mnorm_t[:, 2 * q:2 * q + 2].unsqueeze(2).to_broadcast([P, 2, NM]), ALU.mult
                                          ).then_inc(tp_sb, 1)
                elif m == 19:
                    for tt in range(NT):
                        n = JOB_V + tt
                        take(n, v_tok[:, tt, :] if tt < NT - 1 else v_s[0:NB, :], job_out(n)[0:rows(tt), :])
                    dve.wait_ge(sqrt_ok, MS_QX)
                    link(dve.reciprocal(rs_qx[:, :], rs_qx[:, :]))
                    dve.tensor_scalar(rs_qx[:, :], rs_qx[:, :], X_SCALE, None, ALU.mult).then_inc(qxrs_ok, 1)
                    dve.wait_ge(qxrs_ok, 1)
                    take(JOB_STATE, state_t[:, :, :, :],
                         job_out(JOB_STATE)[:, 0:2 * CW * NB].rearrange("p (j c b) -> p j c b", j=2, c=CW))
                    dve.wait_ge(tp_sb, JOB_STATE + 1)
                elif m in (20, 21, 22, 23):
                    mt, half = divmod(m - 20, 2)
                    n = JOB_MP + m - 20
                    take(n, (mk, mv)[half][:, mt, :], job_out(n))
                    if m == 20:
                        dve.wait_ge(qxsq_ok, 1)
                        dve.tensor_scalar(proj[:, X0:X0 + XH, :], proj[:, X0:X0 + XH, :], qnorm_t[:, 0:1], None,
                                          ALU.mult).then_inc(qxn_ok, 1)
                    if m == 23:
                        dve.wait_ge(tp_sb, n + 1)
                        link(dve.tensor_tensor(mk_sq[:, :, :], mk[:, :, :], mk[:, :, :], ALU.mult))
                        link(dve.tensor_reduce(ss_mk[:, :], mk_sq[:, :, :].rearrange("p t (h d) -> p (t h) d", d=XD),
                                               AX.X, ALU.add))
                        dve.tensor_scalar(ss_mk[:, :], ss_mk[:, :], 1.0 / XD, EPS, ALU.mult, ALU.add).then_inc(ms_ok, 1)
                elif m == 24:
                    take(JOB_Q, q_s[0:NB, :], job_out(JOB_Q)[0:NB, :])
                    dve.wait_ge(tp_ps, JOB_QX + 1)
                    dve.tensor_tensor(qx_s[0:NB, :].rearrange("p (h d) -> p h d", h=XH),
                                      job_out(JOB_QX)[0:NB, :].rearrange("p (h d) -> p h d", h=XH),
                                      rs_qx[0:NB, full:full + XH].unsqueeze(2).to_broadcast([NB, XH, XD]), ALU.mult
                                      ).then_inc(tp_sb, 1)
                elif m == 25:
                    dve.wait_ge(sqrt_ok, MS_MK)
                    link(dve.reciprocal(rs_mk[:, :], rs_mk[:, :]))
                    link(dve.tensor_tensor(heads, heads, rs_mk[:, :].unsqueeze(2).to_broadcast([P, 2 * XH, XD]), ALU.mult))
                    dve.tensor_tensor(heads, heads, knorm_bc[:, :].unsqueeze(1).to_broadcast([P, 2 * XH, XD]),
                                      ALU.mult).then_inc(mk_ok, 1)
                if m in (25, 26):
                    for tt in (range(3) if m == 25 else range(3, NT)):
                        n = JOB_K + tt
                        if 2 <= tt < NT - 1:
                            dve.wait_ge(kout_st[tt % 2], 16)
                        take(n, k_out[:, tt % 2, :] if tt < NT - 1 else k_s[0:NB, :], job_out(n)[0:rows(tt), :])
                if 21 <= m < 21 + CW:
                    c = m - 21
                    dve.wait_ge(pj_sb, PART1 + C0 + c + 3)
                    dve.tensor_tensor(proj[:, C0 + c, :], proj[:, C0 + c, :], proj[:, U0 + c, :], ALU.mult).then_inc(u_ok, 1)
                    dve.wait_ge(u_ok, c + 1)
                    link(dve.tensor_scalar(proj[:, c, :], proj[:, C0 + c, :], conv_t[:, 2, c:c + 1], None, ALU.mult))
                    for back in (1, 2):
                        tap = conv_t[:, 2 - back, c:c + 1]
                        dve.scalar_tensor_tensor(out=proj[:, c, back:SEQ], in0=proj[:, C0 + c, 0:SEQ - back], scalar=tap,
                                                 in1=proj[:, c, back:SEQ], op0=ALU.mult, op1=ALU.add)
                        link(dve.scalar_tensor_tensor(out=proj[:, c, SEQ:TOK], in0=state_t[:, 2 - back, c, :],
                                                      scalar=tap, in1=proj[:, c, SEQ:TOK], op0=ALU.mult, op1=ALU.add))
                if m == 27:
                    take(JOB_U, conv_out[0:2 + NB, :], job_out(JOB_U)[0:2 + NB, :])
                    for q in range(2):
                        n = JOB_MK + q
                        take(n, mk_t[:, 2 * q:2 * q + 2, :], job_out(n).rearrange("p (h m) -> p h m", h=2))
                    dve.wait_ge(pj_sb, IN_CHUNKS + 2)
                    dve.tensor_tensor(proj[:, 0:CW, :], proj[:, 0:CW, :], proj[:, B0:B0 + CW, :], ALU.mult).then_inc(conv_ok, 1)

            def merge(n, place, part):
                dve.wait_ge(gt_sb, n + 1)
                dve.wait_ge(br_ps, n + 1)
                total, gate = halves(place), halves(gate_sb[:, n % 2, :])
                if n < KD:
                    dve.tensor_tensor(total, gate, part, ALU.mult).then_inc(mg_ok, 1)
                else:
                    dve.tensor_tensor(gate, gate, part, ALU.mult).then_inc(term_ok, 1)
                    dve.wait_ge(term_ok, n - KD + 1)
                    dve.tensor_tensor(total, total, gate, ALU.add).then_inc(mg_ok, 1)

            def dots(n):
                b = n % NB
                heads_n, dim = (XH, XD) if n < NB else (HEADS, HD)
                dve.wait_ge(bq_ps, n + 1)
                dve.wait_ge(key_ld[n % KEY_RING], 32 * (n // KEY_RING + 1))
                if n >= 1:
                    dve.wait_ge(dot_ok, n)
                else:
                    dve.wait_ge(mk_st, 16)
                dve.tensor_tensor(dot[:, :, :], keys[:, n % KEY_RING, :, :],
                                  bank(4).unsqueeze(1).to_broadcast([P, 2, W]), ALU.mult).then_inc(bq_used, 1)
                dve.wait_ge(bq_used, n + 1)
                out = zm[:, :, b, :] if n < NB else z_raw[:, :, b, :]
                dve.tensor_reduce(out, dot[:, :, :].rearrange("p j (h d) -> p j h d", d=dim), AX.X, ALU.add).then_inc(dot_ok, 1)

            def two_out(kind, b):
                dve.wait_ge(val_used, kind * NB + b + 2)
                if kind == 1:
                    dve.wait_ge(yt_ps, b // PER + 1)
                at = COLS * (b % PER)
                dve.tensor_copy(y_four[b // PER][at:at + 2 * COLS, :], bank(5)[at:at + 2 * COLS, :]).then_inc(yg_sb, 1)

            m32 = NB * XH
            for n in range(KD):
                u, h, part = n, n // 2, n % 2
                rest_chunk(IN_CHUNKS + n + 2)
                dve.wait_ge(cs_ps, u + 1)
                if u >= 2:
                    dve.wait_ge(cs_exp, 2 * (u - 1))
                link(dve.tensor_reduce(xmax[:, u % 2, :], bank(6).rearrange("p (t m) -> p t m", t=2), AX.X, ALU.max))
                col = 2 * part * XH + h
                dve.scalar_tensor_tensor(out=xneg[:, u % 2, :], in0=xmax[:, u % 2, :], scalar=-1.0,
                                         in1=rs_qx[:, col:col + XH + 1:XH], op0=ALU.mult, op1=ALU.mult).then_inc(cs_mx, 1)
                dots(2 * n)
                if n == 5:
                    dve.wait_ge(pm_exp, 1)
                    link(dve.reciprocal(pm_rec[0:m32, :], pm_sum[0:m32, :]))
                    dve.tensor_scalar(pm[0:m32, :], pm[0:m32, :], pm_rec[0:m32, :], None, ALU.mult).then_inc(pm_ok, 1)
                dve.wait_ge(cs_exp, 2 * (u + 1))
                link(dve.reciprocal(xrec[:, u % 2, :], xsum[:, u % 2, :]))
                dve.tensor_tensor(prob[:, u % 2, :, :], prob[:, u % 2, :, :],
                                  xrec[:, u % 2, :].unsqueeze(2).to_broadcast([P, 2, NM]), ALU.mult).then_inc(cs_nrm, 1)
                merge(n, merged[:, n, :], acc_pair(2))
                dots(2 * n + 1)
                if n == 4:
                    dve.wait_ge(zm_ps, 1)
                    link(dve.tensor_reduce(pm_max[0:m32, :], cols(5, ZM_AT, NM)[0:m32], AX.X, ALU.max))
                    dve.tensor_scalar(pm_neg[0:m32, :], pm_max[0:m32, :], -1.0, None, ALU.mult).then_inc(zm_mx, 1)
                if n == 5:
                    dve.wait_ge(pmt_ps, 1)
                    dve.tensor_copy(pm_t[:, :, :, 0:XH].rearrange("p t b h -> p (t b) h"),
                                    cols(5, PMT_AT, 2 * m32).rearrange("p (t h) -> p t h", h=XH)).then_inc(pmt_sb, 1)
                if n >= 6:
                    two_out(0, 4 * (n - 6))
                    two_out(0, 4 * (n - 6) + 2)
            for g in range(2):
                dve.wait_ge(yt_ps, g + 1)
                turned = bank(5 - g).rearrange("p (c s x) -> p c s x", c=CW, s=PER)
                for c in range(XH):
                    last = dve.tensor_copy(proj[:, B0 + c, SEQ + PER * g:SEQ + PER * (g + 1)], turned[:, c, :, c])
                last.then_inc(yt_sb, 1)
            dve.wait_ge(cs_ps, 2 * XH)
            link(dve.memset(a_s[:, :, :, :], 0.0))

            def softplus(h):
                dve.wait_ge(ln_ok, h + 1)
                dve.scalar_tensor_tensor(out=sp_sb[:, h % 2, :], in0=z_sb[:, h % 2, :], scalar=0.0, in1=sp_sb[:, h % 2, :],
                                         op0=ALU.max, op1=ALU.add).then_inc(sp_ok, 1)

            dve.wait_ge(dot_ok, 2 * NB)
            flat = "p j b h -> p (j b) h"
            dve.scalar_tensor_tensor(out=zs[:, :, :, :].rearrange(flat), in0=z_raw[:, :, :, :].rearrange(flat),
                                     scalar=SB_SCALE, in1=sbias_bc[:, :].unsqueeze(1).to_broadcast([P, 2 * NB, HEADS]),
                                     op0=ALU.mult, op1=ALU.add).then_inc(zs_ok, 1)
            softplus(0)
            dve.wait_ge(zsln_ok, 1)
            dve.scalar_tensor_tensor(out=z_sp[:, :, :, :], in0=zs[:, :, :, :], scalar=0.0, in1=z_abs[:, :, :, :],
                                     op0=ALU.max, op1=ALU.add).then_inc(zssp_ok, 1)
            for h in range(HEADS):
                n = KD + h
                rest_chunk(IN_CHUNKS + n + 2)
                dve.wait_ge(s_ps, h + 1)
                low, cut_at = SUM_AT[2], SCORE_AT[2]
                dve.tensor_tensor(z_sb[:, h % 2, 0:cut_at], z_sb[:, h % 2, 0:cut_at],
                                  acc_all[:, SUM_AT[0]:SUM_AT[0] + cut_at], ALU.subtract)
                dve.tensor_tensor(z_sb[:, h % 2, cut_at:SCORE_N], z_sb[:, h % 2, cut_at:SCORE_N],
                                  acc_all[:, low:low + SCORE_N - cut_at], ALU.subtract).then_inc(t_ok, 1)
                if 2 <= h < 6:
                    two_out(1, 2 * (h - 2))
                elif h >= 6:
                    g = h - 6
                    dve.wait_ge(yt_ps, 3 + g)
                    turned = bank(5).rearrange("p (c s x) -> p c s x", c=CW, s=PER)
                    for c in range(CW):
                        for r in range(2):
                            pr = slice(r * HD, (r + 1) * HD)
                            last = dve.tensor_copy(proj[pr, C0 + c, SEQ + PER * g:SEQ + PER * (g + 1)],
                                                   turned[pr, c, :, 2 * c + r])
                    last.then_inc(yt_sb, 1)
                merge(n, merged[:, h, :], acc_pair(6))
                if h + 1 < HEADS:
                    softplus(h + 1)
                if h == 0:
                    dve.wait_ge(ss_ps, 1)
                    per = NB * HEADS
                    zs_flat = zs[:, :, :, :].rearrange("p j b h -> p j (b h)")
                    dve.tensor_tensor(zs_flat, zs_flat, cols(5, SUMS_AT, 2 * per).rearrange("p (j n) -> p j n", j=2), ALU.subtract).then_inc(ts_ok, 1)

            with dve.Fori(0, KD // RING) as i:
                for j in range(RING):
                    n = 2 * KD + RING * i + j
                    if j < 2:
                        rest((j + 2) % RING, IN_CHUNKS + 2 + n)
                    else:
                        with dve.If(i < 1):
                            rest((j + 2) % RING, IN_CHUNKS + 2 + n)
                    dve.wait_ge(gt_sb, n + 1)
                    dve.wait_ge(br_ps, n + 1)
                    total = halves(merged[:, bass.ds(RING * i + j, 1), :].rearrange("p o n -> p (o n)"))
                    gate = halves(gate_sb[:, j % 2, :])
                    dve.tensor_tensor(gate, gate, acc_pair(2), ALU.mult).then_inc(term_ok, 1)
                    dve.wait_ge(term_ok, n - KD + 1)
                    dve.tensor_tensor(total, total, gate, ALU.add).then_inc(mg_ok, 1)

            dve.wait_ge(x1_ld, 32)
            dve.wait_ge(n2_ld, 16)
            for tt in range(NT):
                n = rows(tt)
                for half in range(2):
                    q = 2 * tt + half
                    dve.wait_ge(wo_ps, q + 1)
                    v = x1[0:n, tt, half * 512:(half + 1) * 512]
                    dve.tensor_tensor(v, v, bank(q % 4)[0:n, :], ALU.add).then_inc(x1_ok, 1)
                dve.wait_ge(ss2_ok, tt + 1)
                dve.tensor_scalar(rs2[0:n, tt:tt + 1], ss2[0:n, tt:tt + 1], 1.0 / D, EPS, ALU.mult, ALU.add).then_inc(ms2_ok, 1)
                dve.wait_ge(rt2_ok, tt + 1)
                link(dve.reciprocal(rs2[0:n, tt:tt + 1], rs2[0:n, tt:tt + 1]))
                dve.scalar_tensor_tensor(out=h_tok[0:n, tt, :], in0=x1[0:n, tt, :], scalar=rs2[0:n, tt:tt + 1],
                                         in1=norm2_bc[0:n, :], op0=ALU.mult, op1=ALU.mult).then_inc(h_ok, 1)

            def bc(v, shape):
                return v.to_broadcast(shape)

            link(dve.memset(logits[:, :, :], 0.0))
            link(dve.memset(picked[:, NT:NT + 1, :], 0.0))
            dve.wait_ge(lg_ps, 1)
            dve.wait_ge(pool_step, POOL_CONSTS)
            lg = bank(0)[:, 0:NT * NR].rearrange("p (t r) -> p t r", t=NT)
            link(dve.tensor_tensor(logits[:, 0:NT - 1, :], lg[:, 0:NT - 1, :], bc(rbias_bc[:, :].unsqueeze(1), [P, NT - 1, NR]), ALU.add))
            link(dve.tensor_tensor(logits[0:NB, NT - 1, :], lg[0:NB, NT - 1, :], rbias_bc[0:NB, :], ALU.add))
            link(dve.tensor_reduce(g_top[:, :], logits[:, :, 0:NG], AX.X, ALU.max))
            dve.tensor_tensor(g_tmp[:, :, :], logits[:, :, 0:NG], bc(g_top[:, :].unsqueeze(2), [P, NT, NG]),
                              ALU.subtract).then_inc(lg_max, 1)

            def first_best(one, values, best, tmp, n):
                link(dve.tensor_tensor(tmp, values, bc(best.unsqueeze(2), [P, NT, n]), ALU.is_equal))
                link(dve.tensor_tensor(tmp, tmp, bc(rev[:, EPG - n:EPG].unsqueeze(1), [P, NT, n]), ALU.mult))
                link(dve.tensor_reduce(best, tmp, AX.X, ALU.max))
                link(dve.tensor_tensor(one, tmp, bc(best.unsqueeze(2), [P, NT, n]), ALU.is_equal))

            dve.wait_ge(lg_exp, 1)
            link(dve.tensor_reduce(g_prob[:, :], g_exp[:, :, :], AX.X, ALU.add))
            link(dve.reciprocal(g_prob[:, :], g_prob[:, :]))
            first_best(g_one[:, :, :], logits[:, :, 0:NG], g_top[:, :], g_tmp[:, :, :], NG)
            link(dve.tensor_tensor(g_one[:, :, :], g_one[:, :, :], bc(valid[:, :].unsqueeze(2), [P, NT, NG]), ALU.mult))
            for tt in range(NT):
                last = dve.tensor_tensor(e_all[:, tt, :, :], logits[:, tt, NG:NR].rearrange("p (g x) -> p g x", g=NG),
                                         bc(g_one[:, tt, :].unsqueeze(2), [P, NG, EPG]), ALU.mult)
            link(last)
            link(dve.tensor_reduce(e_in[:, :, :], e_all[:, :, :, :].rearrange("p t g x -> p t x g"), AX.X, ALU.add))
            link(dve.tensor_reduce(top1[:, :], e_in[:, :, :], AX.X, ALU.max))
            link(dve.tensor_copy(gate1[:, :], top1[:, :]))
            first_best(one1[:, :, :], e_in[:, :, :], top1[:, :], e_tmp[:, :, :], EPG)
            link(dve.scalar_tensor_tensor(out=e_in[:, :, :], in0=one1[:, :, :], scalar=-1e30, in1=e_in[:, :, :],
                                          op0=ALU.mult, op1=ALU.add))
            link(dve.tensor_reduce(top2[:, :], e_in[:, :, :], AX.X, ALU.max))
            link(dve.tensor_tensor(top1[:, :], top2[:, :], gate1[:, :], ALU.subtract))
            first_best(one2[:, :, :], e_in[:, :, :], top2[:, :], e_tmp[:, :, :], EPG)
            dve.sem_inc(top_ok, 1)
            for pick, one in ((pick1, one1), (pick2, one2)):
                for tt in range(NT):
                    last = dve.tensor_tensor(pick[:, tt, :, :], bc(g_one[:, tt, :].unsqueeze(2), [P, NG, EPG]),
                                             bc(one[:, tt, :].unsqueeze(1), [P, NG, EPG]), ALU.mult)
            link(last)
            experts = "p t g x -> p t (g x)"
            dve.tensor_tensor(picked[:, 0:NT, :], pick1[:, :, :, :].rearrange(experts), pick2[:, :, :, :].rearrange(experts),
                              ALU.add).then_inc(pick_ok, 1)
            dve.wait_ge(top_exp, 1)
            link(dve.tensor_scalar(gate1[:, :], top2[:, :], 1.0, None, ALU.add))
            link(dve.reciprocal(gate1[:, :], gate1[:, :]))
            link(dve.tensor_tensor(gate1[:, :], gate1[:, :], g_prob[:, :], ALU.mult))
            link(dve.tensor_tensor(gate2[:, :], gate1[:, :], top2[:, :], ALU.mult))
            dve.wait_ge(rank_ps, 1)
            link(dve.tensor_copy(count[:, :], bank(1)[:, NT * NE:(NT + 1) * NE]))
            link(dve.tensor_tensor(over_part[:, :, :], bc(count[:, :].unsqueeze(2), [P, NE, TOK // CAP]),
                                   bc(limits[:, :].unsqueeze(1), [P, NE, TOK // CAP]), ALU.is_gt))
            link(dve.tensor_reduce(extra[:, :], over_part[:, :, :], AX.X, ALU.add))
            link(dve.tensor_tensor(low_part[:, :, :], low_tri[:, :, :], bc(extra[:, :].unsqueeze(1), [P, NE, NE]), ALU.mult))
            link(dve.tensor_reduce(over_slot[:, :], low_part[:, :, :], AX.X, ALU.add))
            link(dve.tensor_tensor(extra_end[:, :], over_slot[:, :], extra[:, :], ALU.add))
            link(dve.tensor_scalar(over_slot[:, :], over_slot[:, :], float(CAP), float((NE - 1) * CAP), ALU.mult, ALU.add))
            link(dve.tensor_tensor(over_slot[:, :], over_slot[:, :], first_slot[:, :], ALU.subtract))
            rank = bank(1)[:, 0:NT * NE].rearrange("p (t e) -> p t e", t=NT)
            link(dve.tensor_tensor(dest[:, :, :], rank, bc(first_slot[:, :].unsqueeze(1), [P, NT, NE]), ALU.add))
            link(dve.tensor_scalar(over[:, :, :], rank, float(CAP), None, ALU.is_ge))
            link(dve.tensor_tensor(over[:, :, :], over[:, :, :], bc(over_slot[:, :].unsqueeze(1), [P, NT, NE]), ALU.mult))
            link(dve.tensor_tensor(dest[:, :, :], dest[:, :, :], over[:, :, :], ALU.add))
            for pick, d in ((pick1, dest1), (pick2, dest2)):
                link(dve.tensor_tensor(over[:, :, :], dest[:, :, :], pick[:, :, :, :].rearrange(experts), ALU.mult))
                link(dve.tensor_reduce(d, over[:, :, :], AX.X, ALU.add))
            q_n = 2 * NT
            link(dve.tensor_tensor(from_block[:, :, :], bc(dests[:, :].unsqueeze(2), [P, q_n, BLOCKS + 1]),
                                   bc(block_at[:, :].unsqueeze(1), [P, q_n, BLOCKS + 1]), ALU.is_ge))
            link(dve.tensor_reduce(place_in[:, :], from_block[:, :, :], AX.X, ALU.add))
            link(dve.tensor_tensor(in_block[:, :, :], from_block[:, :, 0:BLOCKS], from_block[:, :, 1:BLOCKS + 1], ALU.subtract))
            for which in range(2):
                v = in_block[:, which * NT:(which + 1) * NT, :]
                last = dve.tensor_tensor(v, v, bc(tok_f[:, :].unsqueeze(2), [P, NT, BLOCKS]), ALU.mult)
            link(last)
            link(dve.scalar_tensor_tensor(out=place_in[:, :], in0=place_in[:, :], scalar=-float(CAP), in1=dests[:, :],
                                          op0=ALU.mult, op1=ALU.add))
            dve.tensor_tensor(at_pos[:, :, :], bc(place_in[:, :].unsqueeze(2), [P, q_n, CAP]),
                              bc(pos_at[:, :].unsqueeze(1), [P, q_n, CAP]), ALU.is_equal).then_inc(dest_ok, 1)
            link(dve.tensor_copy(dest1_i[:, :], dest1))
            link(dve.tensor_copy(dest2_i[:, :], dest2))
            link(dve.tensor_tensor(over_who[:, :, :], bc(steps[:, :].unsqueeze(2), [P, EXTRA, NE]),
                                   bc(extra_end[:, :].unsqueeze(1), [P, EXTRA, NE]), ALU.is_ge))
            link(dve.tensor_reduce(over_cnt[:, :], over_who[:, :, :], AX.X, ALU.add))
            link(dve.tensor_scalar(over_cnt[:, :], over_cnt[:, :], float(NE - 1), None, ALU.min))
            link(dve.tensor_copy(over_i[:, 0:EXTRA], over_cnt[:, :]))
            dve.tensor_copy(over_i[:, EXTRA:EXTRA + 1], extra_end[:, NE - 1:NE]).then_inc(over_ok, 1)
            dve.wait_ge(ids_ps, 1)
            dve.tensor_copy(slot_tok[0:CAP, :], bank(3)[0:CAP, 0:BLOCKS]).then_inc(ids_ok, 1)

            def block_dve(slot, n):
                dve.wait_ge(xgt_ps, n + 1)
                dve.tensor_copy(xg_t[:, slot, :, :], bank(4).rearrange("p (k t) -> p k t", k=KD)).then_inc(xgt_sb, 1)
                dve.wait_ge(up_ps, n + 1)
                dve.tensor_copy(up_sb[:, slot, :], bank(5)).then_inc(up_ok, 1)
                dve.wait_ge(sig_ok, n + 1)
                up = bank(6).rearrange("p (c t) -> p c t", c=CW)
                dve.tensor_tensor(gate_h[:, :, :], gate_h[:, :, :], up[:, :, 0:CAP], ALU.mult).then_inc(half_ok, 1)
                dve.wait_ge(half_ok, n + 1)
                dve.tensor_tensor(act_t[:, slot, :, :], gate_h[:, :, :], up[:, :, CAP:P], ALU.mult).then_inc(actt_ok, 1)

            with dve.Fori(0, NE // 2) as i:
                for j in range(2):
                    block_dve(j, 2 * i + j)
            dve.wait_ge(over_ok, 1)
            n_extra = dve.value_load(over_i[0:1, EXTRA:EXTRA + 1], min_val=0, max_val=EXTRA)
            with dve.If(n_extra > 0):
              with dve.Fori(0, EXTRA) as i:
                with dve.If(n_extra > i):
                    block_dve(0, NE + i)
            for tt in range(NT):
                n = rows(tt)
                dve.wait_ge(ys_ld[tt], 32)
                link(dve.scalar_tensor_tensor(out=x1[0:n, tt, :], in0=ya[0:n, tt, :], scalar=gate1[0:n, tt:tt + 1],
                                              in1=x1[0:n, tt, :], op0=ALU.mult, op1=ALU.add))
                dve.scalar_tensor_tensor(out=x1[0:n, tt, :], in0=yb[0:n, tt, :], scalar=gate2[0:n, tt:tt + 1],
                                         in1=x1[0:n, tt, :], op0=ALU.mult, op1=ALU.add).then_inc(y_done, 1)


INS = {
    "x_prompt": (1, SEQ, D), "x_sample": (NB, 1, D), "mem_prompt": (1, NM, D), "cache_k": None, "cache_v": None,
    "cache_mem_k": None, "cache_mem_v": None, "state_conv": None, "page_table": None, "norm1": None, "w_in": None,
    "conv_w": None, "sb_bias": None, "mem_norm": None, "w_mem_kv": None, "q_norm": None, "k_norm": None,
    "w_branch": None, "w_o": None, "norm2": None, "router_w": None, "router_b": None, "w1": None, "w3": None, "w2": None,
}
OUTS = (
    ("y_p", (1, SEQ, D)), ("y_s", (NB, 1, D)), ("k_p", (1, SEQ, HEADS, HD)), ("v_p", (1, SEQ, HEADS, HD)),
    ("conv_p", (1, CONV_K - 1, W)), ("mem_k", (1, NM, XH, XD)), ("mem_v", (1, NM, XH, XD)),
    ("k_s", (NB, 1, HEADS, HD)), ("v_s", (NB, 1, HEADS, HD)), ("conv_s", (NB, CONV_K - 1, W)),
)
FLAT = {
    "y_p": "b s d -> (b s) d", "y_s": "b s d -> (b s) d", "k_p": "b s h d -> (b s) (h d)", "v_p": "b s h d -> (b s) (h d)",
    "conv_p": "b j c -> (b j) c", "mem_k": "b m h d -> (b m) (h d)", "mem_v": "b m h d -> (b m) (h d)",
    "k_s": "b s h d -> (b s) (h d)", "v_s": "b s h d -> (b s) (h d)", "conv_s": "b j c -> b j c",
}


def kernel(**inputs):
    import numpy as np
    import concourse.bacc as bacc
    from concourse.bass_utils import run_bass_kernel_spmd

    U_IN, C_IN, B_IN, Q_IN, K_IN, V_IN, X_IN, GATE_IN = (CW * i for i in range(8))
    a = {name: np.asarray(v) for name, v in inputs.items()}
    a["norm1"] = a["norm1"].reshape(KD, P).T
    a["mem_norm"] = a["mem_norm"].reshape(KD, P).T
    a["q_norm"] = a["q_norm"].reshape(XD, 1)
    a["conv_w"] = a["conv_w"].reshape(CONV_K, CW, P).transpose(2, 0, 1)
    order = [X_IN, V_IN, K_IN, Q_IN, U_IN, C_IN, B_IN] + [GATE_IN + KD * g for g in BRANCH_ORDER]
    order = [c + i for c, n in zip(order, [CW] * 7 + [KD] * 3) for i in range(n)]
    a["w_in"] = a["w_in"].reshape(KD, P, CHUNKS, P).transpose(2, 1, 0, 3)[order]
    a["w_branch"] = a["w_branch"].reshape(3, CW, P, KD, P).transpose(0, 3, 2, 1, 4)[list(BRANCH_ORDER)].reshape(3 * KD, P, CW, P)
    a["router_w"] = np.concatenate([a["w_group"], a["w_router"]], axis=1).reshape(KD, P, NR).transpose(1, 0, 2)
    a["router_b"] = np.concatenate([a["b_group"], a["b_router"]])
    a["cache_k"] = a["cache_k"].reshape(-1, W)
    a["cache_v"] = a["cache_v"].reshape(-1, W)
    a["cache_mem_k"] = a["cache_mem_k"].reshape(NB, NM, W)
    a["cache_mem_v"] = a["cache_mem_v"].reshape(NB, NM, W)

    nc = bacc.Bacc("TRN2", target_bir_lowering=False, num_devices=1)
    arrays, io = {}, {}
    for name in INS:
        v = np.ascontiguousarray(a[name])
        arrays["in_" + name] = v
        io[name] = nc.dram_tensor("in_" + name, v.shape, mybir.dt.from_np(v.dtype), kind="ExternalInput").ap()
    for name, shape in OUTS:
        io[name] = nc.dram_tensor("out_" + name, shape, F32, kind="ExternalOutput").ap().rearrange(FLAT[name])
    build(nc, io)
    r = run_bass_kernel_spmd(nc, [arrays], core_ids=[0])
    return tuple(r.results[0]["out_" + name] for name, _ in OUTS)
```

```python
from contextlib import ExitStack

import concourse.bass as bass
from concourse import mybir

F32 = mybir.dt.float32
F32R = mybir.dt.float32r
I32 = mybir.dt.int32
ALU = mybir.AluOpType
ACT = mybir.ActivationFunctionType
AX = mybir.AxisListType

P = 128
D = 1024
SEQ = 512
NB = 8
TOK = SEQ + NB
NT = SEQ // P + 1
HALF_TOK = TOK // 2
KD = D // P
W = 512
CW = W // P
HEADS, HD = 8, 64
XH, XD = 4, 128
NM = 256
PAST = 256
PAGES = PAST // P
CONV_K = 3
NG, EPG = 4, 8
NE = NG * EPG
NR = NG + NE
DE = 512
EPS = 1e-6
SB_SCALE = HD ** -0.5
X_SCALE = XD ** -0.5

CHUNKS = 6656 // P
IN_CHUNKS = 28
RING = 4
U0, C0, B0, X0, V0, K0, Q0 = (CW * i for i in range(7))
PART1, FIRST = 4 * CW, 3 * CW
BRANCH_ORDER = (0, 2, 1)
YS_AT = (U0, B0, C0)
KEY_RING = 3
COLS = 32
WS, OUTS_KEPT = 3, 4
PER = P // COLS

CAP = 64
EXTRA = (2 * TOK) // CAP
BLOCKS = NE + EXTRA
SLOTS = BLOCKS * CAP

SCORE_AT = (0, 512, 1024, 896)
SCORE_N = 1280
SUM_AT = (1536, 2048, 1280, 2432)


def build(nc, io):
    ctx = ExitStack()
    with ctx:
        start = -(-nc.sbuf_base // 64) * 64
        at = {}
        for name, size in (("x", 20480), ("xn", 33280), ("ws", 32768), ("ys", 24960), ("qk", 33280),
                           ("t", 61824), ("misc", 6144)):
            at[name] = start
            start += size

        def place(name, region, offset, shape, dt=F32):
            return nc.alloc_sbuf_tensor_at(name, [P] + list(shape), dt, offset=at[region] + offset)

        used = [0]

        def misc(name, shape, dt=F32):
            n = 1
            for s in shape:
                n *= s
            t = place(name, "misc", used[0], shape, dt)
            used[0] += -(-4 * n // 32) * 32
            assert used[0] <= 6144, used
            return t

        def sem(name):
            return ctx.enter_context(nc.semaphore(name))

        ident = misc("ident", [P])
        ident_r = misc("ident_r", [NB], F32R)
        tri_from = misc("tri_from", [P])
        tri_before = misc("tri_before", [P])
        ones = misc("ones", [P])
        norm1_t = misc("norm1_t", [KD])
        mnorm_t = misc("mnorm_t", [KD])
        qnorm_t = misc("qnorm_t", [1])
        conv_t = misc("conv_t", [CONV_K, CW])
        sbias_bc = misc("sbias_bc", [HEADS])
        knorm_bc = misc("knorm_bc", [XD])
        rbias_bc = misc("rbias_bc", [NR])
        ss = misc("ss", [NT])
        rs = misc("rs", [NT])
        ss_mem = misc("ss_mem", [2])
        rs_mem = misc("rs_mem", [2])
        ss_mk = misc("ss_mk", [2 * XH])
        rs_mk = misc("rs_mk", [2 * XH])
        ss_qx = misc("ss_qx", [NT * XH])
        rs_qx = misc("rs_qx", [NT * XH])
        page_i = misc("page_i", [NB * PAGES], I32)
        page_f = misc("page_f", [NB * PAGES])
        row_f = misc("row_f", [1])
        page_row = misc("page_row", [NB * PAGES], I32)
        xst_tmp = misc("xst_tmp", [KD, NB])
        state_t = misc("state_t", [2, CW, NB])
        xmax = misc("xmax", [2, 2])
        xneg = misc("xneg", [2, 2])
        xsum = misc("xsum", [2, 2])
        xrec = misc("xrec", [2, 2])
        pm_max = misc("pm_max", [1])
        pm_neg = misc("pm_neg", [1])
        pm_sum = misc("pm_sum", [1])
        pm_rec = misc("pm_rec", [1])

        ss2 = misc("ss2", [NT])
        rs2 = misc("rs2", [NT])

        x_in = place("x_in", "x", 0, [NT, D])
        q_s = place("q_s", "x", 0, [W])
        qx_s = place("qx_s", "x", 2048, [W])
        q_lo = place("q_lo", "x", 0, [W], F32R)
        qx_lo = place("qx_lo", "x", 2048, [W], F32R)
        v_s = place("v_s", "x", 4096, [W])
        k_s = place("k_s", "x", 6144, [W])
        conv_out = place("conv_out", "x", 8192, [W])
        state = place("state", "x", 10240, [2 * W])
        zs = place("zs", "x", 14336, [2, NB, HEADS])
        z_abs = place("z_abs", "x", 14848, [2, NB, HEADS])
        z_sp = place("z_sp", "x", 15360, [2, NB, HEADS])
        z_raw = place("z_raw", "x", 15872, [2, NB, HEADS])
        zm = place("zm", "x", 16384, [2, NB, XH])
        pm = place("pm", "x", 16640, [NM])
        pm_t = place("pm_t", "x", 17664, [2, NB, COLS])
        y_four = [place("y_four0", "x", 12288, [W]), place("y_four1", "x", 2048, [W])]
        vals = place("vals", "x", 4096, [2, PAGES, W])
        x1 = place("x1", "x", 0, [NT, D])
        xn_hi = place("xn_hi", "xn", 0, [KD, TOK], F32R)
        xn_lo = place("xn_lo", "xn", 16640, [KD, TOK], F32R)
        w_raw = place("w_raw", "ws", 0, [RING, KD, P])
        w_lo = place("w_lo", "ws", 0, [RING, KD, P], F32R)
        w_hi = place("w_hi", "ws", 16384, [RING, KD, P], F32R)
        proj = place("proj", "ys", 0, [IN_CHUNKS, TOK])
        w_o = place("w_o_sb", "qk", 0, [KD, D])
        v_tok = place("v_tok", "t", 0, [NT - 1, W])
        mem_t = place("mem_t", "t", 8192, [KD, NM])
        mem_in = place("mem_in", "t", 16384, [2, D])
        junk = place("junk", "t", 24576, [D])
        w_mem = place("w_mem", "t", 29056, [KD, D])
        keys = place("keys", "t", 8192, [KEY_RING, PAGES, W])
        k_out = place("k_out", "t", 16384, [2, W])
        mk = place("mk", "t", 20480, [2, W])
        dot = place("dot", "t", 20480, [2, W])
        mv = place("mv", "t", 24576, [2, W])
        mk_t = place("mk_t", "t", 28672, [XH, NM])
        mk_sq = place("mk_sq", "t", 36992, [2, W])
        a_s = place("a_s", "t", 28672, [2, NB, COLS])
        z_sb = place("z_sb", "t", 8192, [2, SCORE_N])
        y_lo = place("y_lo", "ys", 0, [3 * CW, TOK], F32R)
        w_br_lo = place("w_br_lo", "t", 53632, [RING, CW, P], F32R)
        sp_sb = place("sp_sb", "t", 18432, [2, SCORE_N])
        gate_sb = place("gate_sb", "t", 32768, [2, TOK])
        merged = place("merged", "t", 36992, [KD, TOK])
        qx_hi = place("qx_hi", "t", 36992 + 4 * 4 * TOK, [W], F32R)
        q_hi = place("q_hi", "t", 36992 + 7 * 4 * TOK, [W], F32R)
        w_br = place("w_br", "t", 53632, [RING, CW, P])
        chunk = 4 * TOK
        y_hi_conv = [place(f"y_hi_conv{c}", region, at_chunk * chunk, [TOK], F32R) for c, (region, at_chunk) in enumerate(
            (("ys", C0 + 2), ("ys", C0 + 3), ("qk", V0 - FIRST + 2), ("qk", V0 - FIRST + 3)))]
        y_hi_x = place("y_hi_x", "ys", U0 * chunk, [CW, TOK], F32R)
        y_hi_sb = place("y_hi_sb", "ys", B0 * chunk, [CW, TOK], F32R)
        y_hi = (y_hi_conv, [y_hi_x[:, c, :] for c in range(CW)], [y_hi_sb[:, c, :] for c in range(CW)])
        w_br_hi = [place("w_br_hi_conv", "ys", (B0 + 3) * chunk, [CW, P], F32R),
                   place("w_br_hi_x", "t", 30720, [CW, P], F32R), place("w_br_hi_sb", "ys", U0 * chunk, [CW, P], F32R)]
        qx_sq = place("qx_sq", "ys", U0 * chunk, [XH, TOK])
        prob = place("prob", "ys", C0 * chunk, [2, 2, NM])
        prob_t = place("prob_t", "qk", (V0 - FIRST) * chunk, [2, SEQ])
        a_sb = place("a_sb", "qk", 0, [2, SCORE_N])

        w1_sb = [place("w1_a", "t", 0, [KD, DE]), place("w1_b", "ws", 16384, [KD, DE]), place("w1_c", "xn", 0, [KD, DE])]
        w3_sb = [place("w3_a", "t", 16384, [KD, DE]), place("w3_b", "qk", 0, [KD, DE]), place("w3_c", "ys", 0, [KD, DE])]
        w2_sb = [place("w2_a", "ws", 0, [CW, D]), place("w2_b", "qk", 16384, [CW, D]), place("w2_c", "xn", 16640, [CW, D])]
        h_tok = place("h_tok", "ys", 0, [NT, D])
        norm2_bc = place("norm2_bc", "ys", 20480, [D])
        h_t = place("h_t", "xn", 0, [KD, TOK])
        xg = [place(f"xg_{j}", "t", 44160 + 4096 * j, [D]) for j in range(WS)]
        xg_t = place("xg_t", "t", 56448, [2, KD, CAP])
        y_out = place("y_out", "ys", 16384, [OUTS_KEPT, DE])
        up_sb = place("up_sb", "t", 36992, [2, DE])
        gate_h = place("gate_h", "t", 41088, [CW, CAP])
        act_t = place("act_t", "t", 42112, [2, CW, CAP])
        scan = place("scan", "t", 44160, [2, NE // 2 + NE])
        w_r = place("w_r", "t", 53632, [KD, NR])
        route_at = [53632 + 1152]

        def route(name, shape, dt=F32):
            n = 1
            for v in shape:
                n *= v
            t = place(name, "t", route_at[0], shape, dt)
            route_at[0] += -(-4 * n // 32) * 32
            assert route_at[0] <= 61824
            return t

        junk2 = place("junk2", "xn", 24832, [D])
        logits = route("logits", [NT, NR])
        g_top = route("g_top", [NT])
        g_exp = route("g_exp", [NT, NG])
        g_prob = route("g_prob", [NT])
        g_one = route("g_one", [NT, NG])
        g_tmp = route("g_tmp", [NT, NG])
        e_all = route("e_all", [NT, NG, EPG])
        e_in = route("e_in", [NT, EPG])
        e_tmp = route("e_tmp", [NT, EPG])
        one1 = route("one1", [NT, EPG])
        one2 = route("one2", [NT, EPG])
        top1 = route("top1", [NT])
        top2 = route("top2", [NT])
        gate1 = misc("gate1", [NT])
        gate2 = misc("gate2", [NT])
        valid = route("valid", [NT])
        rev = route("rev", [EPG])
        limits = route("limits", [TOK // CAP])
        over_part = route("over_part", [NE, TOK // CAP])
        pick1 = route("pick1", [NT, NG, EPG])
        pick2 = route("pick2", [NT, NG, EPG])
        picked = route("picked", [NT + 1, NE])
        block_at = place("block_at", "t", 52352, [BLOCKS + 1])
        pos_at = place("pos_at", "t", 52576, [CAP])
        place_in = place("place_in", "t", 52832, [2 * NT])
        dest = route("dest", [NT, NE])
        over = route("over", [NT, NE])
        dests = place("dests", "t", 52896, [2 * NT])
        dest1, dest2 = dests[:, 0:NT], dests[:, NT:2 * NT]
        dest1_i = misc("dest1_i", [NT], I32)
        dest2_i = misc("dest2_i", [NT], I32)

        extra = misc("extra", [NE])
        extra_end = misc("extra_end", [NE])
        first_slot = misc("first_slot", [NE])
        over_slot = misc("over_slot", [NE])
        steps = misc("steps", [EXTRA])
        tok_f = misc("tok_f", [NT])
        over_who = place("over_who", "t", 32768, [EXTRA, NE])
        wo_part = place("wo_part", "t", 32768, [2, DE])
        tile_sum = misc("tile_sum", [NB])
        logits_t = place("logits_t", "t", 32768, [TOK])
        from_block = place("from_block", "t", 34880, [2 * NT, BLOCKS + 1])
        at_pos = place("at_pos", "t", 36992, [2 * NT, CAP])
        in_block = place("in_block", "t", 39552, [2 * NT, BLOCKS])
        over_cnt = misc("over_cnt", [EXTRA])
        over_i = misc("over_i", [EXTRA + 1], I32)

        slot_tok = misc("slot_tok", [BLOCKS], I32)
        slot_now = misc("slot_now", [WS], I32)
        ya = place("ya", "t", 0, [NT, D])
        yb = place("yb", "t", 20480, [NT, D])
        h_dram = nc.dram_tensor("h_dram", [TOK, D], F32, kind="Internal").ap()
        y_dram = nc.dram_tensor("y_dram", [SLOTS, D], F32, kind="Internal").ap()

        acc_all = ctx.enter_context(nc.psum_tensor("acc_all", [P, 8 * 512], F32))

        def bank(b, n=1):
            return acc_all[:, b * 512:(b + n) * 512]

        def acc_pair(b):
            return bank(b, 2).rearrange("p (a n) -> p a n", a=2)[:, :, 0:HALF_TOK]

        def halves(tile):
            return tile.rearrange("p (a n) -> p a n", a=2)

        def rows(tt):
            return P if tt < NT - 1 else NB

        def tok(tt):
            return slice(tt * P, tt * P + rows(tt))

        consts = sem("consts")
        norm_ld, small_ld, mem_ld, proj_ld, page_ld = (sem(n) for n in (
            "norm_ld", "small_ld", "mem_ld", "proj_ld", "page_ld"))
        x_ld = [sem(f"x_ld{t}") for t in range(NT)]
        dve_step, act_step, pool_step = sem("dve_step"), sem("act_step"), sem("pool_step")
        sumsq_ok, ms_ok, sqrt_ok, xn_ok = (sem(n) for n in ("sumsq_ok", "ms_ok", "sqrt_ok", "xn_ok"))
        MS_MEM, MS_QX, MS_MK, MS_H = NT + 1, NT + 2, NT + 3, NT + 4
        xt_ps, xt_hi, xt_lo, xst_ps, xst_f = (sem(n) for n in ("xt_ps", "xt_hi", "xt_lo", "xst_ps", "xst_f"))
        w_ld = [sem(f"w_ld{j}") for j in range(RING)]
        split_hi, split_lo, w_used, pj_sb = (sem(n) for n in ("split_hi", "split_lo", "w_used", "pj_sb"))
        tp_ps, tp_sb = sem("tp_ps"), sem("tp_sb")
        u_ok, qxsq_ok, qxn_ok = (sem(n) for n in ("u_ok", "qxsq_ok", "qxn_ok"))
        mk_ok = sem("mk_ok")
        kout_st, mid_st, out_st = [sem("kout_st0"), sem("kout_st1")], sem("mid_st"), sem("out_st")
        rows_ok, key_ld = sem("rows_ok"), [sem(f"key_ld{j}") for j in range(KEY_RING)]
        val_ld, mval_ld, val_used = [sem("val_ld0"), sem("val_ld1")], [sem("mval_ld0"), sem("mval_ld1")], sem("val_used")
        bq_ps, bq_used, dot_ok = sem("bq_ps"), sem("bq_used"), sem("dot_ok")
        cs_ps, cs_mx, cs_exp, cs_nrm, ct_ps, ct_sb, cy_ps, cy_sb = (sem(n) for n in (
            "cs_ps", "cs_mx", "cs_exp", "cs_nrm", "ct_ps", "ct_sb", "cy_ps", "cy_sb"))
        z_ps, z_read, ln_ok, sp_ok, sp_cut, s_ps, t_ok, t_cut, a_ok, y_ps, y_sb = (sem(n) for n in (
            "z_ps", "z_read", "ln_ok", "sp_ok", "sp_cut", "s_ps", "t_ok", "t_cut", "a_ok", "y_ps", "y_sb"))
        zs_ok, zsln_ok, zssp_ok, ss_ps, ts_ok, as_ok = (sem(n) for n in (
            "zs_ok", "zsln_ok", "zssp_ok", "ss_ps", "ts_ok", "as_ok"))
        zm_ps, zm_mx, pm_exp, pm_ok, pmt_ps, pmt_sb = (sem(n) for n in (
            "zm_ps", "zm_mx", "pm_exp", "pm_ok", "pmt_ps", "pmt_sb"))
        yg_sb, yt_ps, yt_sb = (sem(n) for n in ("yg_sb", "yt_ps", "yt_sb"))
        br_ld = [sem(f"br_ld{j}") for j in range(RING)]
        wb_hi, wb_lo = sem("wb_hi"), sem("wb_lo")
        gt_ps, gt_sb, br_ps, term_ok, mg_ok = (sem(n) for n in ("gt_ps", "gt_sb", "br_ps", "term_ok", "mg_ok"))
        GATES, MID_STORES = 3 * KD, 16 * (11 + EXTRA * CAP // SEQ)
        POOL_CONSTS = 3 + 9 + 1
        carried_pe, carried_pool = sem("carried_pe"), sem("carried_pool")
        wo_ld, x1_ld, route_ld, wo_ps, x1_ok = (sem(n) for n in ("wo_ld", "x1_ld", "route_ld", "wo_ps", "x1_ok"))
        part_ps, part_sb = sem("part_ps"), sem("part_sb")
        h_ok, ht_ps, ht_sb, h_st = (sem(n) for n in ("h_ok", "ht_ps", "ht_sb", "h_st"))
        lgt_ps, lgt_sb, lg_ps, lg_max, lg_exp, pick_ok, rank_ps, dest_ok, ids_ps, ids_ok, over_ok = (
            sem(n) for n in ("lgt_ps", "lgt_sb", "lg_ps", "lg_max", "lg_exp", "pick_ok", "rank_ps",
                             "dest_ok", "ids_ps", "ids_ok", "over_ok"))
        w13_ld = [[sem(f"w13_ld{j}{part}") for part in "ab"] for j in range(WS)]
        w2_ld = [sem(f"w2_ld{j}") for j in range(WS)]
        now_ok, xgt_ps, xgt_sb, up_ps, up_ok, upt_ps, sig_ok, half_ok, actt_ok, y2_ps, y2_sb = (sem(n) for n in (
            "now_ok", "xgt_ps", "xgt_sb", "up_ps", "up_ok", "upt_ps", "sig_ok", "half_ok", "actt_ok", "y2_ps", "y2_sb"))
        xg_ld = [sem(f"xg_ld{j}") for j in range(WS)]
        ydr_st, ys_ld, y_done = [sem(f"ydr_st{j}") for j in range(OUTS_KEPT)], [sem(f"ys_ld{t}") for t in range(NT)], sem("y_done")

        (JOB_QSS, JOB_MT, JOB_V, JOB_STATE, JOB_MP, JOB_Q, JOB_QX, JOB_K, JOB_U, JOB_MK, JOBS) = (
            0, 1, 5, 10, 11, 15, 16, 17, 22, 23, 25)

        START_TILES = (NT - 1, 0, 1, 2, 3)

        def cols(b, first, n):
            return acc_all[:, b * 512 + first:b * 512 + first + n]

        MERGE_TILES = (0, NT - 1, 1, 2, 3)

        ZM_AT, PMT_AT, SUMS_AT = 0, 256, 0

        def cut(pool, h, tile, ready, fill, done):
            pool.wait_ge(ready, h + 1)
            for kb in range(4):
                v = tile[:, h % 2, SCORE_AT[kb]:SCORE_AT[kb] + P]
                pool.affine_select(out=v, in_=v, compare_op=ALU.is_gt, fill=fill, base=0,
                                   pattern=[[1, P]], channel_multiplier=-1).then_inc(done, 1)

        block = ctx.enter_context(nc.Block())

        @block.sync
        def _(sp):
            for t in START_TILES:
                if t == NT - 1:
                    sp.dma_start(x_in[0:NB, t, :], io["x_sample"].rearrange("b s d -> (b s) d")).then_inc(x_ld[t], 16)
                else:
                    sp.dma_start(x_in[:, t, :], io["x_prompt"].rearrange("b s d -> (b s) d")[tok(t), :]).then_inc(x_ld[t], 16)
            sp.dma_start(norm1_t[:, :], io["norm1"]).then_inc(norm_ld, 16)
            for j in range(2):
                sp.dma_start(w_raw[:, j, :, :], io["w_in"][j]).then_inc(w_ld[j], 16)
            for tile, name in ((mnorm_t, "mem_norm"), (qnorm_t, "q_norm")):
                sp.dma_start(tile[:, :], io[name]).then_inc(small_ld, 16)
            for j in range(2, RING):
                sp.dma_start(w_raw[:, j, :, :], io["w_in"][j]).then_inc(w_ld[j], 16)
            sp.dma_start(mem_in[:, :, :], io["mem_prompt"].rearrange("b (t p) d -> p (b t) d", p=P)).then_inc(mem_ld, 16)
            sp.dma_start(conv_t[:, :, :], io["conv_w"]).then_inc(small_ld, 16)
            sp.dma_start(sbias_bc[:, :], io["sb_bias"].partition_broadcast(P)).then_inc(small_ld, 16)
            sp.dma_start(knorm_bc[:, :], io["k_norm"].partition_broadcast(P)).then_inc(small_ld, 16)
            sp.dma_start(rbias_bc[:, :], io["router_b"].partition_broadcast(P)).then_inc(small_ld, 16)

            def load_chunk(m):
                sp.wait_ge(w_used, m - RING + 1)
                sp.dma_start(w_raw[:, m % RING, :, :], io["w_in"][m]).then_inc(w_ld[m % RING], 16)

            load_chunk(RING)
            load_chunk(RING + 1)
            sp.dma_start(w_mem[:, :, :], io["w_mem_kv"].rearrange("(k p) n -> p k n", p=P)).then_inc(proj_ld, 16)
            load_chunk(RING + 2)
            load_chunk(RING + 3)
            with sp.Fori(1, PART1 // RING) as i:
                for j in range(RING):
                    sp.wait_ge(w_used, RING * i + j + 1)
                    sp.dma_start(w_raw[:, j, :, :], io["w_in"][RING * i + RING + j]).then_inc(w_ld[j], 16)
            sp.dma_start(state[0:NB, :], io["state_conv"].rearrange("b j c -> b (j c)")).then_inc(proj_ld, 16)
            for part in range(EXTRA * CAP // SEQ):
                at_row = NE * CAP + part * SEQ
                sp.dma_start(y_dram[at_row:at_row + SEQ, :], io["x_prompt"].rearrange("b s d -> (b s) d")).then_inc(mid_st, 16)

            def load_branch(n):
                sp.dma_start(w_br[:, n % RING, :, :], io["w_branch"][n]).then_inc(br_ld[n % RING], 16)

            def store_keys(tt):
                sp.wait_ge(tp_sb, JOB_K + tt + 1)
                if tt < NT - 1:
                    sp.dma_start(io["k_p"][tok(tt), :], k_out[:, tt % 2, :]).then_inc(kout_st[tt % 2], 16)
                else:
                    sp.dma_start(io["k_s"], k_s[0:NB, :]).then_inc(mid_st, 16)

            for m in range(PART1, IN_CHUNKS):
                if m == 26:
                    store_keys(0)
                    store_keys(1)
                elif m == 27:
                    for tt in range(2, NT):
                        store_keys(tt)
                load_chunk(m + RING)
                if m == 20:
                    sp.wait_ge(tp_sb, JOB_V + NT)
                    for tt in range(NT - 1):
                        sp.dma_start(io["v_p"][tok(tt), :], v_tok[:, tt, :]).then_inc(mid_st, 16)
                    sp.dma_start(io["v_s"], v_s[0:NB, :]).then_inc(mid_st, 16)
                if m == 24:
                    sp.wait_ge(tp_sb, JOB_MP + 4)
                    sp.dma_start(io["mem_v"].rearrange("(t p) c -> p t c", p=P), mv[:, :, :]).then_inc(mid_st, 16)
                    for n in range(RING):
                        load_branch(n)
                if m == 25:
                    sp.wait_ge(mk_ok, 1)
                    sp.dma_start(io["mem_k"].rearrange("(t p) c -> p t c", p=P), mk[:, :, :]).then_inc(mid_st, 16)
                    sp.dma_start(io["conv_s"][:, 0, :], state[0:NB, W:2 * W]).then_inc(mid_st, 16)
            sp.wait_ge(tp_sb, JOB_U + 1)
            sp.dma_start(io["conv_p"], conv_out[0:2, :]).then_inc(mid_st, 16)
            sp.dma_start(io["conv_s"][:, 1, :], conv_out[2:2 + NB, :]).then_inc(mid_st, 16)
            w1_d = io["w1"].rearrange("e (p k) n -> e p k n", p=P)
            w3_d = io["w3"].rearrange("e (p k) n -> e p k n", p=P)
            w2_d = io["w2"].rearrange("e (p c) n -> e p c n", p=P)
            with sp.Fori(0, 2 * KD // RING) as i:
                for j in range(RING):
                    sp.wait_ge(mg_ok, RING * i + j + 3)
                    sp.dma_start(w_raw[:, j, :, :], io["w_in"][IN_CHUNKS + RING * i + RING + j]).then_inc(w_ld[j], 16)
                    sp.dma_start(w_br[:, j, :, :], io["w_branch"][RING * i + RING + j]).then_inc(br_ld[j], 16)
            sp.wait_ge(y_sb, HEADS // 2)
            sp.wait_ge(yt_sb, 4)
            sp.dma_start(w_o[:, :, :], io["w_o"].rearrange("(k p) n -> p k n", p=P)).then_inc(wo_ld, 16)
            sp.dma_start(x1[:, 0:NT - 1, :], io["x_prompt"].rearrange("b (t p) d -> p (b t) d", p=P)).then_inc(x1_ld, 16)
            sp.dma_start(x1[0:NB, NT - 1, :], io["x_sample"].rearrange("b s d -> (b s) d")).then_inc(x1_ld, 16)
            for j in range(RING):
                n = 2 * KD + j
                sp.wait_ge(mg_ok, n + 3)
                sp.dma_start(w_raw[:, j, :, :], io["w_in"][IN_CHUNKS + RING + n]).then_inc(w_ld[j], 16)
                load_branch(n + RING)

            def load_up(e, j, *which, before=None):
                for part in range(2):
                    if before is not None:
                        sp.wait_ge(up_ps, 2 * before + part - 1)
                    ks = slice(part * KD // 2, (part + 1) * KD // 2)
                    for tiles, dram in (which,) if which else ((w1_sb, w1_d), (w3_sb, w3_d)):
                        sp.dma_start(tiles[j][:, ks, :], dram[e][:, ks, :]).then_inc(w13_ld[j][part], 16)

            sp.wait_ge(mid_st, MID_STORES)
            load_up(0, 0)
            sp.wait_ge(mg_ok, GATES + 2)
            sp.dma_start(norm2_bc[:, :], io["norm2"].partition_broadcast(P)).then_inc(route_ld, 16)
            sp.dma_start(w_r[:, :, :], io["router_w"]).then_inc(route_ld, 16)
            sp.dma_start(w2_sb[0][:, :, :], w2_d[0]).then_inc(w2_ld[0], 16)
            load_up(1, 1, w1_sb, w1_d)
            sp.wait_ge(wo_ps, 2 * NT)
            load_up(1, 1, w3_sb, w3_d)
            sp.dma_start(w2_sb[1][:, :, :], w2_d[1]).then_inc(w2_ld[1], 16)
            sp.wait_ge(lgt_ps, 1)
            load_up(2, 2, w1_sb, w1_d)
            sp.wait_ge(h_st, 16 * NT)
            load_up(2, 2, w3_sb, w3_d)
            sp.dma_start(w2_sb[2][:, :, :], w2_d[2]).then_inc(w2_ld[2], 16)

            def load_expert(e, j, before):
                load_up(e, j, before=before)
                sp.wait_ge(y2_ps, before)
                sp.dma_start(w2_sb[j][:, :, :], w2_d[e]).then_inc(w2_ld[j], 16)

            with sp.Fori(0, NE // WS - 1) as i:
                for j in range(WS):
                    load_expert(WS * i + WS + j, j, WS * i + j + 1)
            for e in range(NE // WS * WS, NE):
                load_expert(e, e % WS, e - WS + 1)
            sp.wait_ge(over_ok, 1)
            n_extra = sp.value_load(over_i[0:1, EXTRA:EXTRA + 1], min_val=0, max_val=EXTRA)
            with sp.If(n_extra > 0):
                with sp.Fori(0, EXTRA) as i:
                    with sp.If(n_extra > i):
                        e = sp.value_load(over_i[0:1, bass.ds(i, 1)], min_val=0, max_val=NE - 1)
                        sp.wait_ge(y2_ps, NE + i)
                        load_up(e, 0)
                        sp.dma_start(w2_sb[0][:, :, :], w2_d[e]).then_inc(w2_ld[0], 16)
            sp.wait_ge(mid_st, MID_STORES)
            for i, tt in enumerate(START_TILES):
                sp.wait_ge(y_done, i + 1)
                if tt < NT - 1:
                    sp.dma_start(io["y_p"][tok(tt), :], x1[:, tt, :]).then_inc(out_st, 16)
                else:
                    sp.dma_start(io["y_s"], x1[0:NB, tt, :]).then_inc(out_st, 16)
            sp.wait_ge(out_st, 16 * NT)
            for j in range(2):
                sp.wait_ge(kout_st[j], 32)

        @block.gpsimd
        def _(pool):
            steps_done = [0]

            def link(ins):
                steps_done[0] += 1
                ins.then_inc(pool_step, 1)
                pool.wait_ge(pool_step, steps_done[0])

            pool.memset(ident[:, :], 0.0).then_inc(pool_step, 1)
            pool.memset(tri_from[:, :], 1.0).then_inc(pool_step, 1)
            pool.memset(tri_before[:, :], 1.0).then_inc(pool_step, 1)
            steps_done[0] += 3
            pool.wait_ge(pool_step, 3)
            pool.affine_select(out=ident[:, :], in_=ident[:, :], compare_op=ALU.not_equal, fill=1.0, base=0,
                               pattern=[[-1, P]], channel_multiplier=1).then_inc(consts, 1)
            pool.affine_select(out=tri_from[:, :], in_=tri_from[:, :], compare_op=ALU.is_ge, fill=0.0, base=0,
                               pattern=[[-1, P]], channel_multiplier=1).then_inc(consts, 1)
            pool.affine_select(out=tri_before[:, :], in_=tri_before[:, :], compare_op=ALU.is_gt, fill=0.0, base=0,
                               pattern=[[1, P]], channel_multiplier=-1).then_inc(consts, 1)
            pool.memset(ones[:, :], 1.0).then_inc(consts, 1)
            pool.dma_start(page_i[:, :], io["page_table"].rearrange("b j -> (b j)").partition_broadcast(P)).then_inc(page_ld, 16)
            pool.iota(row_f[:, :], pattern=[[0, 1]], base=0, channel_multiplier=1,
                      allow_small_or_imprecise_dtypes=True).then_inc(consts, 1)
            pool.wait_ge(rows_ok, 1)

            def load_key(n):
                slot, b = n % KEY_RING, n % NB
                if n < NB:
                    pool.dma_start(keys[:, slot, :, :], io["cache_mem_k"][b].rearrange("(t p) c -> p t c", p=P)
                                   ).then_inc(key_ld[slot], 32)
                else:
                    for j in range(PAGES):
                        pool.indirect_dma_start(
                            out=keys[:, slot, j, :], out_offset=None, in_=io["cache_k"],
                            in_offset=bass.IndirectOffsetOnAxis(ap=page_row[:, b * PAGES + j:b * PAGES + j + 1], axis=0),
                        ).then_inc(key_ld[slot], 16)

            def load_val(b):
                slot = b % 2
                pool.wait_ge(val_used, NB + b - 1)
                for j in range(PAGES):
                    pool.indirect_dma_start(
                        out=vals[:, slot, j, :], out_offset=None, in_=io["cache_v"],
                        in_offset=bass.IndirectOffsetOnAxis(ap=page_row[:, b * PAGES + j:b * PAGES + j + 1], axis=0),
                    ).then_inc(val_ld[slot], 16)

            pool.wait_ge(tp_sb, JOB_MP + 4)
            load_key(0)
            load_key(1)
            for j in range(2):
                pool.wait_ge(kout_st[j], 32)
            load_key(2)

            for n in range(KEY_RING, 2 * NB):
                pool.wait_ge(bq_used, n - KEY_RING + 1)
                load_key(n)
            for h in range(HEADS):
                if h == 0:
                    cut(pool, 0, sp_sb, sp_ok, 0.0, sp_cut)
                if h + 1 < HEADS:
                    cut(pool, h + 1, sp_sb, sp_ok, 0.0, sp_cut)
                cut(pool, h, z_sb, t_ok, -1e30, t_cut)
                if h < 2:
                    load_val(h)
                elif h < 5:
                    load_val(2 * h - 2)
                    load_val(2 * h - 1)
            pool.wait_ge(wo_ps, 2 * NT)
            pool.iota(tok_f[:, :], pattern=[[P, NT]], base=0, channel_multiplier=1,
                      allow_small_or_imprecise_dtypes=True).then_inc(pool_step, 1)
            pool.iota(steps[:, :], pattern=[[1, EXTRA]], base=0, channel_multiplier=0,
                      allow_small_or_imprecise_dtypes=True).then_inc(pool_step, 1)
            pool.iota(first_slot[:, :], pattern=[[CAP, NE]], base=0, channel_multiplier=0,
                      allow_small_or_imprecise_dtypes=True).then_inc(pool_step, 1)
            pool.iota(rev[:, :], pattern=[[-1, EPG]], base=EPG, channel_multiplier=0,
                      allow_small_or_imprecise_dtypes=True).then_inc(pool_step, 1)
            pool.iota(limits[:, :], pattern=[[CAP, TOK // CAP]], base=CAP, channel_multiplier=0,
                      allow_small_or_imprecise_dtypes=True).then_inc(pool_step, 1)
            pool.iota(block_at[:, :], pattern=[[CAP, BLOCKS + 1]], base=0, channel_multiplier=0,
                      allow_small_or_imprecise_dtypes=True).then_inc(pool_step, 1)
            pool.iota(pos_at[:, :], pattern=[[1, CAP]], base=-CAP, channel_multiplier=0,
                      allow_small_or_imprecise_dtypes=True).then_inc(pool_step, 1)
            pool.memset(scan[:, :, :], 0.0).then_inc(pool_step, 1)
            pool.memset(valid[:, :], 1.0).then_inc(pool_step, 1)
            steps_done[0] += 9
            pool.wait_ge(pool_step, steps_done[0])

            link(pool.affine_select(out=valid[:, NT - 1:NT], in_=valid[:, NT - 1:NT], compare_op=ALU.is_gt, fill=0.0,
                                    base=NB, pattern=[[0, 1]], channel_multiplier=-1))
            pool.wait_ge(ids_ok, 1)
            pool.wait_ge(h_st, 16 * NT)

            def gather(slot, block):
                pool.tensor_copy(slot_now[0:CAP, slot:slot + 1], slot_tok[0:CAP, bass.ds(block, 1)]).then_inc(now_ok, 1)
                pool.wait_ge(now_ok, block + 1)
                pool.sem_inc(carried_pool, 1)
                pool.indirect_dma_start(
                    out=xg[slot][0:CAP, :], out_offset=None, in_=h_dram,
                    in_offset=bass.IndirectOffsetOnAxis(ap=slot_now[0:CAP, slot:slot + 1], axis=0)).then_inc(xg_ld[slot], 16)

            for j in range(WS):
                gather(j, j)
            with pool.Fori(0, NE // WS - 1) as i:
                for j in range(WS):
                    pool.wait_ge(xgt_ps, WS * i + j + 1)
                    gather(j, WS * i + j + WS)
            for n in range(NE // WS * WS, NE):
                pool.wait_ge(xgt_ps, n - WS + 1)
                gather(n % WS, n)
            pool.wait_ge(over_ok, 1)
            n_extra = pool.value_load(over_i[0:1, EXTRA:EXTRA + 1], min_val=0, max_val=EXTRA)
            for j in range(OUTS_KEPT):
                pool.wait_ge(ydr_st[j], 32 * (NE // OUTS_KEPT + 1))
            with pool.If(n_extra > 0):
                with pool.Fori(0, EXTRA) as i:
                    with pool.If(n_extra > i):
                        pool.wait_ge(xgt_ps, NE + i)
                        gather(0, NE + i)
                        pool.wait_ge(ydr_st[0], 32 * (NE // OUTS_KEPT + 2) + 32 * i)
            for tt, which in ((tt, which) for tt in START_TILES for which in range(2)):
                buf, d = ((ya, dest1_i), (yb, dest2_i))[which]
                pool.indirect_dma_start(
                    out=buf[0:rows(tt), tt, :], out_offset=None, in_=y_dram,
                    in_offset=bass.IndirectOffsetOnAxis(ap=d[0:rows(tt), tt:tt + 1], axis=0)).then_inc(ys_ld[tt], 16)

        @block.tensor
        def _(pe):
            def turn(out, in_, k):
                return pe.transpose(out, in_, ident[0:k, 0:k])

            pe.wait_ge(consts, 5)
            pe.wait_ge(xn_ok, 1)
            for k in range(KD):
                mm = turn(cols(2, 384 + k * NB, NB), x_in[0:NB, NT - 1, k * P:(k + 1) * P], NB)
            mm.then_inc(xst_ps, 1)

            for tt in range(NT - 1):
                pe.wait_ge(xn_ok, tt + 2)
                for k in range(4):
                    mm = turn(bank(4 + k)[:, tok(tt)], x_in[:, tt, k * P:(k + 1) * P], P)
                    if tt == NT - 2:
                        mm.then_inc(xt_ps, 1)

            def three_products(slot, k, out):
                for w, x, first, last in ((w_hi, xn_hi, k == 0, False), (w_hi, xn_lo, False, False),
                                          (w_lo, xn_hi, False, k == KD - 1)):
                    for a in range(2):
                        mm = pe.matmul(out[:, a, :], w[:, slot, k, :], x[:, k, a * HALF_TOK:(a + 1) * HALF_TOK],
                                       start=first, stop=last)
                return mm

            def three_pass(slot, out):
                for k in range(KD):
                    mm = three_products(slot, k, out)
                return mm

            pe.wait_ge(split_lo, 1)
            pe.wait_ge(xt_lo, 1)
            for k in range(KD):
                pe.wait_ge(xt_lo, k + 2)
                if k + 4 < KD:
                    for tt in range(NT - 1):
                        mm = turn(bank(4 + k)[:, tok(tt)], x_in[:, tt, (k + 4) * P:(k + 5) * P], P)
                    mm.then_inc(xt_ps, 1)
                three_products(0, k, acc_pair(0))
                pe.wait_ge(split_lo, 2)
                mm = three_products(1, k, acc_pair(2))
            mm.then_inc(w_used, 2)

            def project(m, slot):
                pe.wait_ge(split_lo, m + 1)
                pe.wait_ge(pj_sb, m + 1)
                three_pass(slot, acc_pair(2 * (slot % 2))).then_inc(w_used, 1)

            project(2, 2)
            project(3, 3)
            with pe.Fori(1, PART1 // RING) as i:
                for j in range(RING):
                    project(RING * i + j, j)

            def job_bank(n):
                if n >= 4:
                    pe.wait_ge(tp_sb, n - 3)
                return bank(4 + n % 4)

            def turn_tokens(n, first, tt):
                out = job_bank(n)
                for c in range(CW):
                    mm = turn(out[0:rows(tt), c * P:(c + 1) * P], proj[:, first + c, tok(tt)], P)
                mm.then_inc(tp_ps, 1)

            def turn_memory(q):
                out = job_bank(JOB_MT + q)
                for kk in range(2):
                    for mt in range(2):
                        mm = turn(out[:, kk * NM + mt * P:kk * NM + (mt + 1) * P],
                                  mem_in[:, mt, (2 * q + kk) * P:(2 * q + kk + 1) * P], P)
                mm.then_inc(tp_ps, 1)

            def project_memory(q):
                mt, half = divmod(q, 2)
                out = job_bank(JOB_MP + q)
                for k in range(KD):
                    mm = pe.matmul(out, mem_t[:, k, mt * P:(mt + 1) * P], w_mem[:, k, half * W:(half + 1) * W],
                                   start=(k == 0), stop=(k == KD - 1))
                mm.then_inc(tp_ps, 1)

            for m in range(PART1, IN_CHUNKS):
                project(m, m % RING)
                if m == 16:
                    pe.wait_ge(qxsq_ok, 1)
                    out = job_bank(JOB_QSS)
                    for tt in range(NT):
                        for h in range(XH):
                            mm = pe.matmul(out[0:rows(tt), tt * XH + h:tt * XH + h + 1], qx_sq[:, h, tok(tt)],
                                           ones[:, 0:1], start=True, stop=True)
                    mm.then_inc(tp_ps, 1)
                    pe.wait_ge(xn_ok, NT + 2)
                elif m in (17, 18):
                    turn_memory(2 * (m - 17))
                    turn_memory(2 * (m - 17) + 1)
                elif m == 19:
                    for tt in range(NT):
                        turn_tokens(JOB_V + tt, V0, tt)
                    pe.wait_ge(proj_ld, 32)
                    out = job_bank(JOB_STATE)
                    for q in range(2 * CW):
                        mm = turn(out[:, q * NB:(q + 1) * NB], state[0:NB, q * P:(q + 1) * P], NB)
                    mm.then_inc(tp_ps, 1)
                elif m in (20, 21, 22, 23):
                    pe.wait_ge(proj_ld, 32)
                    if m == 20:
                        pe.wait_ge(tp_sb, JOB_MT + 4)
                    project_memory(m - 20)
                elif m == 24:
                    turn_tokens(JOB_Q, Q0, NT - 1)
                    pe.wait_ge(qxn_ok, 1)
                    turn_tokens(JOB_QX, X0, NT - 1)
                elif m == 25:
                    for tt in range(3):
                        turn_tokens(JOB_K + tt, K0, tt)
                elif m == 26:
                    for tt in range(3, NT):
                        turn_tokens(JOB_K + tt, K0, tt)
                elif m == 27:
                    pe.wait_ge(u_ok, CW)
                    out = job_bank(JOB_U)
                    for c in range(CW):
                        mm = turn(out[0:2 + NB, c * P:(c + 1) * P], proj[:, C0 + c, SEQ - 2:TOK], P)
                    mm.then_inc(tp_ps, 1)
                    pe.wait_ge(mk_ok, 1)
                    for q in range(2):
                        out = job_bank(JOB_MK + q)
                        for hh in range(2):
                            for mt in range(2):
                                mm = turn(out[:, hh * NM + mt * P:hh * NM + (mt + 1) * P],
                                          mk[:, mt, (2 * q + hh) * XD:(2 * q + hh + 1) * XD], P)
                        mm.then_inc(tp_ps, 1)

            def branch(slot, group, out):
                first = YS_AT[group]
                for c in range(CW):
                    hi, lo = y_hi[group][c], y_lo[:, first + c, :]
                    for w, x, begin, end in ((w_br_hi[group][:, c, :], hi, c == 0, False),
                                             (w_br_hi[group][:, c, :], lo, False, False),
                                             (w_br_lo[:, slot, c, :], hi, False, c == CW - 1)):
                        for a in range(2):
                            mm = pe.matmul(out[:, a, :], w, x[:, a * HALF_TOK:(a + 1) * HALF_TOK], start=begin, stop=end)
                return mm

            def broadcast_query(n):
                if n >= 1:
                    pe.wait_ge(bq_used, n)
                b = n % NB
                hi, lo = (qx_hi, qx_lo) if n < NB else (q_hi, q_lo)
                row = ident_r[0:NB, b:b + 1].to_broadcast([NB, P])
                pe.matmul(bank(4), row, hi[0:NB, :], start=True, stop=False)
                pe.matmul(bank(4), row, lo[0:NB, :], start=False, stop=True).then_inc(bq_ps, 1)

            def cross_scores(u):
                h, part = divmod(u, 2)
                if u >= 1:
                    pe.wait_ge(cs_exp, 2 * u)
                out = bank(6).rearrange("p (t m) -> p t m", t=2)
                for t in range(2):
                    mm = pe.matmul(out[:, t, :], proj[:, X0 + h, tok(2 * part + t)], mk_t[:, h, :], start=True, stop=True)
                mm.then_inc(cs_ps, 1)

            def turn_probs(u):
                h, part = divmod(u, 2)
                pe.wait_ge(cs_nrm, u + 1)
                if u >= 1:
                    pe.wait_ge(ct_sb, u)
                if h >= 1:
                    pe.wait_ge(cy_sb, h)
                for mt in range(2):
                    for t in range(2):
                        mm = turn(bank(7)[:, (2 * mt + t) * P:(2 * mt + t + 1) * P], prob[:, u % 2, t, mt * P:(mt + 1) * P], P)
                mm.then_inc(ct_ps, 1)

            def cross_values(h):
                pe.wait_ge(ct_sb, 2 * h + 2)
                for mt in range(2):
                    mm = pe.matmul(bank(7), mv[:, mt, h * XD:(h + 1) * XD], prob_t[:, mt, :], start=(mt == 0), stop=(mt == 1))
                mm.then_inc(cy_ps, 1)

            def two_values(kind, b, weight):
                for slot in range(2):
                    pe.wait_ge((mval_ld if kind == 0 else val_ld)[slot], (16 if kind == 0 else 32) * (b // 2 + 1))
                for j in range(2):
                    for s in (b, b + 1):
                        at = COLS * (s % PER)
                        mm = pe.matmul(bank(5)[at:at + COLS, :], weight[:, j, s, :], vals[:, s % 2, j, :], start=(j == 0),
                                       stop=(j == 1))
                mm.then_inc(val_used, 2)

            def turn_four(kind, g, b):
                pe.wait_ge(yg_sb, 4 * kind + 2 * g + 2)
                for c in range(CW):
                    mm = turn(bank(b)[:, c * P:(c + 1) * P], y_four[g][:, c * P:(c + 1) * P], P)
                mm.then_inc(yt_ps, 1)

            def point(p):
                if p % 2 == 0 and p >= 2:
                    turn_probs(p // 2 - 1)
                broadcast_query(p)
                if p % 2 == 0:
                    cross_scores(p // 2)
                if p % 4 == 1 and p >= 5:
                    cross_values((p - 5) // 4)
                if p == 8:
                    pe.wait_ge(dot_ok, NB)
                    for mt in range(2):
                        mm = turn(cols(5, ZM_AT + mt * P, P)[0:NB * XH, :], zm[:, mt, :, :].rearrange("p b h -> p (b h)"), P)
                    mm.then_inc(zm_ps, 1)
                if p == 10:
                    pe.wait_ge(pm_ok, 1)
                    for mt in range(2):
                        mm = turn(cols(5, PMT_AT + mt * NB * XH, NB * XH), pm[0:NB * XH, mt * P:(mt + 1) * P], NB * XH)
                    mm.then_inc(pmt_ps, 1)
                if 11 <= p < 15:
                    pe.wait_ge(pmt_sb, 1)
                    if p >= 13:
                        pe.wait_ge(yg_sb, p - 12)
                    two_values(0, 2 * (p - 11), pm_t)

            pe.wait_ge(tp_sb, JOBS)
            for n in range(KD):
                pe.wait_ge(split_lo, IN_CHUNKS + n + 1)
                if n == 0:
                    pe.wait_ge(pj_sb, IN_CHUNKS + 2)
                else:
                    pe.wait_ge(gt_sb, n)
                three_pass(n % RING, acc_pair(0)).then_inc(gt_ps, 1)
                point(2 * n)
                pe.wait_ge(wb_lo, n + 1)
                pe.wait_ge(xt_lo, KD + 2)
                pe.wait_ge(mg_ok, n + 2)
                branch(n % RING, 0, acc_pair(2)).then_inc(br_ps, 1)
                point(2 * n + 1)

            def scores(h):
                r, c = HD * (h % 2), h // 2
                if h >= 1:
                    pe.wait_ge(z_read, h)
                for kb in range(4):
                    mm = pe.matmul(acc_all[:, SCORE_AT[kb]:SCORE_AT[kb] + SEQ - kb * P],
                                   proj[r:r + HD, K0 + c, kb * P:(kb + 1) * P], proj[r:r + HD, Q0 + c, kb * P:SEQ],
                                   start=True, stop=True, skip_group_check=True)
                mm.then_inc(z_ps, 1)

            def suffix_sums(h):
                pe.wait_ge(sp_cut, 4 * (h + 1))
                if h >= 1:
                    pe.wait_ge(t_ok, h)
                for kb in (0, 1, 3, 2):
                    if kb == 2 and h + 1 < HEADS:
                        pe.wait_ge(z_read, h + 2)
                    mm = pe.matmul(acc_all[:, SUM_AT[kb]:SUM_AT[kb] + SEQ - kb * P], tri_from[:, :],
                                   sp_sb[:, h % 2, SCORE_AT[kb]:SCORE_AT[kb] + SEQ - kb * P], start=True, stop=(kb == 3),
                                   skip_group_check=True)
                    for later in range(kb + 1, 4):
                        off = (later - kb) * P
                        mm = pe.matmul(acc_all[:, SUM_AT[kb] + off:SUM_AT[kb] + SEQ - kb * P], ones[:, :],
                                       sp_sb[:, h % 2, SCORE_AT[later]:SCORE_AT[later] + SEQ - later * P],
                                       start=False, stop=(later == 3), skip_group_check=True)
                mm.then_inc(s_ps, 1)

            def values(pair):
                pe.wait_ge(a_ok, 2 * pair + 2)
                if pair == 0:
                    pe.wait_ge(ts_ok, 1)
                else:
                    pe.wait_ge(y_sb, pair)
                    if pair < HEADS // 2 - 1:
                        pe.wait_ge(yg_sb, 4 + 2 * pair)
                    else:
                        pe.wait_ge(yt_sb, 4)
                for kb in range(4):
                    for r in range(2):
                        h = 2 * pair + r
                        mm = pe.matmul(bank(5)[r * HD:(r + 1) * HD, kb * P:SEQ], v_tok[:, kb, h * HD:(h + 1) * HD],
                                       a_sb[:, r, SCORE_AT[kb]:SCORE_AT[kb] + SEQ - kb * P],
                                       start=(kb == 0), stop=(kb == 3), skip_group_check=True)
                mm.then_inc(y_ps, 1)

            pe.wait_ge(mg_ok, KD + 2)
            pe.wait_ge(gt_sb, KD)
            scores(0)
            turn_probs(2 * XH - 1)
            cross_values(XH - 1)
            pe.wait_ge(yg_sb, 4)
            turn_four(0, 0, 5)
            pe.wait_ge(bq_used, 2 * NB)
            turn_four(0, 1, 4)
            pe.wait_ge(yt_sb, 2)
            for h in range(HEADS):
                n = KD + h
                pe.wait_ge(split_lo, IN_CHUNKS + n + 1)
                if h == 0:
                    pe.wait_ge(cs_exp, 4 * XH)
                    pe.wait_ge(cy_sb, XH)
                    pe.wait_ge(bq_used, 2 * NB)
                else:
                    pe.wait_ge(term_ok, h)
                three_pass(n % RING, acc_pair(6)).then_inc(gt_ps, 1)
                if h >= 2 and h % 2 == 0:
                    values(h // 2 - 1)
                if h + 1 < HEADS:
                    scores(h + 1)
                suffix_sums(h)
                if h >= 2:
                    pe.wait_ge(y_sb, h // 2)
                    if h < 6:
                        pe.wait_ge(as_ok, 1)
                        two_values(1, 2 * (h - 2), a_s)
                    else:
                        turn_four(1, h - 6, 5)
                pe.wait_ge(wb_lo, n + 1)
                pe.wait_ge(xt_lo, KD + 3)
                pe.wait_ge(gt_sb, n + 1)
                branch(n % RING, 1, acc_pair(6)).then_inc(br_ps, 1)
                if h == 0:
                    pe.wait_ge(zssp_ok, 1)
                    per = NB * HEADS
                    pe.matmul(cols(5, SUMS_AT, per), tri_from[:, :], z_sp[:, 0, :, :], start=True, stop=False,
                              skip_group_check=True)
                    pe.matmul(cols(5, SUMS_AT, per), ones[:, :], z_sp[:, 1, :, :], start=False, stop=True,
                              skip_group_check=True)
                    pe.matmul(cols(5, SUMS_AT + per, per), tri_from[:, :], z_sp[:, 1, :, :], start=True, stop=True,
                              skip_group_check=True).then_inc(ss_ps, 1)
            values(HEADS // 2 - 1)

            pe.wait_ge(z_read, HEADS)
            pe.wait_ge(t_ok, HEADS)
            pe.wait_ge(y_sb, HEADS // 2)
            pe.wait_ge(yt_sb, 4)
            with pe.Fori(0, KD // RING) as i:
                for j in range(RING):
                    n = 2 * KD + RING * i + j
                    pe.wait_ge(split_lo, IN_CHUNKS + n + 1)
                    pe.wait_ge(gt_sb, n)
                    three_pass(j, acc_pair(0)).then_inc(gt_ps, 1)
                    pe.wait_ge(wb_lo, n + 1)
                    pe.wait_ge(xt_lo, KD + 4)
                    pe.wait_ge(term_ok, n - KD)
                    branch(j, 2, acc_pair(2)).then_inc(br_ps, 1)
            pe.wait_ge(wo_ld, 16)
            def merge_parts():
                for half in range(2):
                    for round_ in range(KD // PER):
                        for s in range(PER):
                            k = PER * round_ + s
                            mm = pe.matmul(bank(4 + half)[COLS * s:COLS * (s + 1), :], merged[:, k, TOK - COLS:TOK],
                                           w_o[:, k, half * 512:(half + 1) * 512], start=(round_ == 0),
                                           stop=(round_ == KD // PER - 1))
                mm.then_inc(part_ps, 1)

            def merge_out(n):
                i, half = divmod(n, 2)
                tt = MERGE_TILES[i]
                if n >= 4:
                    pe.wait_ge(x1_ok, n - 3)
                if tt == NT - 1:
                    pe.wait_ge(part_sb, 1)
                    mm = pe.matmul(bank(n % 4)[0:NB, :], tile_sum[:, :], wo_part[:, half, :], start=True, stop=True)
                else:
                    for k in range(KD):
                        mm = pe.matmul(bank(n % 4), merged[:, k, tok(tt)], w_o[:, k, half * 512:(half + 1) * 512],
                                       start=(k == 0), stop=(k == KD - 1))
                mm.then_inc(wo_ps, 1)

            def turn_h(i):
                tt = MERGE_TILES[i]
                pe.wait_ge(h_ok, i + 1)
                for q in range(2):
                    n = 2 * i + q
                    if n >= 2:
                        pe.wait_ge(ht_sb, n - 1)
                    for kk in range(4):
                        k = 4 * q + kk
                        mm = turn(bank(4 + n % 2)[:, kk * rows(tt):(kk + 1) * rows(tt)],
                                  h_tok[0:rows(tt), tt, k * P:(k + 1) * P], rows(tt))
                    mm.then_inc(ht_ps, 1)

            def route_h(i):
                tt = MERGE_TILES[i]
                pe.wait_ge(ht_sb, 2 * i + 2)
                out = bank(6)[0:NR, tok(tt)] if tt < NT - 1 else bank(7)[0:NR, 0:NB]
                for k in range(KD):
                    mm = pe.matmul(out, w_r[:, k, :], h_t[:, k, tok(tt)], start=(k == 0), stop=(k == KD - 1))
                return mm

            pe.wait_ge(mg_ok, GATES + 2)
            merge_parts()
            for i in range(NT):
                merge_out(2 * i)
                merge_out(2 * i + 1)
                if i == 0:
                    pe.wait_ge(route_ld, 32)
                if i == 2:
                    turn_h(0)
                if i >= 2:
                    turn_h(i - 1)
                if i == 3:
                    route_h(0)
                if i >= 3:
                    route_h(i - 2)
            route_h(NT - 2)
            turn_h(NT - 1)
            route_h(NT - 1).then_inc(lgt_ps, 1)
            pe.wait_ge(lgt_sb, 2)
            pe.wait_ge(x1_ok, 2 * NT)
            for tt in range(NT):
                mm = turn(bank(0)[0:rows(tt), tt * NR:(tt + 1) * NR], logits_t[0:NR, tok(tt)], NR)
            mm.then_inc(lg_ps, 1)
            pe.wait_ge(pick_ok, 1)
            o = bank(1)[:, 0:(NT + 1) * NE]
            pe.matmul(o, tri_before[:, :], picked[:, :, :], start=True, stop=False, skip_group_check=True)
            for back in range(1, NT + 1):
                mm = pe.matmul(o[:, back * NE:], ones[:, :], picked[:, 0:NT + 1 - back, :], start=False, stop=(back == NT),
                               skip_group_check=True)
            mm.then_inc(rank_ps, 1)
            pe.wait_ge(dest_ok, 1)
            for q in range(2 * NT):
                n = rows(q % NT)
                mm = pe.matmul(bank(3)[0:CAP, 0:BLOCKS], at_pos[0:n, q, :], in_block[0:n, q, :], start=(q == 0),
                               stop=(q == 2 * NT - 1))
            mm.then_inc(ids_ps, 1)

            def expert(w, slot, n, loads):
                pe.wait_ge(xg_ld[w], 16 * loads)
                pe.sem_inc(carried_pe, 1)
                for k in range(KD):
                    mm = turn(bank(4)[:, k * CAP:(k + 1) * CAP], xg[w][0:CAP, k:D:KD], CAP)
                mm.then_inc(xgt_ps, 1)
                pe.wait_ge(w13_ld[w][0], 32 * loads)
                pe.wait_ge(xgt_sb, n + 1)
                for k in range(KD):
                    if k == KD // 2:
                        pe.wait_ge(w13_ld[w][1], 32 * loads)
                    pe.matmul(bank(5)[0:CAP, :], xg_t[:, slot, k, :], w1_sb[w][:, k, :], start=(k == 0), stop=(k == KD - 1))
                    mm = pe.matmul(bank(5)[CAP:P, :], xg_t[:, slot, k, :], w3_sb[w][:, k, :], start=(k == 0),
                                   stop=(k == KD - 1))
                    if k in (KD // 2 - 1, KD - 1):
                        mm.then_inc(up_ps, 1)
                pe.wait_ge(up_ok, n + 1)
                for c in range(CW):
                    mm = turn(bank(6)[:, c * P:(c + 1) * P], up_sb[:, slot, c:DE:CW], P)
                mm.then_inc(upt_ps, 1)
                pe.wait_ge(w2_ld[w], 16 * loads)
                pe.wait_ge(actt_ok, n + 1)
                pe.wait_ge(y2_sb, n + 1)
                for c in range(CW):
                    pe.matmul(bank(7)[0:CAP, :], act_t[:, slot, c, :], w2_sb[w][:, c, 0:DE], start=(c == 0),
                              stop=(c == CW - 1))
                    mm = pe.matmul(bank(7)[CAP:P, :], act_t[:, slot, c, :], w2_sb[w][:, c, DE:D], start=(c == 0),
                                   stop=(c == CW - 1))
                mm.then_inc(y2_ps, 1)

            both = 2 * WS
            with pe.Fori(0, NE // both) as i:
                for j in range(both):
                    expert(j % WS, j % 2, both * i + j, 2 * i + j // WS + 1)
            for e in range(NE // both * both, NE):
                expert(e % WS, e % 2, e, e // WS + 1)
            pe.wait_ge(over_ok, 1)
            n_extra = pe.value_load(over_i[0:1, EXTRA:EXTRA + 1], min_val=0, max_val=EXTRA)
            with pe.If(n_extra > 0):
                with pe.Fori(0, EXTRA) as i:
                    with pe.If(n_extra > i):
                        expert(0, 0, NE + i, -(-NE // WS) + 1 + i)

        @block.scalar
        def _(act):
            steps_done = [0]

            def link(ins):
                steps_done[0] += 1
                ins.then_inc(act_step, 1)
                act.wait_ge(act_step, steps_done[0])

            act.wait_ge(consts, 5)
            act.activation(rs_mem[:, :], ones[:, 0:2], ACT.Sqrt).then_inc(act_step, 1)
            steps_done[0] += 1

            def root(i):
                t = START_TILES[i]
                n = rows(t)
                act.wait_ge(ms_ok, i + 1)
                act.activation(rs[0:n, t:t + 1], ss[0:n, t:t + 1], ACT.Sqrt).then_inc(sqrt_ok, 1)

            for i, t in enumerate(START_TILES):
                n = rows(t)
                act.wait_ge(x_ld[t], 16)
                if i >= 1:
                    act.wait_ge(sumsq_ok, i)
                act.activation(junk[0:n, :], x_in[0:n, t, :], ACT.Square, accum_out=ss[0:n, t:t + 1]).then_inc(sumsq_ok, 1)
                if i >= 1:
                    root(i - 1)
            root(NT - 1)

            act.sem_inc(pj_sb, 2)
            act.sem_inc(y2_sb, 1)
            for j in range(OUTS_KEPT):
                act.sem_inc(ydr_st[j], 32)

            def split(slot, loads):
                act.wait_ge(w_ld[slot], loads)
                act.activation(w_hi[:, slot, :, :], w_raw[:, slot, :, :], ACT.Copy).then_inc(split_hi, 1)

            def split_chunk(m):
                split(m % RING, 16 * (m // RING + 1))

            def copy_chunk(m, slot, place):
                act.wait_ge(w_used, m + 1)
                act.activation(halves(place), acc_pair(2 * (slot % 2)), ACT.Copy).then_inc(pj_sb, 1)

            split_chunk(0)
            act.wait_ge(xst_f, 1)
            act.activation(xn_hi[:, :, SEQ:TOK], xst_tmp[:, :, :], ACT.Copy).then_inc(xt_hi, 1)
            split_chunk(1)
            act.wait_ge(norm_ld, 16)
            for k in range(KD):
                act.wait_ge(xt_ps, k + 1)
                act.activation(xn_hi[:, k, 0:SEQ], bank(4 + k % 4), ACT.Copy, scale=norm1_t[:, k:k + 1]).then_inc(xt_hi, 1)
            split_chunk(2)
            split_chunk(3)
            for m in range(RING):
                copy_chunk(m, m, proj[:, FIRST + m, :])
                if m < 2:
                    act.wait_ge(mem_ld, 16)
                    act.wait_ge(sumsq_ok, NT + m)
                    act.activation(junk[:, :], mem_in[:, m, :], ACT.Square, accum_out=ss_mem[:, m:m + 1]).then_inc(sumsq_ok, 1)
                else:
                    if m == 2:
                        act.wait_ge(ms_ok, MS_MEM)
                        act.activation(rs_mem[:, :], ss_mem[:, :], ACT.Sqrt).then_inc(sqrt_ok, 1)
                    split_chunk(m + 2)
            with act.Fori(1, PART1 // RING) as i:
                for j in range(RING):
                    split((j + 2) % RING, 16 * i + (16 if j < 2 else 32))
                    copy_chunk(RING * i + j, j, proj[:, bass.ds(RING * i + j + FIRST, 1), :].rearrange("p o n -> p (o n)"))
            for m in range(PART1, IN_CHUNKS):
                split_chunk(m + 2)
                if m == 16:
                    act.wait_ge(pj_sb, RING + 2)
                    act.activation(qx_sq[:, :, :], proj[:, X0:X0 + XH, :], ACT.Square).then_inc(qxsq_ok, 1)
                    act.wait_ge(tp_ps, JOB_QSS + 1)
                if m == 18:
                    act.wait_ge(ms_ok, MS_QX)
                    act.activation(rs_qx[:, :], ss_qx[:, :], ACT.Sqrt).then_inc(sqrt_ok, 1)
                copy_chunk(m, m % RING, proj[:, m - PART1, :])
                if m == 24:
                    act.wait_ge(ms_ok, MS_MK)
                    act.activation(rs_mk[:, :], ss_mk[:, :], ACT.Sqrt).then_inc(sqrt_ok, 1)

            def sigmoid(n, pair):
                act.wait_ge(gt_ps, n + 1)
                act.wait_ge(mg_ok, n + 1)
                act.activation(halves(gate_sb[:, n % 2, :]), acc_pair(pair), ACT.Sigmoid).then_inc(gt_sb, 1)

            def split_branch(n, slot, group, loads):
                act.wait_ge(br_ld[slot], loads)
                act.activation(w_br_hi[group][:, :, :], w_br[:, slot, :, :], ACT.Copy).then_inc(wb_hi, 1)

            def turned_out(u):
                act.wait_ge(ct_ps, u + 1)
                act.activation(prob_t[:, :, u % 2 * 2 * P:(u % 2 + 1) * 2 * P], bank(7).rearrange("p (t n) -> p t n", t=2),
                               ACT.Copy).then_inc(ct_sb, 1)

            def load_memory_values(b):
                if b == 0:
                    act.wait_ge(mid_st, MID_STORES)
                else:
                    act.wait_ge(val_used, b)
                for v in (b, b + 1):
                    act.dma_start(vals[:, v % 2, :, :], io["cache_mem_v"][v].rearrange("(t p) c -> p t c", p=P)
                                  ).then_inc(mval_ld[v % 2], 16)

            act.wait_ge(u_ok, CW + 1)
            for c in range(CW):
                ins = act.activation(y_hi_conv[c][:, :], proj[:, U0 + c, :], ACT.Copy)
            ins.then_inc(xt_hi, 1)
            for n in range(KD):
                if n >= 1:
                    act.wait_ge(br_ps, n)
                split_branch(n, n % RING, 0, 16 * (n // RING + 1))
                split_chunk(IN_CHUNKS + n + 2)
                sigmoid(n, 0)
                u, h, part = n, n // 2, n % 2
                if n >= 1:
                    turned_out(u - 1)
                act.wait_ge(cs_mx, u + 1)
                if u >= 2:
                    act.wait_ge(ct_ps, u - 1)
                out = bank(6).rearrange("p (t m) -> p t m", t=2)
                for t in range(2):
                    col = (2 * part + t) * XH + h
                    act.activation(prob[:, u % 2, t, :], out[:, t, :], ACT.Exp, bias=xneg[:, u % 2, t:t + 1],
                                   scale=rs_qx[:, col:col + 1], accum_out=xsum[:, u % 2, t:t + 1]).then_inc(cs_exp, 1)
                if n == 4:
                    act.wait_ge(zm_mx, 1)
                    act.activation(pm[0:NB * XH, :], cols(5, ZM_AT, NM)[0:NB * XH], ACT.Exp, bias=pm_neg[0:NB * XH, :],
                                   accum_out=pm_sum[0:NB * XH, :]).then_inc(pm_exp, 1)
                if n in (2, 5, 6):
                    load_memory_values(max(0, 2 * (n - 4)))
                if n == 6:
                    load_memory_values(6)
                if n % 2 == 0 and n >= 2:
                    act.wait_ge(cy_ps, n // 2)
                    act.activation(proj[:, B0 + n // 2 - 1, 0:SEQ], bank(7), ACT.Copy).then_inc(cy_sb, 1)
            turned_out(2 * XH - 1)

            def front(h):
                act.wait_ge(z_ps, h + 1)
                if h >= 2:
                    act.wait_ge(a_ok, h - 1)
                    act.wait_ge(s_ps, h - 1)
                else:
                    act.wait_ge(dot_ok, 2 * NB)
                act.activation(z_sb[:, h % 2, :], acc_all[:, 0:SCORE_N], ACT.Identity, bias=sbias_bc[:, h:h + 1],
                               scale=SB_SCALE)
                act.activation(sp_sb[:, h % 2, :], acc_all[:, 0:SCORE_N], ACT.Abs, bias=sbias_bc[:, h:h + 1],
                               scale=SB_SCALE).then_inc(z_read, 1)
                act.wait_ge(z_read, h + 1)
                link(act.activation(sp_sb[:, h % 2, :], sp_sb[:, h % 2, :], ACT.Exp, scale=-1.0))
                act.activation(sp_sb[:, h % 2, :], sp_sb[:, h % 2, :], ACT.Ln, bias=1.0).then_inc(ln_ok, 1)

            def weights(h):
                act.wait_ge(t_cut, 4 * (h + 1))
                if h >= 2:
                    act.wait_ge(y_ps, h // 2)
                act.activation(a_sb[:, h % 2, :], z_sb[:, h % 2, :], ACT.Exp).then_inc(a_ok, 1)

            def stick_out(pair):
                act.wait_ge(y_ps, pair + 1)
                act.activation(proj[:, C0 + pair, 0:SEQ], bank(5), ACT.Copy).then_inc(y_sb, 1)

            act.wait_ge(small_ld, 16 * 6)
            front(0)
            act.wait_ge(cy_ps, XH)
            act.activation(proj[:, B0 + XH - 1, 0:SEQ], bank(7), ACT.Copy).then_inc(cy_sb, 1)
            act.wait_ge(yt_sb, 2)
            act.wait_ge(br_ps, KD)
            act.wait_ge(cy_sb, XH)
            act.activation(y_hi_x[:, :, :], proj[:, B0:B0 + CW, :], ACT.Copy).then_inc(xt_hi, 1)
            split_branch(KD, 0, 1, 16 * (KD // RING + 1))
            split_chunk(IN_CHUNKS + KD + 2)
            act.wait_ge(zs_ok, 1)
            link(act.activation(z_abs[:, :, :, :], zs[:, :, :, :], ACT.Abs))
            link(act.activation(z_abs[:, :, :, :], z_abs[:, :, :, :], ACT.Exp, scale=-1.0))
            act.activation(z_abs[:, :, :, :], z_abs[:, :, :, :], ACT.Ln, bias=1.0).then_inc(zsln_ok, 1)
            for h in range(HEADS):
                n = KD + h
                if h >= 1:
                    split_chunk(IN_CHUNKS + n + 2)
                    act.wait_ge(br_ps, n)
                    split_branch(n, n % RING, 1, 16 * (n // RING + 1))
                if h == 1:
                    act.wait_ge(ts_ok, 1)
                    act.activation(a_s[:, :, :, 0:HEADS].rearrange("p j b h -> p (j b) h"),
                                   zs[:, :, :, :].rearrange("p j b h -> p (j b) h"), ACT.Exp).then_inc(as_ok, 1)
                sigmoid(n, 6)
                if h >= 2 and h % 2 == 0:
                    stick_out(h // 2 - 1)
                if h + 1 < HEADS:
                    front(h + 1)
                weights(h)
            stick_out(HEADS // 2 - 1)

            act.wait_ge(br_ps, 2 * KD)
            act.wait_ge(y_sb, HEADS // 2)
            act.wait_ge(yt_sb, 4)
            act.activation(y_hi_sb[:, :, :], proj[:, C0:C0 + CW, :], ACT.Copy).then_inc(xt_hi, 1)
            with act.Fori(0, KD // RING) as i:
                for j in range(RING):
                    n = 2 * KD + RING * i + j
                    act.wait_ge(br_ps, n)
                    split_branch(n, j, 2, 16 * (i + 2 * KD // RING + 1))
                    loads = 16 * (2 * KD // RING + 7) + 16 * i + (16 if j < 2 else 32)
                    if j < 2:
                        split((j + 2) % RING, loads)
                    else:
                        with act.If(i < 1):
                            split((j + 2) % RING, loads)
                    act.wait_ge(gt_ps, n + 1)
                    act.wait_ge(mg_ok, n + 1)
                    act.activation(halves(gate_sb[:, j % 2, :]), acc_pair(0), ACT.Sigmoid).then_inc(gt_sb, 1)

            act.wait_ge(part_ps, 1)
            act.activation(wo_part[:, :, :], bank(4, 2).rearrange("p (h n) -> p h n", h=2), ACT.Copy).then_inc(part_sb, 1)
            def copy_h(i):
                tt = MERGE_TILES[i]
                n = rows(tt)
                for q in range(2):
                    m = 2 * i + q
                    act.wait_ge(ht_ps, m + 1)
                    act.activation(h_t[:, 4 * q:4 * q + 4, tok(tt)],
                                   bank(4 + m % 2)[:, 0:4 * n].rearrange("p (k n) -> p k n", k=4), ACT.Copy).then_inc(ht_sb, 1)

            for i, tt in enumerate(MERGE_TILES):
                n = rows(tt)
                act.wait_ge(x1_ok, 2 * i + 2)
                act.wait_ge(sumsq_ok, NT + 2 + i)
                act.activation(junk2[0:n, :], x1[0:n, tt, :], ACT.Square, accum_out=ss2[0:n, tt:tt + 1]).then_inc(sumsq_ok, 1)
                act.wait_ge(ms_ok, MS_H + i)
                act.activation(rs2[0:n, tt:tt + 1], rs2[0:n, tt:tt + 1], ACT.Sqrt).then_inc(sqrt_ok, 1)
                act.wait_ge(h_ok, i + 1)
                act.dma_start(h_dram[tok(tt), :], h_tok[0:n, tt, :]).then_inc(h_st, 16)
                if i == 1:
                    copy_h(0)
                if 1 <= i < NT - 1:
                    copy_h(i)
            copy_h(NT - 1)
            act.wait_ge(lgt_ps, 1)
            act.activation(logits_t[0:NR, 0:SEQ], bank(6)[0:NR, :], ACT.Copy).then_inc(lgt_sb, 1)
            act.activation(logits_t[0:NR, SEQ:TOK], bank(7)[0:NR, 0:NB], ACT.Copy).then_inc(lgt_sb, 1)
            act.wait_ge(lg_max, 1)
            act.activation(g_exp[:, :, :], g_tmp[:, :, :], ACT.Exp).then_inc(lg_exp, 1)
            act.wait_ge(lg_max, 2)
            act.activation(top2[:, :], top1[:, :], ACT.Exp).then_inc(lg_exp, 1)

            def block_act(slot, n, store, stored):
                act.wait_ge(upt_ps, n + 1)
                up = bank(6).rearrange("p (c t) -> p c t", c=CW)
                act.activation(gate_h[:, :, :], up[:, :, 0:CAP], ACT.Sigmoid).then_inc(sig_ok, 1)
                act.wait_ge(y2_ps, n + 1)
                act.wait_ge(ydr_st[slot], stored)
                act.activation(y_out[:, slot, :], bank(7), ACT.Copy).then_inc(y2_sb, 1)
                act.wait_ge(y2_sb, n + 2)
                for half in range(2):
                    act.dma_start(store[:, half * DE:(half + 1) * DE], y_out[half * CAP:(half + 1) * CAP, slot, :]
                                  ).then_inc(ydr_st[slot], 16)

            with act.Fori(0, NE // OUTS_KEPT) as i:
                for j in range(OUTS_KEPT):
                    block_act(j, OUTS_KEPT * i + j, y_dram[bass.ds((OUTS_KEPT * i + j) * CAP, CAP), :], 32 * i + 32)
            act.wait_ge(over_ok, 1)
            n_extra = act.value_load(over_i[0:1, EXTRA:EXTRA + 1], min_val=0, max_val=EXTRA)
            with act.If(n_extra > 0):
                with act.Fori(0, EXTRA) as i:
                    with act.If(n_extra > i):
                        block_act(0, NE + i, y_dram[bass.ds((NE + i) * CAP, CAP), :],
                                  32 * (NE // OUTS_KEPT + 1) + 32 * i)

        @block.vector
        def _(dve):
            steps_done = [0]

            def link(ins):
                steps_done[0] += 1
                ins.then_inc(dve_step, 1)
                dve.wait_ge(dve_step, steps_done[0])

            dve.sem_inc(mg_ok, 2)

            def mean_square(i):
                t = START_TILES[i]
                n = rows(t)
                dve.wait_ge(sumsq_ok, i + 1)
                dve.tensor_scalar(ss[0:n, t:t + 1], ss[0:n, t:t + 1], 1.0 / D, EPS, ALU.mult, ALU.add).then_inc(ms_ok, 1)

            mean_square(0)
            for i, t in enumerate(START_TILES):
                n = rows(t)
                if i + 1 < NT:
                    mean_square(i + 1)
                dve.wait_ge(sqrt_ok, i + 1)
                link(dve.reciprocal(rs[0:n, t:t + 1], rs[0:n, t:t + 1]))
                dve.tensor_scalar(x_in[0:n, t, :], x_in[0:n, t, :], rs[0:n, t:t + 1], None, ALU.mult).then_inc(xn_ok, 1)

            def rest(slot, m):
                dve.wait_ge(split_hi, m + 1)
                dve.tensor_tensor(w_lo[:, slot, :, :], w_raw[:, slot, :, :], w_hi[:, slot, :, :].bitcast(F32),
                                  ALU.subtract).then_inc(split_lo, 1)

            def rest_chunk(m):
                rest(m % RING, m)

            dve.wait_ge(norm_ld, 16)
            dve.wait_ge(xst_ps, 1)
            dve.tensor_tensor(xst_tmp[:, :, :], cols(2, 384, KD * NB).rearrange("p (k b) -> p k b", k=KD),
                              norm1_t[:, :].unsqueeze(2).to_broadcast([P, KD, NB]), ALU.mult).then_inc(xst_f, 1)
            rest_chunk(0)
            dve.wait_ge(xt_hi, 1)
            dve.tensor_tensor(xn_lo[:, :, SEQ:TOK], xst_tmp[:, :, :], xn_hi[:, :, SEQ:TOK].bitcast(F32),
                              ALU.subtract).then_inc(xt_lo, 1)
            rest_chunk(1)
            for k in range(KD):
                dve.wait_ge(xt_hi, k + 2)
                dve.scalar_tensor_tensor(out=xn_lo[:, k, 0:SEQ], in0=bank(4 + k % 4), scalar=norm1_t[:, k:k + 1],
                                         in1=xn_hi[:, k, 0:SEQ].bitcast(F32), op0=ALU.mult, op1=ALU.subtract).then_inc(xt_lo, 1)
            rest_chunk(2)
            rest_chunk(3)
            dve.wait_ge(sumsq_ok, NT + 2)
            dve.tensor_scalar(ss_mem[:, :], ss_mem[:, :], 1.0 / D, EPS, ALU.mult, ALU.add).then_inc(ms_ok, 1)
            rest_chunk(4)
            dve.wait_ge(sqrt_ok, MS_MEM)
            link(dve.reciprocal(rs_mem[:, :], rs_mem[:, :]))
            rest_chunk(5)
            dve.wait_ge(page_ld, 16)
            dve.wait_ge(consts, 5)
            link(dve.tensor_copy(page_f[:, :], page_i[:, :]))
            link(dve.tensor_reduce(tile_sum[:, :], ident[:, :].rearrange("p (s x) -> p x s", s=PER)[:, COLS - NB:, :],
                                   AX.X, ALU.add))
            link(dve.tensor_copy(ident_r[:, :], ident[:, 0:NB]))
            link(dve.tensor_scalar(page_f[:, :], page_f[:, :], float(P), row_f[:, 0:1], ALU.mult, ALU.add))
            dve.tensor_copy(page_row[:, :], page_f[:, :]).then_inc(rows_ok, 1)
            with dve.Fori(1, PART1 // RING) as i:
                for j in range(RING):
                    rest((j + 2) % RING, RING * i + j + 2)
            for t in range(2):
                dve.tensor_scalar(mem_in[:, t, :], mem_in[:, t, :], rs_mem[:, t:t + 1], None, ALU.mult).then_inc(xn_ok, 1)

            def take(n, out, src):
                dve.wait_ge(tp_ps, n + 1)
                dve.tensor_copy(out, src).then_inc(tp_sb, 1)

            def job_out(n):
                return bank(4 + n % 4)

            full = (NT - 1) * XH
            heads = mk[:, :, :].rearrange("p t (h d) -> p (t h) d", d=XD)
            dve.wait_ge(xt_ps, KD)
            dve.memset(ss_qx[:, :], 1.0).then_inc(dve_step, 1)
            dve.memset(pm_t[:, :, :, :], 0.0).then_inc(dve_step, 1)
            steps_done[0] += 2
            dve.wait_ge(small_ld, 16 * 6)
            for m in range(PART1, IN_CHUNKS):
                rest_chunk(m + 2)
                if m == 16:
                    dve.wait_ge(tp_ps, JOB_QSS + 1)
                    dve.wait_ge(dve_step, steps_done[0])
                    out = job_out(JOB_QSS)
                    link(dve.tensor_scalar(ss_qx[:, 0:full], out[:, 0:full], 1.0 / XD, EPS, ALU.mult, ALU.add))
                    dve.tensor_scalar(ss_qx[0:NB, full:full + XH], out[0:NB, full:full + XH], 1.0 / XD, EPS, ALU.mult,
                                      ALU.add).then_inc(tp_sb, 1)
                    dve.wait_ge(tp_sb, JOB_QSS + 1)
                    dve.sem_inc(ms_ok, 1)
                elif m in (17, 18):
                    for q in (2 * (m - 17), 2 * (m - 17) + 1):
                        n = JOB_MT + q
                        dve.wait_ge(tp_ps, n + 1)
                        dve.tensor_tensor(mem_t[:, 2 * q:2 * q + 2, :], job_out(n).rearrange("p (k m) -> p k m", k=2),
                                          mnorm_t[:, 2 * q:2 * q + 2].unsqueeze(2).to_broadcast([P, 2, NM]), ALU.mult
                                          ).then_inc(tp_sb, 1)
                elif m == 19:
                    for tt in range(NT):
                        n = JOB_V + tt
                        take(n, v_tok[:, tt, :] if tt < NT - 1 else v_s[0:NB, :], job_out(n)[0:rows(tt), :])
                    dve.wait_ge(sqrt_ok, MS_QX)
                    link(dve.reciprocal(rs_qx[:, :], rs_qx[:, :]))
                    link(dve.tensor_scalar(rs_qx[:, :], rs_qx[:, :], X_SCALE, None, ALU.mult))
                    take(JOB_STATE, state_t[:, :, :, :],
                         job_out(JOB_STATE)[:, 0:2 * CW * NB].rearrange("p (j c b) -> p j c b", j=2, c=CW))
                    dve.wait_ge(tp_sb, JOB_STATE + 1)
                elif m in (20, 21, 22, 23):
                    mt, half = divmod(m - 20, 2)
                    n = JOB_MP + m - 20
                    take(n, (mk, mv)[half][:, mt, :], job_out(n))
                    if m == 20:
                        dve.wait_ge(qxsq_ok, 1)
                        dve.tensor_scalar(proj[:, X0:X0 + XH, :], proj[:, X0:X0 + XH, :], qnorm_t[:, 0:1], None,
                                          ALU.mult).then_inc(qxn_ok, 1)
                    if m == 23:
                        dve.wait_ge(tp_sb, n + 1)
                        link(dve.tensor_tensor(mk_sq[:, :, :], mk[:, :, :], mk[:, :, :], ALU.mult))
                        link(dve.tensor_reduce(ss_mk[:, :], mk_sq[:, :, :].rearrange("p t (h d) -> p (t h) d", d=XD),
                                               AX.X, ALU.add))
                        dve.tensor_scalar(ss_mk[:, :], ss_mk[:, :], 1.0 / XD, EPS, ALU.mult, ALU.add).then_inc(ms_ok, 1)
                elif m == 24:
                    take(JOB_Q, q_s[0:NB, :], job_out(JOB_Q)[0:NB, :])
                    dve.wait_ge(tp_ps, JOB_QX + 1)
                    dve.tensor_tensor(qx_s[0:NB, :].rearrange("p (h d) -> p h d", h=XH),
                                      job_out(JOB_QX)[0:NB, :].rearrange("p (h d) -> p h d", h=XH),
                                      rs_qx[0:NB, full:full + XH].unsqueeze(2).to_broadcast([NB, XH, XD]), ALU.mult
                                      ).then_inc(tp_sb, 1)
                    dve.wait_ge(tp_sb, JOB_QX + 1)
                    dve.tensor_copy(q_hi[0:NB, :], q_s[0:NB, :])
                    link(dve.tensor_copy(qx_hi[0:NB, :], qx_s[0:NB, :]))
                    dve.tensor_tensor(q_lo[0:NB, :], q_s[0:NB, :], q_hi[0:NB, :].bitcast(F32), ALU.subtract)
                    link(dve.tensor_tensor(qx_lo[0:NB, :], qx_s[0:NB, :], qx_hi[0:NB, :].bitcast(F32), ALU.subtract))
                elif m == 25:
                    dve.wait_ge(sqrt_ok, MS_MK)
                    link(dve.reciprocal(rs_mk[:, :], rs_mk[:, :]))
                    link(dve.tensor_tensor(heads, heads, rs_mk[:, :].unsqueeze(2).to_broadcast([P, 2 * XH, XD]), ALU.mult))
                    dve.tensor_tensor(heads, heads, knorm_bc[:, :].unsqueeze(1).to_broadcast([P, 2 * XH, XD]),
                                      ALU.mult).then_inc(mk_ok, 1)
                if m in (25, 26):
                    for tt in (range(3) if m == 25 else range(3, NT)):
                        n = JOB_K + tt
                        if 2 <= tt < NT - 1:
                            dve.wait_ge(kout_st[tt % 2], 16)
                        take(n, k_out[:, tt % 2, :] if tt < NT - 1 else k_s[0:NB, :], job_out(n)[0:rows(tt), :])
                if 21 <= m < 21 + CW:
                    c = m - 21
                    dve.wait_ge(pj_sb, PART1 + C0 + c + 3)
                    dve.tensor_tensor(proj[:, C0 + c, :], proj[:, C0 + c, :], proj[:, U0 + c, :], ALU.mult).then_inc(u_ok, 1)
                    dve.wait_ge(u_ok, c + 1)
                    link(dve.tensor_scalar(proj[:, c, :], proj[:, C0 + c, :], conv_t[:, 2, c:c + 1], None, ALU.mult))
                    for back in (1, 2):
                        tap = conv_t[:, 2 - back, c:c + 1]
                        dve.scalar_tensor_tensor(out=proj[:, c, back:SEQ], in0=proj[:, C0 + c, 0:SEQ - back], scalar=tap,
                                                 in1=proj[:, c, back:SEQ], op0=ALU.mult, op1=ALU.add)
                        link(dve.scalar_tensor_tensor(out=proj[:, c, SEQ:TOK], in0=state_t[:, 2 - back, c, :],
                                                      scalar=tap, in1=proj[:, c, SEQ:TOK], op0=ALU.mult, op1=ALU.add))
                if m == 27:
                    take(JOB_U, conv_out[0:2 + NB, :], job_out(JOB_U)[0:2 + NB, :])
                    for q in range(2):
                        n = JOB_MK + q
                        take(n, mk_t[:, 2 * q:2 * q + 2, :], job_out(n).rearrange("p (h m) -> p h m", h=2))
                    dve.wait_ge(pj_sb, IN_CHUNKS + 2)
                    dve.tensor_tensor(proj[:, 0:CW, :], proj[:, 0:CW, :], proj[:, B0:B0 + CW, :], ALU.mult).then_inc(u_ok, 1)

            def merge(n, place, part):
                dve.wait_ge(gt_sb, n + 1)
                dve.wait_ge(br_ps, n + 1)
                total, gate = halves(place), halves(gate_sb[:, n % 2, :])
                if n < KD:
                    dve.tensor_tensor(total, gate, part, ALU.mult).then_inc(mg_ok, 1)
                else:
                    dve.tensor_tensor(gate, gate, part, ALU.mult).then_inc(term_ok, 1)
                    dve.wait_ge(term_ok, n - KD + 1)
                    dve.tensor_tensor(total, total, gate, ALU.add).then_inc(mg_ok, 1)

            def dots(n):
                b = n % NB
                heads_n, dim = (XH, XD) if n < NB else (HEADS, HD)
                dve.wait_ge(bq_ps, n + 1)
                dve.wait_ge(key_ld[n % KEY_RING], 32 * (n // KEY_RING + 1))
                if n >= 1:
                    dve.wait_ge(dot_ok, n)
                else:
                    dve.wait_ge(mid_st, MID_STORES)
                dve.tensor_tensor(dot[:, :, :], keys[:, n % KEY_RING, :, :],
                                  bank(4).unsqueeze(1).to_broadcast([P, 2, W]), ALU.mult).then_inc(bq_used, 1)
                dve.wait_ge(bq_used, n + 1)
                out = zm[:, :, b, :] if n < NB else z_raw[:, :, b, :]
                dve.tensor_reduce(out, dot[:, :, :].rearrange("p j (h d) -> p j h d", d=dim), AX.X, ALU.add).then_inc(dot_ok, 1)

            def two_out(kind, b):
                dve.wait_ge(val_used, kind * NB + b + 2)
                if kind == 1:
                    dve.wait_ge(yt_ps, b // PER + 1)
                at = COLS * (b % PER)
                dve.tensor_copy(y_four[b // PER][at:at + 2 * COLS, :], bank(5)[at:at + 2 * COLS, :]).then_inc(yg_sb, 1)

            def rest_branch(n, slot, group):
                dve.wait_ge(wb_hi, n + 1)
                dve.tensor_tensor(w_br_lo[:, slot, :, :], w_br[:, slot, :, :], w_br_hi[group][:, :, :].bitcast(F32),
                                  ALU.subtract).then_inc(wb_lo, 1)

            def rest_inputs(group, hi):
                dve.wait_ge(xt_hi, KD + 2 + group)
                first = YS_AT[group]
                if group == 0:
                    for c in range(CW):
                        last = dve.tensor_tensor(y_lo[:, first + c, :], proj[:, first + c, :], hi[c][:, :].bitcast(F32),
                                                 ALU.subtract)
                else:
                    last = dve.tensor_tensor(y_lo[:, first:first + CW, :], proj[:, first:first + CW, :],
                                             hi[:, :, :].bitcast(F32), ALU.subtract)
                last.then_inc(xt_lo, 1)

            m32 = NB * XH
            rest_inputs(0, y_hi_conv)
            for n in range(KD):
                u, h, part = n, n // 2, n % 2
                rest_branch(n, n % RING, 0)
                rest_chunk(IN_CHUNKS + n + 2)
                dve.wait_ge(cs_ps, u + 1)
                if u >= 2:
                    dve.wait_ge(cs_exp, 2 * (u - 1))
                link(dve.tensor_reduce(xmax[:, u % 2, :], bank(6).rearrange("p (t m) -> p t m", t=2), AX.X, ALU.max))
                col = 2 * part * XH + h
                dve.scalar_tensor_tensor(out=xneg[:, u % 2, :], in0=xmax[:, u % 2, :], scalar=-1.0,
                                         in1=rs_qx[:, col:col + XH + 1:XH], op0=ALU.mult, op1=ALU.mult).then_inc(cs_mx, 1)
                dots(2 * n)
                if n == 4:
                    dve.wait_ge(zm_ps, 1)
                    link(dve.tensor_reduce(pm_max[0:m32, :], cols(5, ZM_AT, NM)[0:m32], AX.X, ALU.max))
                    dve.tensor_scalar(pm_neg[0:m32, :], pm_max[0:m32, :], -1.0, None, ALU.mult).then_inc(zm_mx, 1)
                if n == 5:
                    dve.wait_ge(pmt_ps, 1)
                    dve.tensor_copy(pm_t[:, :, :, 0:XH].rearrange("p t b h -> p (t b) h"),
                                    cols(5, PMT_AT, 2 * m32).rearrange("p (t h) -> p t h", h=XH)).then_inc(pmt_sb, 1)
                if n >= 6:
                    two_out(0, 2 + 4 * (n - 6))
                if n == KD - 1:
                    dve.wait_ge(bq_ps, 2 * NB)
                merge(n, merged[:, n, :], acc_pair(2))
                dots(2 * n + 1)
                dve.wait_ge(cs_exp, 2 * (u + 1))
                link(dve.reciprocal(xrec[:, u % 2, :], xsum[:, u % 2, :]))
                dve.tensor_tensor(prob[:, u % 2, :, :], prob[:, u % 2, :, :],
                                  xrec[:, u % 2, :].unsqueeze(2).to_broadcast([P, 2, NM]), ALU.mult).then_inc(cs_nrm, 1)
                if n == 4:
                    dve.wait_ge(pm_exp, 1)
                    link(dve.reciprocal(pm_rec[0:m32, :], pm_sum[0:m32, :]))
                    dve.tensor_scalar(pm[0:m32, :], pm[0:m32, :], pm_rec[0:m32, :], None, ALU.mult).then_inc(pm_ok, 1)
                if n in (5, 6):
                    two_out(0, 4 * (n - 5))
            for g in range(2):
                dve.wait_ge(yt_ps, g + 1)
                turned = bank(5 - g).rearrange("p (c s x) -> p c s x", c=CW, s=PER)
                for c in range(XH):
                    last = dve.tensor_copy(proj[:, B0 + c, SEQ + PER * g:SEQ + PER * (g + 1)], turned[:, c, :, c])
                last.then_inc(yt_sb, 1)
            dve.wait_ge(cs_ps, 2 * XH)
            link(dve.memset(a_s[:, :, :, :], 0.0))

            def softplus(h):
                dve.wait_ge(ln_ok, h + 1)
                dve.scalar_tensor_tensor(out=sp_sb[:, h % 2, :], in0=z_sb[:, h % 2, :], scalar=0.0, in1=sp_sb[:, h % 2, :],
                                         op0=ALU.max, op1=ALU.add).then_inc(sp_ok, 1)

            dve.wait_ge(dot_ok, 2 * NB)
            flat = "p j b h -> p (j b) h"
            dve.scalar_tensor_tensor(out=zs[:, :, :, :].rearrange(flat), in0=z_raw[:, :, :, :].rearrange(flat),
                                     scalar=SB_SCALE, in1=sbias_bc[:, :].unsqueeze(1).to_broadcast([P, 2 * NB, HEADS]),
                                     op0=ALU.mult, op1=ALU.add).then_inc(zs_ok, 1)
            softplus(0)
            dve.wait_ge(zsln_ok, 1)
            dve.scalar_tensor_tensor(out=z_sp[:, :, :, :], in0=zs[:, :, :, :], scalar=0.0, in1=z_abs[:, :, :, :],
                                     op0=ALU.max, op1=ALU.add).then_inc(zssp_ok, 1)
            for h in range(HEADS):
                n = KD + h
                if h == 0:
                    rest_inputs(1, y_hi_x)
                rest_branch(n, n % RING, 1)
                rest_chunk(IN_CHUNKS + n + 2)
                dve.wait_ge(s_ps, h + 1)
                low, cut_at = SUM_AT[2], SCORE_AT[2]
                dve.tensor_tensor(z_sb[:, h % 2, 0:cut_at], z_sb[:, h % 2, 0:cut_at],
                                  acc_all[:, SUM_AT[0]:SUM_AT[0] + cut_at], ALU.subtract)
                dve.tensor_tensor(z_sb[:, h % 2, cut_at:SCORE_N], z_sb[:, h % 2, cut_at:SCORE_N],
                                  acc_all[:, low:low + SCORE_N - cut_at], ALU.subtract).then_inc(t_ok, 1)
                if 2 <= h < 6:
                    two_out(1, 2 * (h - 2))
                elif h >= 6:
                    g = h - 6
                    dve.wait_ge(yt_ps, 3 + g)
                    turned = bank(5).rearrange("p (c s x) -> p c s x", c=CW, s=PER)
                    for c in range(CW):
                        for r in range(2):
                            pr = slice(r * HD, (r + 1) * HD)
                            last = dve.tensor_copy(proj[pr, C0 + c, SEQ + PER * g:SEQ + PER * (g + 1)],
                                                   turned[pr, c, :, 2 * c + r])
                    last.then_inc(yt_sb, 1)
                merge(n, merged[:, h, :], acc_pair(6))
                if h + 1 < HEADS:
                    softplus(h + 1)
                if h == 0:
                    dve.wait_ge(ss_ps, 1)
                    per = NB * HEADS
                    zs_flat = zs[:, :, :, :].rearrange("p j b h -> p j (b h)")
                    dve.tensor_tensor(zs_flat, zs_flat, cols(5, SUMS_AT, 2 * per).rearrange("p (j n) -> p j n", j=2),
                                      ALU.subtract).then_inc(ts_ok, 1)

            rest_inputs(2, y_hi_sb)
            with dve.Fori(0, KD // RING) as i:
                for j in range(RING):
                    n = 2 * KD + RING * i + j
                    rest_branch(n, j, 2)
                    if j < 2:
                        rest((j + 2) % RING, IN_CHUNKS + 2 + n)
                    else:
                        with dve.If(i < 1):
                            rest((j + 2) % RING, IN_CHUNKS + 2 + n)
                    dve.wait_ge(gt_sb, n + 1)
                    dve.wait_ge(br_ps, n + 1)
                    total = halves(merged[:, bass.ds(RING * i + j, 1), :].rearrange("p o n -> p (o n)"))
                    gate = halves(gate_sb[:, j % 2, :])
                    dve.tensor_tensor(gate, gate, acc_pair(2), ALU.mult).then_inc(term_ok, 1)
                    dve.wait_ge(term_ok, n - KD + 1)
                    dve.tensor_tensor(total, total, gate, ALU.add).then_inc(mg_ok, 1)

            dve.wait_ge(x1_ld, 32)
            dve.wait_ge(route_ld, 32)
            for i, tt in enumerate(MERGE_TILES):
                n = rows(tt)
                for half in range(2):
                    q = 2 * i + half
                    dve.wait_ge(wo_ps, q + 1)
                    v = x1[0:n, tt, half * 512:(half + 1) * 512]
                    dve.tensor_tensor(v, v, bank(q % 4)[0:n, :], ALU.add).then_inc(x1_ok, 1)
                dve.wait_ge(sumsq_ok, NT + 3 + i)
                dve.tensor_scalar(rs2[0:n, tt:tt + 1], ss2[0:n, tt:tt + 1], 1.0 / D, EPS, ALU.mult, ALU.add).then_inc(ms_ok, 1)
                dve.wait_ge(sqrt_ok, MS_H + i)
                link(dve.reciprocal(rs2[0:n, tt:tt + 1], rs2[0:n, tt:tt + 1]))
                dve.scalar_tensor_tensor(out=h_tok[0:n, tt, :], in0=x1[0:n, tt, :], scalar=rs2[0:n, tt:tt + 1],
                                         in1=norm2_bc[0:n, :], op0=ALU.mult, op1=ALU.mult).then_inc(h_ok, 1)

            def bc(v, shape):
                return v.to_broadcast(shape)

            link(dve.memset(logits[:, :, :], 0.0))
            link(dve.memset(picked[:, NT:NT + 1, :], 0.0))
            dve.wait_ge(lg_ps, 1)
            dve.wait_ge(pool_step, POOL_CONSTS)
            lg = bank(0)[:, 0:NT * NR].rearrange("p (t r) -> p t r", t=NT)
            link(dve.tensor_tensor(logits[:, 0:NT - 1, :], lg[:, 0:NT - 1, :], bc(rbias_bc[:, :].unsqueeze(1), [P, NT - 1, NR]), ALU.add))
            link(dve.tensor_tensor(logits[0:NB, NT - 1, :], lg[0:NB, NT - 1, :], rbias_bc[0:NB, :], ALU.add))
            link(dve.tensor_reduce(g_top[:, :], logits[:, :, 0:NG], AX.X, ALU.max))
            dve.tensor_tensor(g_tmp[:, :, :], logits[:, :, 0:NG], bc(g_top[:, :].unsqueeze(2), [P, NT, NG]),
                              ALU.subtract).then_inc(lg_max, 1)

            def first_best(one, values, best, tmp, n):
                link(dve.tensor_tensor(tmp, values, bc(best.unsqueeze(2), [P, NT, n]), ALU.is_equal))
                link(dve.tensor_tensor(tmp, tmp, bc(rev[:, EPG - n:EPG].unsqueeze(1), [P, NT, n]), ALU.mult))
                link(dve.tensor_reduce(best, tmp, AX.X, ALU.max))
                link(dve.tensor_tensor(one, tmp, bc(best.unsqueeze(2), [P, NT, n]), ALU.is_equal))

            dve.wait_ge(lg_exp, 1)
            first_best(g_one[:, :, :], logits[:, :, 0:NG], g_top[:, :], g_tmp[:, :, :], NG)
            link(dve.tensor_tensor(g_one[:, :, :], g_one[:, :, :], bc(valid[:, :].unsqueeze(2), [P, NT, NG]), ALU.mult))
            shape4 = [P, NT, NG, EPG]
            link(dve.tensor_tensor(e_all[:, :, :, :], logits[:, :, NG:NR].rearrange("p t (g x) -> p t g x", g=NG),
                                   bc(g_one[:, :, :].unsqueeze(3), shape4), ALU.mult))
            link(dve.tensor_reduce(e_in[:, :, :], e_all[:, :, :, :].rearrange("p t g x -> p t x g"), AX.X, ALU.add))
            link(dve.tensor_reduce(top1[:, :], e_in[:, :, :], AX.X, ALU.max))
            link(dve.tensor_copy(gate1[:, :], top1[:, :]))
            first_best(one1[:, :, :], e_in[:, :, :], top1[:, :], e_tmp[:, :, :], EPG)
            link(dve.scalar_tensor_tensor(out=e_in[:, :, :], in0=one1[:, :, :], scalar=-1e30, in1=e_in[:, :, :],
                                          op0=ALU.mult, op1=ALU.add))
            link(dve.tensor_reduce(top2[:, :], e_in[:, :, :], AX.X, ALU.max))
            link(dve.tensor_tensor(top1[:, :], top2[:, :], gate1[:, :], ALU.subtract))
            first_best(one2[:, :, :], e_in[:, :, :], top2[:, :], e_tmp[:, :, :], EPG)
            dve.sem_inc(lg_max, 1)
            for pick, one in ((pick1, one1), (pick2, one2)):
                last = dve.tensor_tensor(pick[:, :, :, :], bc(g_one[:, :, :].unsqueeze(3), shape4),
                                         bc(one[:, :, :].unsqueeze(2), shape4), ALU.mult)
            link(last)
            experts = "p t g x -> p t (g x)"
            dve.tensor_tensor(picked[:, 0:NT, :], pick1[:, :, :, :].rearrange(experts), pick2[:, :, :, :].rearrange(experts),
                              ALU.add).then_inc(pick_ok, 1)
            link(dve.tensor_reduce(g_prob[:, :], g_exp[:, :, :], AX.X, ALU.add))
            link(dve.reciprocal(g_prob[:, :], g_prob[:, :]))
            dve.wait_ge(lg_exp, 2)
            link(dve.tensor_scalar(gate1[:, :], top2[:, :], 1.0, None, ALU.add))
            link(dve.reciprocal(gate1[:, :], gate1[:, :]))
            link(dve.tensor_tensor(gate1[:, :], gate1[:, :], g_prob[:, :], ALU.mult))
            link(dve.tensor_tensor(gate2[:, :], gate1[:, :], top2[:, :], ALU.mult))
            dve.wait_ge(rank_ps, 1)
            count = bank(1)[:, NT * NE:(NT + 1) * NE]
            link(dve.tensor_tensor(over_part[:, :, :], bc(count.unsqueeze(2), [P, NE, TOK // CAP]),
                                   bc(limits[:, :].unsqueeze(1), [P, NE, TOK // CAP]), ALU.is_gt))
            link(dve.tensor_reduce(extra[:, :], over_part[:, :, :], AX.X, ALU.add))
            pad = NE // 2
            link(dve.tensor_copy(scan[:, 0, pad:], extra[:, :]))
            for i in range(NE.bit_length() - 1):
                src, back = scan[:, i % 2, :], 2 ** i
                sums = extra_end[:, :] if 2 * back == NE else scan[:, (i + 1) % 2, pad:]
                link(dve.tensor_tensor(sums, src[:, pad:], src[:, pad - back:pad + NE - back], ALU.add))
            link(dve.tensor_tensor(over_slot[:, :], extra_end[:, :], extra[:, :], ALU.subtract))
            link(dve.tensor_scalar(over_slot[:, :], over_slot[:, :], float(CAP), float((NE - 1) * CAP), ALU.mult, ALU.add))
            link(dve.tensor_tensor(over_slot[:, :], over_slot[:, :], first_slot[:, :], ALU.subtract))
            rank = bank(1)[:, 0:NT * NE].rearrange("p (t e) -> p t e", t=NT)
            link(dve.tensor_tensor(dest[:, :, :], rank, bc(first_slot[:, :].unsqueeze(1), [P, NT, NE]), ALU.add))
            link(dve.scalar_tensor_tensor(out=over[:, :, :], in0=rank, scalar=float(CAP),
                                          in1=bc(over_slot[:, :].unsqueeze(1), [P, NT, NE]), op0=ALU.is_ge, op1=ALU.mult))
            link(dve.tensor_tensor(dest[:, :, :], dest[:, :, :], over[:, :, :], ALU.add))
            for pick, d in ((pick1, dest1), (pick2, dest2)):
                link(dve.tensor_tensor(over[:, :, :], dest[:, :, :], pick[:, :, :, :].rearrange(experts), ALU.mult))
                link(dve.tensor_reduce(d, over[:, :, :], AX.X, ALU.add))
            q_n = 2 * NT
            link(dve.tensor_tensor(from_block[:, :, :], bc(dests[:, :].unsqueeze(2), [P, q_n, BLOCKS + 1]),
                                   bc(block_at[:, :].unsqueeze(1), [P, q_n, BLOCKS + 1]), ALU.is_ge))
            link(dve.tensor_reduce(place_in[:, :], from_block[:, :, :], AX.X, ALU.add))
            link(dve.tensor_tensor(in_block[:, :, :], from_block[:, :, 0:BLOCKS], from_block[:, :, 1:BLOCKS + 1], ALU.subtract))
            for which in range(2):
                v = in_block[:, which * NT:(which + 1) * NT, :]
                last = dve.tensor_tensor(v, v, bc(tok_f[:, :].unsqueeze(2), [P, NT, BLOCKS]), ALU.mult)
            link(last)
            link(dve.scalar_tensor_tensor(out=place_in[:, :], in0=place_in[:, :], scalar=-float(CAP), in1=dests[:, :],
                                          op0=ALU.mult, op1=ALU.add))
            dve.tensor_tensor(at_pos[:, :, :], bc(place_in[:, :].unsqueeze(2), [P, q_n, CAP]),
                              bc(pos_at[:, :].unsqueeze(1), [P, q_n, CAP]), ALU.is_equal).then_inc(dest_ok, 1)
            link(dve.tensor_copy(dest1_i[:, :], dest1))
            link(dve.tensor_copy(dest2_i[:, :], dest2))
            link(dve.tensor_tensor(over_who[:, :, :], bc(steps[:, :].unsqueeze(2), [P, EXTRA, NE]),
                                   bc(extra_end[:, :].unsqueeze(1), [P, EXTRA, NE]), ALU.is_ge))
            link(dve.tensor_reduce(over_cnt[:, :], over_who[:, :, :], AX.X, ALU.add))
            link(dve.tensor_scalar(over_cnt[:, :], over_cnt[:, :], float(NE - 1), None, ALU.min))
            link(dve.tensor_copy(over_i[:, 0:EXTRA], over_cnt[:, :]))
            dve.tensor_copy(over_i[:, EXTRA:EXTRA + 1], extra_end[:, NE - 1:NE]).then_inc(over_ok, 1)
            dve.wait_ge(ids_ps, 1)
            dve.tensor_copy(slot_tok[0:CAP, :], bank(3)[0:CAP, 0:BLOCKS]).then_inc(ids_ok, 1)

            def block_dve(slot, n):
                dve.wait_ge(xgt_ps, n + 1)
                dve.tensor_copy(xg_t[:, slot, :, :], bank(4).rearrange("p (k t) -> p k t", k=KD)).then_inc(xgt_sb, 1)
                dve.wait_ge(up_ps, 2 * n + 2)
                dve.tensor_copy(up_sb[:, slot, :], bank(5)).then_inc(up_ok, 1)
                dve.wait_ge(sig_ok, n + 1)
                up = bank(6).rearrange("p (c t) -> p c t", c=CW)
                dve.tensor_tensor(gate_h[:, :, :], gate_h[:, :, :], up[:, :, 0:CAP], ALU.mult).then_inc(half_ok, 1)
                dve.wait_ge(half_ok, n + 1)
                dve.tensor_tensor(act_t[:, slot, :, :], gate_h[:, :, :], up[:, :, CAP:P], ALU.mult).then_inc(actt_ok, 1)

            with dve.Fori(0, NE // 2) as i:
                for j in range(2):
                    block_dve(j, 2 * i + j)
            dve.wait_ge(over_ok, 1)
            n_extra = dve.value_load(over_i[0:1, EXTRA:EXTRA + 1], min_val=0, max_val=EXTRA)
            with dve.If(n_extra > 0):
                with dve.Fori(0, EXTRA) as i:
                    with dve.If(n_extra > i):
                        block_dve(0, NE + i)
            for tt in START_TILES:
                n = rows(tt)
                dve.wait_ge(ys_ld[tt], 32)
                link(dve.scalar_tensor_tensor(out=x1[0:n, tt, :], in0=ya[0:n, tt, :], scalar=gate1[0:n, tt:tt + 1],
                                              in1=x1[0:n, tt, :], op0=ALU.mult, op1=ALU.add))
                dve.scalar_tensor_tensor(out=x1[0:n, tt, :], in0=yb[0:n, tt, :], scalar=gate2[0:n, tt:tt + 1],
                                         in1=x1[0:n, tt, :], op0=ALU.mult, op1=ALU.add).then_inc(y_done, 1)


INS = {
    "x_prompt": (1, SEQ, D), "x_sample": (NB, 1, D), "mem_prompt": (1, NM, D), "cache_k": None, "cache_v": None,
    "cache_mem_k": None, "cache_mem_v": None, "state_conv": None, "page_table": None, "norm1": None, "w_in": None,
    "conv_w": None, "sb_bias": None, "mem_norm": None, "w_mem_kv": None, "q_norm": None, "k_norm": None,
    "w_branch": None, "w_o": None, "norm2": None, "router_w": None, "router_b": None, "w1": None, "w3": None, "w2": None,
}
OUTS = (
    ("y_p", (1, SEQ, D)), ("y_s", (NB, 1, D)), ("k_p", (1, SEQ, HEADS, HD)), ("v_p", (1, SEQ, HEADS, HD)),
    ("conv_p", (1, CONV_K - 1, W)), ("mem_k", (1, NM, XH, XD)), ("mem_v", (1, NM, XH, XD)),
    ("k_s", (NB, 1, HEADS, HD)), ("v_s", (NB, 1, HEADS, HD)), ("conv_s", (NB, CONV_K - 1, W)),
)
FLAT = {
    "y_p": "b s d -> (b s) d", "y_s": "b s d -> (b s) d", "k_p": "b s h d -> (b s) (h d)", "v_p": "b s h d -> (b s) (h d)",
    "conv_p": "b j c -> (b j) c", "mem_k": "b m h d -> (b m) (h d)", "mem_v": "b m h d -> (b m) (h d)",
    "k_s": "b s h d -> (b s) (h d)", "v_s": "b s h d -> (b s) (h d)", "conv_s": "b j c -> b j c",
}


def kernel(**inputs):
    import numpy as np
    import concourse.bacc as bacc
    from concourse.bass_utils import run_bass_kernel_spmd

    U_IN, C_IN, B_IN, Q_IN, K_IN, V_IN, X_IN, GATE_IN = (CW * i for i in range(8))
    a = {name: np.asarray(v) for name, v in inputs.items()}
    a["norm1"] = a["norm1"].reshape(KD, P).T
    a["mem_norm"] = a["mem_norm"].reshape(KD, P).T
    a["q_norm"] = a["q_norm"].reshape(XD, 1)
    a["conv_w"] = a["conv_w"].reshape(CONV_K, CW, P).transpose(2, 0, 1)
    order = [X_IN, V_IN, K_IN, Q_IN, U_IN, C_IN, B_IN] + [GATE_IN + KD * g for g in BRANCH_ORDER]
    order = [c + i for c, n in zip(order, [CW] * 7 + [KD] * 3) for i in range(n)]
    a["w_in"] = a["w_in"].reshape(KD, P, CHUNKS, P).transpose(2, 1, 0, 3)[order]
    a["w_branch"] = a["w_branch"].reshape(3, CW, P, KD, P).transpose(0, 3, 2, 1, 4)[list(BRANCH_ORDER)].reshape(3 * KD, P, CW, P)
    a["router_w"] = np.concatenate([a["w_group"], a["w_router"]], axis=1).reshape(KD, P, NR).transpose(1, 0, 2)
    a["router_b"] = np.concatenate([a["b_group"], a["b_router"]])
    a["cache_k"] = a["cache_k"].reshape(-1, W)
    a["cache_v"] = a["cache_v"].reshape(-1, W)
    a["cache_mem_k"] = a["cache_mem_k"].reshape(NB, NM, W)
    a["cache_mem_v"] = a["cache_mem_v"].reshape(NB, NM, W)

    nc = bacc.Bacc("TRN2", target_bir_lowering=False, num_devices=1)
    arrays, io = {}, {}
    for name in INS:
        v = np.ascontiguousarray(a[name])
        arrays["in_" + name] = v
        io[name] = nc.dram_tensor("in_" + name, v.shape, mybir.dt.from_np(v.dtype), kind="ExternalInput").ap()
    for name, shape in OUTS:
        io[name] = nc.dram_tensor("out_" + name, shape, F32, kind="ExternalOutput").ap().rearrange(FLAT[name])
    build(nc, io)
    r = run_bass_kernel_spmd(nc, [arrays], core_ids=[0])
    return tuple(r.results[0]["out_" + name] for name, _ in OUTS)
```
